# Optimizing a Trainium2 kernel written in Bass

```python
import math
import functools
import jax
import jax.numpy as jnp
from jax import lax
import numpy as np

D_MODEL = 2048
BATCH = 1
SEQ = 256
DEPTH = 1
DEC_BATCH = 8
DEC_SEQ = 8
PAST_LEN = 256
PAGE_SIZE = 128

HEAD_DIM = 128
N_HEADS = D_MODEL // HEAD_DIM
N_ATT_HEADS = N_HEADS // 2
N_GDN_HEADS = N_HEADS - N_ATT_HEADS
W_ATT = N_ATT_HEADS * HEAD_DIM
W_GDN = N_GDN_HEADS * HEAD_DIM
D_IN = 3 * W_ATT + 4 * W_GDN + 2 * N_GDN_HEADS
MOBA_BLOCK = 256
MOBA_TOP_K = 3
Q_CHUNK = 16
GDN_CONV = 4
GDN_CHUNK = 64
D_FF = 256 * ((8 * D_MODEL // 3 + 255) // 256)
FFN_CONV = 3
NUM_BUCKETS = 32
MAX_DISTANCE = 128
EPS = 1e-6
NEG = -1e30

kernel_name = 'hymba_gdn_moba_convffn_step'

def _rmsnorm(x, w):
    x32 = x.astype(jnp.float32)
    y = x32 * lax.rsqrt(jnp.mean(x32 * x32, axis=-1, keepdims=True) + EPS)
    return (y * w.astype(jnp.float32)).astype(x.dtype)

def _l2norm(x):
    return x * lax.rsqrt(jnp.sum(x * x, axis=-1, keepdims=True) + 1e-6)

def _causal_dwconv(u, w, prev):
    t = u.shape[1]
    ext = jnp.concatenate([prev.astype(u.dtype), u], axis=1)
    y = ext[:, 0:t] * w[0]
    for j in range(1, w.shape[0]):
        y = y + ext[:, j:j + t] * w[j]
    return y, ext[:, t:]

def _rel_bucket(dist):
    n = jnp.maximum(dist, 0)
    max_exact = NUM_BUCKETS // 2
    nf = jnp.maximum(n, 1).astype(jnp.float32)
    large = max_exact + (jnp.log(nf / max_exact) / math.log(MAX_DISTANCE / max_exact)
                         * (NUM_BUCKETS - max_exact)).astype(jnp.int32)
    large = jnp.minimum(large, NUM_BUCKETS - 1)
    return jnp.where(n < max_exact, n, large)

def _moba_core(q, q_pos, k_own, v_own, own_pos, rel_bias, sel=None):
    scale = HEAD_DIM ** -0.5
    lo = jnp.einsum('bqhd,bkhd->bqhk', q, k_own).astype(jnp.float32) * scale
    b_own = rel_bias[_rel_bucket(q_pos[:, None] - own_pos[None, :])].astype(jnp.float32)
    lo = lo + jnp.transpose(b_own, (0, 2, 1))[None]
    causal = (own_pos[None, :] <= q_pos[:, None])[None, :, None, :]
    lo = jnp.where(causal, lo, NEG)
    if sel is None:
        p = jax.nn.softmax(lo, axis=-1).astype(v_own.dtype)
        return jnp.einsum('bqhk,bkhd->bqhd', p, v_own)
    k_sel, v_sel, sel_pos, sel_ok = sel
    ls = jnp.einsum('bqhd,bqhsd->bqhs', q, k_sel).astype(jnp.float32) * scale
    hidx = jnp.arange(q.shape[2])[:, None]
    ls = ls + rel_bias[_rel_bucket(q_pos[None, :, None, None] - sel_pos), hidx].astype(jnp.float32)
    ls = jnp.where(sel_ok, ls, NEG)
    n_s = ls.shape[-1]
    p = jax.nn.softmax(jnp.concatenate([ls, lo], axis=-1), axis=-1).astype(v_own.dtype)
    return (jnp.einsum('bqhs,bqhsd->bqhd', p[..., :n_s], v_sel)
            + jnp.einsum('bqhk,bkhd->bqhd', p[..., n_s:], v_own))

def _select_blocks(q, means, cur, n_sel):
    s = jnp.einsum('bqhd,bjhd->bqhj', q.astype(jnp.float32), means)
    valid = jnp.arange(means.shape[1])[None, None, None, :] < cur[None, :, None, None]
    s = jnp.where(valid, s, NEG)
    _, idx = lax.top_k(s, n_sel)
    ok = jnp.arange(n_sel)[None, None, None, :] < cur[None, :, None, None]
    return idx, jnp.broadcast_to(ok, idx.shape)

def _moba_prompt(q, k, v, rel_bias):
    b, s, h, d = q.shape
    nb = -(-s // MOBA_BLOCK)
    pad = nb * MOBA_BLOCK - s
    kb = jnp.pad(k, ((0, 0), (0, pad), (0, 0), (0, 0))).reshape(b, nb, MOBA_BLOCK, h, d)
    vb = jnp.pad(v, ((0, 0), (0, pad), (0, 0), (0, 0))).reshape(b, nb, MOBA_BLOCK, h, d)
    n_sel = min(MOBA_TOP_K, nb - 1)
    n_chunks = s // Q_CHUNK
    qc = q.reshape(b, n_chunks, Q_CHUNK, h, d).swapaxes(0, 1)
    blk_off = jnp.arange(MOBA_BLOCK)
    bidx = jnp.arange(b)[:, None, None, None]
    hidx = jnp.arange(h)[None, None, :, None]
    if n_sel > 0:
        means = kb[:, :nb - 1].astype(jnp.float32).sum(axis=2) / MOBA_BLOCK

    def one_chunk(args):
        c, q_c = args
        q_pos = c * Q_CHUNK + jnp.arange(Q_CHUNK)
        blk = (c * Q_CHUNK) // MOBA_BLOCK
        k_own = lax.dynamic_index_in_dim(kb, blk, axis=1, keepdims=False)
        v_own = lax.dynamic_index_in_dim(vb, blk, axis=1, keepdims=False)
        own_pos = blk * MOBA_BLOCK + blk_off
        sel = None
        if n_sel > 0:
            idx, ok = _select_blocks(q_c, means, q_pos // MOBA_BLOCK, n_sel)
            k_sel = kb[bidx, idx, :, hidx].reshape(b, Q_CHUNK, h, n_sel * MOBA_BLOCK, d)
            v_sel = vb[bidx, idx, :, hidx].reshape(b, Q_CHUNK, h, n_sel * MOBA_BLOCK, d)
            sel_pos = (idx[..., None] * MOBA_BLOCK + blk_off).reshape(b, Q_CHUNK, h, -1)
            sel_ok = jnp.broadcast_to(ok[..., None], idx.shape + (MOBA_BLOCK,)).reshape(b, Q_CHUNK, h, -1)
            sel = (k_sel, v_sel, sel_pos, sel_ok)
        return _moba_core(q_c, q_pos, k_own, v_own, own_pos, rel_bias, sel)

    out = lax.map(one_chunk, (jnp.arange(n_chunks), qc))
    return out.swapaxes(0, 1).reshape(b, s, h, d)

def _moba_sample(q, k_new, v_new, cache_k, cache_v, page_table, rel_bias):
    db, t, h, d = q.shape
    n_pages = page_table.shape[1]
    past = n_pages * PAGE_SIZE
    ppb = MOBA_BLOCK // PAGE_SIZE
    cur = past // MOBA_BLOCK
    q_pos = past + jnp.arange(t)
    first_own_page = cur * ppb
    n_own_past = n_pages - first_own_page
    if n_own_past > 0:
        pt = page_table[:, first_own_page:]
        k_own = jnp.concatenate([cache_k[pt].reshape(db, n_own_past * PAGE_SIZE, h, d), k_new], axis=1)
        v_own = jnp.concatenate([cache_v[pt].reshape(db, n_own_past * PAGE_SIZE, h, d), v_new], axis=1)
    else:
        k_own, v_own = k_new, v_new
    own_pos = cur * MOBA_BLOCK + jnp.arange(k_own.shape[1])
    n_sel = min(MOBA_TOP_K, cur)
    if n_sel == 0:
        return _moba_core(q, q_pos, k_own, v_own, own_pos, rel_bias)
    page_sums = lax.map(lambda j: cache_k[page_table[:, j]].astype(jnp.float32).sum(axis=1),
                        jnp.arange(cur * ppb))
    means = page_sums.swapaxes(0, 1).reshape(db, cur, ppb, h, d).sum(axis=2) / MOBA_BLOCK
    idx, ok = _select_blocks(q, means, q_pos // MOBA_BLOCK, n_sel)
    pidx = jnp.arange(db)[:, None, None, None, None]
    hidx = jnp.arange(h)[None, None, :, None, None]
    page_off = jnp.arange(ppb)
    row_off = jnp.arange(PAGE_SIZE)

    def one_tok(args):
        q_t, idx_t, ok_t, pos_t = args
        q_t, idx_t, ok_t = q_t[:, None], idx_t[:, None], ok_t[:, None]
        logical = idx_t[..., None] * ppb + page_off
        phys = page_table[pidx, logical]
        k_sel = cache_k[phys, :, hidx].reshape(db, 1, h, n_sel * MOBA_BLOCK, d)
        v_sel = cache_v[phys, :, hidx].reshape(db, 1, h, n_sel * MOBA_BLOCK, d)
        sel_pos = (logical[..., None] * PAGE_SIZE + row_off).reshape(db, 1, h, -1)
        sel_ok = jnp.broadcast_to(ok_t[..., None, None], logical.shape + (PAGE_SIZE,)).reshape(db, 1, h, -1)
        o = _moba_core(q_t, pos_t[None], k_own, v_own, own_pos, rel_bias, (k_sel, v_sel, sel_pos, sel_ok))
        return o[:, 0]

    out = lax.map(one_tok, (q.swapaxes(0, 1), idx.swapaxes(0, 1), ok.swapaxes(0, 1), q_pos))
    return out.swapaxes(0, 1)

def _gated_delta_chunked(q, k, v, g, beta, s0, chunk):
    b, t, h, _ = q.shape
    dv = v.shape[-1]
    n = t // chunk

    def blocks(x):
        x = x.reshape((b, n, chunk, h) + x.shape[3:])
        return jnp.moveaxis(x, (1, 3), (0, 2))

    incl = jnp.tri(chunk, dtype=bool)
    strict = jnp.tri(chunk, k=-1, dtype=bool)
    eye = jnp.eye(chunk, dtype=jnp.float32)

    def step(s, xs):
        qc, kc, vc, gc, bc = xs
        cg = jnp.cumsum(gc, axis=-1)
        decay = jnp.exp(jnp.where(incl, cg[..., :, None] - cg[..., None, :], -jnp.inf))
        kk = jnp.einsum('bhid,bhjd->bhij', kc, kc)
        lower = eye + jnp.where(strict, bc[..., :, None] * decay * kk, 0.0)
        eg = jnp.exp(cg)
        rhs = bc[..., None] * vc - (bc * eg)[..., None] * jnp.einsum('bhcd,bhde->bhce', kc, s)
        u = lax.linalg.triangular_solve(lower, rhs, left_side=True, lower=True, unit_diagonal=True)
        qk = jnp.einsum('bhid,bhjd->bhij', qc, kc) * decay
        o = eg[..., None] * jnp.einsum('bhcd,bhde->bhce', qc, s) + jnp.einsum('bhij,bhje->bhie', qk, u)
        g_last = cg[..., -1]
        k_dec = kc * jnp.exp(g_last[..., None] - cg)[..., None]
        s_new = jnp.exp(g_last)[..., None, None] * s + jnp.einsum('bhcd,bhce->bhde', k_dec, u)
        return s_new, o

    s, o = lax.scan(step, s0, (blocks(q), blocks(k), blocks(v), blocks(g), blocks(beta)))
    o = jnp.moveaxis(o, (0, 2), (1, 3)).reshape(b, t, h, dv)
    return o, s

def _gated_deltanet(qkv, z, a, b_logit, conv_w, conv_prev, a_log, dt_bias, norm_w, s0):
    bsz, t, _ = qkv.shape
    qkv_c, conv_new = _causal_dwconv(qkv, conv_w, conv_prev)
    qkv_c = jax.nn.silu(qkv_c.astype(jnp.float32))
    q = qkv_c[..., 0:W_GDN].reshape(bsz, t, N_GDN_HEADS, HEAD_DIM)
    k = qkv_c[..., W_GDN:2 * W_GDN].reshape(bsz, t, N_GDN_HEADS, HEAD_DIM)
    v = qkv_c[..., 2 * W_GDN:3 * W_GDN].reshape(bsz, t, N_GDN_HEADS, HEAD_DIM)
    q = _l2norm(q) * HEAD_DIM ** -0.5
    k = _l2norm(k)
    beta = jax.nn.sigmoid(b_logit.astype(jnp.float32))
    g = -jnp.exp(a_log.astype(jnp.float32)) * jax.nn.softplus(a.astype(jnp.float32) + dt_bias.astype(jnp.float32))
    chunk = GDN_CHUNK if t % GDN_CHUNK == 0 else t
    o, s = _gated_delta_chunked(q, k, v, g, beta, s0.astype(jnp.float32), chunk)
    zg = jax.nn.silu(z.astype(jnp.float32)).reshape(bsz, t, N_GDN_HEADS, HEAD_DIM)
    o = o * lax.rsqrt(jnp.mean(o * o, axis=-1, keepdims=True) + EPS) * norm_w.astype(jnp.float32) * zg
    return o.reshape(bsz, t, W_GDN).astype(qkv.dtype), s.astype(s0.dtype), conv_new

def _conv_ffn(h, w_up, conv_w, conv_b, w_down, prev):
    u = h @ w_up
    u, new_prev = _causal_dwconv(u, conv_w, prev)
    gate, val = jnp.split(u + conv_b, 2, axis=-1)
    return (jax.nn.silu(gate) * val) @ w_down, new_prev

def _layer(x, gdn_s0, gdn_conv_prev, ffn_conv_prev, attend, rms_mix_w, w_in, gdn_conv_w, gdn_a_log,
           gdn_dt_bias, gdn_norm_w, w_out, rms_ffn_w, w_up, ffn_conv_w, ffn_conv_b, w_down):
    b, t, _ = x.shape
    p = _rmsnorm(x, rms_mix_w) @ w_in
    q_att = p[..., 0:W_ATT].reshape(b, t, N_ATT_HEADS, HEAD_DIM)
    k_att = p[..., W_ATT:2 * W_ATT].reshape(b, t, N_ATT_HEADS, HEAD_DIM)
    v_att = p[..., 2 * W_ATT:3 * W_ATT].reshape(b, t, N_ATT_HEADS, HEAD_DIM)
    o = 3 * W_ATT
    qkv_gdn = p[..., o:o + 3 * W_GDN]
    o += 3 * W_GDN
    z = p[..., o:o + W_GDN]
    o += W_GDN
    a = p[..., o:o + N_GDN_HEADS]
    o += N_GDN_HEADS
    b_logit = p[..., o:o + N_GDN_HEADS]
    att = attend(q_att, k_att, v_att).reshape(b, t, W_ATT)
    gdn, s_new, gconv_new = _gated_deltanet(qkv_gdn, z, a, b_logit, gdn_conv_w, gdn_conv_prev,
                                            gdn_a_log, gdn_dt_bias, gdn_norm_w, gdn_s0)
    x = x + jnp.concatenate([att, gdn], axis=-1) @ w_out
    f, fconv_new = _conv_ffn(_rmsnorm(x, rms_ffn_w), w_up, ffn_conv_w, ffn_conv_b, w_down, ffn_conv_prev)
    return x + f, k_att, v_att, s_new, gconv_new, fconv_new

def setup_inputs(seed: int = 0) -> dict:
    key = jax.random.key(seed)
    ks = jax.random.split(key, 24)
    f32 = jnp.float32
    n_pages = PAST_LEN // PAGE_SIZE
    n_pool = (5 * DEC_BATCH * n_pages + 3) // 4

    def nrm(k, shape, s):
        return jax.random.normal(k, shape, f32) * s

    page_table = jax.random.permutation(ks[4], n_pool)[:DEC_BATCH * n_pages].reshape(DEC_BATCH, n_pages).astype(jnp.int32)
    dt = jnp.exp(jax.random.uniform(ks[12], (DEPTH, N_GDN_HEADS), f32, math.log(1e-3), math.log(1e-1)))
    return {
        'x_prompt': nrm(ks[0], (BATCH, SEQ, D_MODEL), 1.0),
        'x_sample': nrm(ks[1], (DEC_BATCH, DEC_SEQ, D_MODEL), 1.0),
        'cache_k': nrm(ks[2], (DEPTH, n_pool, PAGE_SIZE, N_ATT_HEADS, HEAD_DIM), 1.0),
        'cache_v': nrm(ks[3], (DEPTH, n_pool, PAGE_SIZE, N_ATT_HEADS, HEAD_DIM), 1.0),
        'page_table': page_table,
        'state_gdn': nrm(ks[5], (DEPTH, DEC_BATCH, N_GDN_HEADS, HEAD_DIM, HEAD_DIM), 0.1),
        'state_gdn_conv': nrm(ks[6], (DEPTH, DEC_BATCH, GDN_CONV - 1, 3 * W_GDN), 1.0),
        'state_ffn_conv': nrm(ks[7], (DEPTH, DEC_BATCH, FFN_CONV - 1, 2 * D_FF), 1.0),
        'rms_mix_w': 1.0 + nrm(ks[8], (DEPTH, D_MODEL), 0.02),
        'w_in': nrm(ks[9], (DEPTH, D_MODEL, D_IN), D_MODEL ** -0.5),
        'gdn_conv_w': nrm(ks[10], (DEPTH, GDN_CONV, 3 * W_GDN), GDN_CONV ** -0.5),
        'gdn_a_log': jnp.log(jax.random.uniform(ks[11], (DEPTH, N_GDN_HEADS), f32, 1.0, 16.0)),
        'gdn_dt_bias': dt + jnp.log(-jnp.expm1(-dt)),
        'gdn_norm_w': 1.0 + nrm(ks[13], (DEPTH, HEAD_DIM), 0.02),
        'w_out': nrm(ks[14], (DEPTH, D_MODEL, D_MODEL), D_MODEL ** -0.5),
        'rms_ffn_w': 1.0 + nrm(ks[15], (DEPTH, D_MODEL), 0.02),
        'w_up': nrm(ks[16], (DEPTH, D_MODEL, 2 * D_FF), D_MODEL ** -0.5),
        'ffn_conv_w': nrm(ks[17], (DEPTH, FFN_CONV, 2 * D_FF), FFN_CONV ** -0.5),
        'ffn_conv_b': nrm(ks[18], (DEPTH, 2 * D_FF), 0.02),
        'w_down': nrm(ks[19], (DEPTH, D_FF, D_MODEL), D_FF ** -0.5),
        'rel_bias': nrm(ks[20], (NUM_BUCKETS, N_ATT_HEADS), 0.5),
        'final_norm_w': 1.0 + nrm(ks[21], (D_MODEL,), 0.02),
    }

def reference(x_prompt, x_sample, cache_k, cache_v, page_table, state_gdn, state_gdn_conv, state_ffn_conv,
              rms_mix_w, w_in, gdn_conv_w, gdn_a_log, gdn_dt_bias, gdn_norm_w, w_out, rms_ffn_w, w_up,
              ffn_conv_w, ffn_conv_b, w_down, rel_bias, final_norm_w):
    b = x_prompt.shape[0]
    dt = x_prompt.dtype
    xp, xs = x_prompt, x_sample
    kp_l, vp_l, sp_l, gcp_l, fcp_l = [], [], [], [], []
    ks_l, vs_l, ss_l, gcs_l, fcs_l = [], [], [], [], []
    attend_p = functools.partial(_moba_prompt, rel_bias=rel_bias)
    for l in range(DEPTH):
        wl = (rms_mix_w[l], w_in[l], gdn_conv_w[l], gdn_a_log[l], gdn_dt_bias[l], gdn_norm_w[l], w_out[l],
              rms_ffn_w[l], w_up[l], ffn_conv_w[l], ffn_conv_b[l], w_down[l])
        xp, kp, vp, sp, gcp, fcp = _layer(
            xp, jnp.zeros((b, N_GDN_HEADS, HEAD_DIM, HEAD_DIM), dt),
            jnp.zeros((b, GDN_CONV - 1, 3 * W_GDN), dt), jnp.zeros((b, FFN_CONV - 1, 2 * D_FF), dt),
            attend_p, *wl)
        attend_s = functools.partial(_moba_sample, cache_k=cache_k[l], cache_v=cache_v[l],
                                     page_table=page_table, rel_bias=rel_bias)
        xs, ks_, vs_, ss, gcs, fcs = _layer(xs, state_gdn[l], state_gdn_conv[l], state_ffn_conv[l], attend_s, *wl)
        kp_l.append(kp); vp_l.append(vp); sp_l.append(sp); gcp_l.append(gcp); fcp_l.append(fcp)
        ks_l.append(ks_); vs_l.append(vs_); ss_l.append(ss); gcs_l.append(gcs); fcs_l.append(fcs)
    y_prompt = _rmsnorm(xp, final_norm_w)
    y_sample = _rmsnorm(xs, final_norm_w)
    return (y_prompt, y_sample,
            jnp.stack(kp_l), jnp.stack(vp_l), jnp.stack(sp_l), jnp.stack(gcp_l), jnp.stack(fcp_l),
            jnp.stack(ks_l), jnp.stack(vs_l), jnp.stack(ss_l), jnp.stack(gcs_l), jnp.stack(fcs_l))


_drawn_inputs = setup_inputs


def setup_inputs(seed=0):
    import zlib

    import numpy as np

    out = dict(_drawn_inputs(seed))
    spreads = {}
    factors = {'gdn_norm_w': 6.364, 'rms_ffn_w': 2.745, 'ffn_conv_b': 4.121, 'final_norm_w': 2.765}
    for name, (base, spread) in spreads.items():
        noise = np.random.default_rng([zlib.crc32(name.encode()), seed]).standard_normal(out[name].shape)
        drawn = base * np.exp(spread * noise) if base else spread * noise
        out[name] = jnp.asarray(drawn.astype(out[name].dtype))
    for name, factor in factors.items():
        out[name] = (out[name] * factor).astype(out[name].dtype)
    return out
```

```python
import math

import numpy as np

import concourse.bass as bass
from concourse import mybir

F32 = mybir.dt.float32
F32R = mybir.dt.float32r
I32 = mybir.dt.int32
ACT = mybir.ActivationFunctionType
ALU = mybir.AluOpType
AX = mybir.AxisListType

P = 128
DM = 2048
KT = DM // P
SEQ, DB, DT = 256, 8, 8
NS = DB * DT
TOK = SEQ + NS
NH = 8
W = NH * P
DIN = 7 * W + 2 * NH
DFF = 5632
FT = DFF // P
NBK = 32
NEG = -1e30
EPS = 1e-6
SCALE = P ** -0.5
CQ = 4
CC = 256
RING = 4

LEVELS = [1, 2, 4, 8, 16, 32, 64]
CONST_COLS = {}


def constants():
    i = np.arange(P)
    c, r = i[None, :], i[:, None]
    parts = {
        "ident": c == r,
        "flip": c == P - 1 - r,
        "ones": np.ones((P, P)),
        "upto": r <= c,
        "upto8": (r <= c) & (r // DT == c // DT),
        "same8": r // DT == c // DT,
        "negP": np.where(r <= c, 0.0, NEG),
        "neg8": np.where((r <= c) & (r // DT == c // DT), 0.0, NEG),
        "causal": np.where(c <= r, 0.0, NEG),
        "batch": (r // DT == np.arange(DB)[None, :]),
    }
    for s in LEVELS:
        parts[f"lev{s}"] = (r // (2 * s) == c // (2 * s)) & (r // s != c // s) & (r < c)
    m = np.arange(3 * P)
    n = np.maximum(2 * P - 1 - m, 0)
    nf = np.maximum(n, 1).astype(np.float32)
    half = NBK // 2
    large = half + (np.log(nf / np.float32(half)) / np.float32(math.log(128 / half)) * half).astype(np.int32)
    bucket = np.where(n < half, n, np.minimum(large, NBK - 1))
    parts["bucket"] = np.concatenate([bucket[None, :] == np.arange(NBK)[:, None], np.zeros((P - NBK, 3 * P))], 0)
    at = 0
    for k, v in parts.items():
        CONST_COLS[k] = (at, v.shape[1])
        at += v.shape[1]
    return np.concatenate([np.asarray(v, np.float32) for v in parts.values()], 1)


CONSTS = constants()


PHASES = [("g0", 8, 4), ("g1", 8, 4), ("a0", 6, 4), ("a1", 6, 4), ("wg", 8, 2), ("wa", 8, 2)]


def chunk_list():
    out = []
    for name, pairs, per in PHASES:
        for p in range(pairs):
            for q in range(per):
                out.append((name, p, q, per))
    return out


CHUNKS = chunk_list()
NC1 = len(CHUNKS)
FIRST = {}
for _n, (_name, _p, _q, _per) in enumerate(CHUNKS):
    FIRST.setdefault(_name, _n)
FIRST["end"] = NC1
PAIRS = [(n, p) for n, ps, _ in PHASES for p in range(ps)]


def pair_index(name, p):
    return PAIRS.index((name, p))


def tile_of(name, p, j):
    t = 2 * p + j
    return t // 4, t % 4


def setup_steps():
    s = [("V", "init"), ("A", "alog"), ("P", "rows"), ("V", "rows"), ("A", "prev"), ("P", "rb"), ("A", "rb"), ("G", "rbout")]
    for t in range(3):
        s += [("A", "sq", t), ("V", "ms", t), ("G", "rs", t), ("V", "xs", t)]
        for q in range(4):
            s += [("P", "xt", t, q), ("V", "xw", t, q), ("A", "xh", t, q), ("V", "xl", t, q)]
    return s


def scalar_steps():
    return [("V", "wab"), ("P", "ab"), ("A", "ab"), ("P", "abt"), ("V", "sc1"), ("A", "sc2"), ("V", "sc3"), ("P", "cum"),
            ("V", "sc4"), ("A", "sc5")]


def raw_steps():
    return [x for t in range(3) for q in range(4) for x in (("P", "rt", t, q), ("A", "rt", t, q))]


def gdn_steps(g):
    s = []
    for u in (0, 1, 2):
        k = (g, u)
        s += [("P", "tr", *k), ("A", "cp", *k), ("V", "ss", *k), ("G", "rn", *k), ("V", "sc", *k),
              ("P", "tb1", *k), ("A", "tb1", *k), ("V", "tb1", *k), ("P", "tb2", *k), ("A", "tb2", *k),
              ("V", "gt", *k), ("P", "cg", *k), ("V", "dm", *k), ("A", "de", *k), ("P", "kk", *k),
              ("V", "kk", *k), ("P", "x1", *k), ("A", "x1", *k)]
        levels = LEVELS[1:] if u < 2 else [2, 4]
        for l in levels:
            s += [("P", "pl", *k, l), ("A", "pl", *k, l), ("P", "dl", *k, l), ("V", "dl", *k, l)]
        if u == 1:
            s += [("P", "ks", *k), ("V", "ks", *k)]
        if u == 2:
            for h in range(4):
                s += [("G", "si", g, h), ("P", "sh", g, h)]
            s += [("A", "sh", g, 0), ("P", "ks", *k), ("V", "ks", *k)]
        s += [("P", "u", *k), ("A", "u", *k), ("P", "os", *k)]
        if u < 2:
            s += [("V", "st", *k)]
            if u == 1:
                s += [("G", "so", g, 4)]
        s += [("A", "o", *k), ("V", "o1", *k), ("G", "or", *k), ("V", "o2", *k), ("P", "ot", *k), ("V", "oz", *k)]
        if u == 2:
            for h in range(4):
                s += [("G", "s2", g, h), ("V", "um", g, h), ("P", "us", g, h), ("V", "us", g, h), ("G", "so", g, h)]
    return s


def state_steps():
    s = []
    for r in range(6):
        s += [("P", "gs", r), ("A", "gs", r), ("G", "gs", r)]
    return s


def att_steps(g):
    s = [("G", "hk", g), ("P", "hk", g), ("V", "hk", g)]
    for t in range(3):
        s += [("P", "kv", g, t), ("A", "kv", g, t), ("G", "kv", g, t)]
    for h in range(4):
        s += [("P", "S", g, h), ("V", "S", g, h), ("A", "E", g, h), ("V", "N", g, h), ("P", "T", g, h),
              ("A", "T", g, h), ("P", "O", g, h), ("A", "O", g, h)]
    for b in range(DB):
        s += [("G", "pg", g, b), ("P", "kt", g, b), ("A", "kt", g, b), ("V", "kt", g, b), ("P", "SS", g, b), ("V", "SS", g, b),
              ("A", "SE", g, b), ("V", "SN", g, b), ("P", "PT", g, b), ("A", "PT", g, b), ("P", "PV", g, b),
              ("A", "PV", g, b), ("P", "OT", g, b), ("A", "OT", g, b)]
    return s


def ffn_param_steps():
    s = []
    for r in range(5):
        s += [("P", "fp", r), ("A", "fp", r)]
    return s


def schedule():
    slots = {c: [] for c in range(-1, NC1)}

    def spread(steps, lo, hi):
        n = len(steps)
        for i, x in enumerate(steps):
            slots[lo + i * (hi - lo) // n].append(x)

    slots[-1] = setup_steps()
    spread(scalar_steps(), 0, 8)
    spread(raw_steps(), 8, FIRST["g1"] - 1)
    spread(gdn_steps(0), FIRST["g1"] + 2, FIRST["a0"] - 1)
    spread(state_steps(), FIRST["a0"] + 1, FIRST["a0"] + 2)
    spread(gdn_steps(1), FIRST["a0"] + 2, FIRST["a1"] - 1)
    spread(att_steps(0), FIRST["a1"] + 2, FIRST["wg"] - 1)
    spread(att_steps(1), FIRST["wg"] + 2, FIRST["wa"] - 1)
    slots[FIRST["wg"] - 1] += [("A", "mg"), ("V", "mg")]
    slots[FIRST["wa"] - 1] += [("A", "ma"), ("V", "ma")]
    slots[FIRST["wa"]] += [("G", "fload")]
    spread(ffn_param_steps(), FIRST["wa"] + 1, NC1 - 1)
    return slots


SLOTS = schedule()


TRANSFERS = {"si", "s2", "so", "gs", "hk", "kv", "pg"}


def tallies():
    n, at = {}, {}
    for c in sorted(SLOTS):
        for x in SLOTS[c]:
            if x[0] == "G" and x[1] in TRANSFERS:
                continue
            n[x[0]] = n.get(x[0], 0) + 1
            at[x] = n[x[0]]
    return at


TALLY = tallies()

NGA = 28
NB = FT // 4
NLOOP = (NB - 1) // 2
NROWS = 10


def before_unit(g, u):
    if u:
        return ("V", "oz", g, u - 1)
    return ("V", "us", 0, 3) if g else ("A", "rt", 2, 3)


def wa_pair(c):
    d = c - FIRST["wa"]
    return d // 2 if d >= 0 and d % 2 == 1 and c < NC1 else None


def block_start(blk):
    if isinstance(blk, int) and blk == 0:
        return NC1
    return blk * 24 + (NC1 + 16 - 24)


def down_start(blk):
    return blk * 24 + (NC1 + 16 + 16) if not (isinstance(blk, int) and blk == NB - 1) else NC1 + 16 + 24 * (NB - 1)


def heads(ap, n):
    return ap[:, 0:4 * n].rearrange("p (h n) -> p h n", h=4)


def build(nc, I, O):
    base = -(-nc.sbuf_base // 64) * 64
    top = nc.sbuf_usable_end

    class Span:
        def __init__(self, at):
            self.at = at

        def put(self, name, shape, dt=F32):
            size = 4 * int(np.prod(shape[1:]))
            t = nc.alloc_sbuf_tensor_at(name, shape, dt, offset=self.at)
            self.at += -(-size // 64) * 64
            assert self.at <= top, (name, self.at - top)
            return t

    sp_ = Span(base)
    raw = sp_.put("w_raw", [P, RING, CQ, CC])
    whi = sp_.put("w_hi", [P, RING, CQ, CC], F32R)
    wlo = sp_.put("w_lo", [P, RING, CQ, CC], F32R)
    xres = sp_.put("x_res", [P, KT, TOK])
    yo_at = sp_.at
    xhi = sp_.put("x_hi", [P, KT, TOK], F32R)
    xlo = sp_.put("x_lo", [P, KT, TOK], F32R)
    cst = sp_.put("consts", [P, CONSTS.shape[1]])
    small = sp_.put("small", [P, 640])
    pT = sp_.put("params_t", [P, 160])
    ptab = sp_.put("page_table_row", [1, 16], I32)
    mixer_at = sp_.at

    m = Span(mixer_at)
    reg = [m.put(f"reg{g}", [P, 12, TOK]) for g in range(2)]
    zz = m.put("z_gate", [P, 8, TOK])
    work_at = m.at
    qn = m.put("q_norm", [P, 4, TOK])
    kb = m.put("k_beta", [P, 4, TOK])
    setat = m.at
    tq = m.put("tok_q", [P, 4, P])
    tk = m.put("tok_k", [P, 4, P])
    bv = m.put("tok_bv", [P, 4, P])
    qk = m.put("qk_t", [P, 4, P])
    at_ = m.put("a_t", [P, 4, P])
    xx = m.put("inv", [P, 4, P])
    pp = m.put("prod", [P, 4, P])
    dec = m.put("decay", [P, 4, P])
    xt = m.put("inv_t", [P, 4, P])
    ub = m.put("u_tok", [P, 4, P])
    S = m.put("state", [P, 4, P])
    ssm = m.put("state_s", [P, DB, P])
    ue_at = m.at
    ue = m.put("u_ext", [P, 2, 348])
    acc = m.put("conv_acc", [P, 2, 348])
    prevT = m.put("prev_t", [P, DB * 3, 24])
    gnew = m.put("gdn_new", [P, 27, 24])
    umask = nc.alloc_sbuf_tensor_at("u_mask", [P, DB, P], F32, offset=setat + 4 * 2048)
    w = Span(work_at)
    xraw = w.put("x_raw", [P, 3, DM])
    tmpx = w.put("x_tmp", [P, 2, 4, P])
    prow = w.put("p_rows", [P, 7, P])
    assert w.at <= work_at + 5120 * 2 + 2048 * 10 + 2048 + 4096
    r0 = Span(mixer_at)
    xs = r0.put("x_scaled", [P, 2, DM])
    wab = r0.put("w_ab", [P, KT, 16])
    wabh = r0.put("w_ab_hi", [P, KT * 16 + 112], F32R)
    wabl = r0.put("w_ab_lo", [P, KT * 16 + 112], F32R)
    abT = r0.put("ab_t", [P, TOK])
    rsb0 = r0.put("rb_rows", [P, 3 * P])
    a = Span(work_at)
    vt = a.put("v_tok", [P, 3, 4, P])
    kst = a.put("k_tok", [P, 4, P])
    hk = a.put("hankel", [P, 4, 2 * P])
    bm = a.put("bias_q", [P, 4, 2 * P])
    bs = a.put("bias_s", [P, 2 * P + 120])
    sc = a.put("scores", [P, 2, 384])
    pt = a.put("probs_t", [P, 2, 384])
    ktp = a.put("k_t_past", [P, 4, 2 * P])
    kp = a.put("k_pages", [P, 2, 4, P])
    vp = a.put("v_pages", [P, 2, 4, P])
    ob = a.put("o_tok", [P, P])
    ast = a.put("att_small", [P, 16])
    assert a.at <= work_at + 10240 + 20480 + 2048 + 4096 + 2800 + 2800 + 2304
    gst = nc.alloc_sbuf_tensor_at("gdn_new_rows", [P, 6, P], F32, offset=ue_at)

    fm = Span(mixer_at)
    pF = fm.put("ffn_params_t", [P, 2 * FT, 20])
    fnewT = fm.put("ffn_new_t", [P, 2 * FT, 18])
    frow = fm.put("ffn_rows", [P, 20, P])
    hhi = fm.put("hid_hi", [P, 2, 4, TOK], F32R)
    hlo = fm.put("hid_lo", [P, 2, 4, TOK], F32R)
    hf = fm.put("hid", [P, 2, 2, TOK])
    fue = fm.put("ffn_ext", [P, 2, 2, 338])
    facc = fm.put("ffn_acc", [P, 2, 2, 338])
    sqb = fm.put("squares", [P, 2, 2, TOK])
    rs2 = fm.put("root", [P, TOK])
    xn = fm.put("x_normed", [P, 2, 4, TOK])
    fst = fm.put("ffn_stage", [P, 2, 2, 4, 20])
    yo = nc.alloc_sbuf_tensor_at("y_rows", [P, 3, DM], F32, offset=yo_at)

    n_pool = I["cache_k"].shape[1]
    rb_dram = nc.dram_tensor("rb_scratch", (NH, 3 * P), F32, kind="Internal").ap()
    psA = nc.alloc_psum_tensor("ps_proj", [P, 4, 512], F32)
    psB = nc.alloc_psum_tensor("ps_small", [P, 4, 512], F32)
    b0, b1, b2, b3 = (psB[:, i, :] for i in range(4))

    def C(name, n=P, m_=None):
        at, width = CONST_COLS[name]
        return cst[0:n, at:at + (width if m_ is None else m_)]

    cols = {}
    at = 0
    for name, n in (("ssx", 3), ("rsx", 3), ("mh", 8), ("dtb", 8), ("alog", 8), ("ab", 48), ("sa", 24), ("sb", 24),
                    ("beta", 24), ("g", 24), ("cg", 24), ("eg", 24), ("kd", 24), ("eglP", 16), ("eglS", 64),
                    ("ss", 8), ("rn", 8), ("f", 24), ("so", 4), ("ro", 4), ("gm", 64), ("nkd", 24), ("rb", 8), ("tmp", 24)):
        cols[name] = (at, n)
        at += n
    assert at <= 640

    def sm(name, n=P, lo=0, hi=None):
        a0, width = cols[name]
        return small[0:n, a0 + lo:a0 + (width if hi is None else hi)]

    def over_free(ap, count):
        return ap.unsqueeze(2).broadcast_to([ap.shape[0], ap.shape[1], count])

    def over_heads(ap, count):
        return ap.unsqueeze(1).broadcast_to([ap.shape[0], count, ap.shape[1]])

    def per_head(name, n, u, g):
        return sm(name, n, 8 * u + 4 * g, 8 * u + 4 * g + 4)

    def f_sample(kind, j):
        return facc[:, kind, j, 258:338].rearrange("p (b s) -> p b s", b=DB)[:, :, 0:DT]

    def sample_of_acc(j):
        return acc[:, j, 259:347].rearrange("p (b s) -> p b s", b=DB)[:, :, 0:DT]

    sems = {}

    def sem(name):
        sems[name] = nc.alloc_semaphore(name)
        return sems[name]

    raw_in = [sem(f"raw_in{i}") for i in range(RING)]
    hi_done, lo_done, mm_done = sem("hi_done"), sem("lo_done"), sem("mm_done")
    evac_done, conv_done, silu_done = sem("evac_done"), sem("conv_done"), sem("silu_done")
    pads_done, new_done, add_done = sem("pads_done"), sem("new_done"), sem("add_done")
    done = {"P": sem("pe_step"), "V": sem("dve_step"), "A": sem("act_step"), "G": sem("pool_step")}
    link_sem = {"V": sem("dve_link"), "A": sem("act_link"), "G": sem("pool_link")}
    consts_in, rows_in, x_in = sem("consts_in"), sem("rows_in"), [sem(f"x_in{t}") for t in range(3)]
    ab_in, pt_in = sem("ab_in"), sem("page_table_in")
    rb_out, hk_in, kv_out = sem("rb_out"), sem("hankel_in"), sem("kv_out")
    pg_in, s_in, s_out, st_out, gs_out, fl_in = (sem("pages_in"), sem("state_in"), sem("state_out"), sem("stateP_out"),
                                                 sem("gnew_out"), sem("ffn_rows_in"))
    sq2, ssq2, xn_a, xn_v, xn_h = sem("sq2"), sem("ssq2"), sem("rms2_root"), sem("xn_made"), sem("xn_hi")
    xn_l, rms_v = sem("xn_lo"), sem("rms_mean")
    f = {k: sem("ffn_" + k) for k in ("evac", "pad", "conv", "silu", "h", "hhi", "hlo", "add", "stage", "tap")}
    fin = {k: sem("fin_" + k) for k in ("sq", "ss", "ms", "root", "rs", "y", "t", "ev", "out", "nt", "ne", "no")}

    links = {"V": 0, "A": 0, "G": 0}

    def link(e, E, ins):
        links[E] += 1
        ins.then_inc(link_sem[E], 1)
        e.wait_ge(link_sem[E], links[E])

    def after(e, *key):
        e.wait_ge(done[key[0]], TALLY[key])

    def unit(u):
        return (P, u * P) if u < 2 else (NS, SEQ)

    w_in, w_out, w_up, w_down = (I[k][0] for k in ("w_in", "w_out", "w_up", "w_down"))

    def chunk_source(c):
        name, p, q, per = CHUNKS[c]
        if name[0] == "w":
            k0 = (q + (2 if name == "wg" else 0)) * CQ
            return w_out[k0 * P:(k0 + CQ) * P, p * CC:(p + 1) * CC].rearrange("(k p) n -> p k n", p=P)
        kind, _ = tile_of(name, p, 0)
        g = int(name[1])
        col = (3 * W if name[0] == "g" else 0) + kind * W + g * 512 + (p % 2) * CC
        return w_in[q * CQ * P:(q + 1) * CQ * P, col:col + CC].rearrange("(k p) n -> p k n", p=P)

    block = nc.Block()
    with block:
        @block.sync
        def _(sp):
            def load(slot, src, use):
                sp.dma_start(raw[:, slot], src).then_inc(raw_in[slot], 16)

            for t, (r_, n) in enumerate(((0, P), (P, P), (0, NS))):
                x = I["x_prompt"][0] if t < 2 else I["x_sample"].rearrange("b t d -> (b t) d")
                sp.dma_start(xraw[0:n, t], x[r_:r_ + n, :]).then_inc(x_in[t], 16)
                if t == 0:
                    sp.dma_start(cst[:, :], I["consts"]).then_inc(consts_in, 16)
            for c in range(NC1):
                if c >= RING:
                    sp.wait_ge(hi_done, c - RING + 1)
                    sp.wait_ge(lo_done, c - RING + 1)
                load(c % RING, chunk_source(c), c)

            def up_source(i, q):
                pp_, kind, kq = q // 8, (q // 4) % 2, q % 4
                rows = w_up[kq * CQ * P:(kq + 1) * CQ * P, :].rearrange("(k p) n -> p k n", p=P)
                return rows[:, :, bass.DynSlice(i * 512 + kind * DFF + pp_ * CC, CC)]

            def down_source(i, d):
                return w_down[bass.DynSlice(i * 512, 512), d * CC:(d + 1) * CC].rearrange("(k p) n -> p k n", p=P)

            def stream(c, src):
                sp.wait_ge(hi_done, c - RING + 1)
                sp.wait_ge(lo_done, c - RING + 1)

            c = NC1
            for q in range(16):
                stream(c + q, None)
                load((c + q) % RING, up_source(0, q), None)
            c += 16
            with sp.Fori(0, NLOOP) as it:
                for t in range(48):
                    half, q = t // 24, t % 24
                    stream(it * 48 + (c + t), None)
                    i = it * 2 + half
                    load(t % RING, up_source(i + 1, q) if q < 16 else down_source(i, q - 16), None)
            c += 48 * NLOOP
            for d in range(8):
                stream(c + d, None)
                load(d % RING, down_source(NB - 1, d), None)

        @block.scalar
        def _(act):
            def finish(ins):
                ins.then_inc(done["A"], 1)

            def hi_part(c, slot, use):
                act.wait_ge(raw_in[slot], use * 16 + 16)
                if not isinstance(c, int) or c >= RING:
                    act.wait_ge(mm_done, c - RING + 1)
                act.activation(whi[:, slot], raw[:, slot], ACT.Copy).then_inc(hi_done, 1)

            def evac(n):
                name, p = PAIRS[n]
                bank = 2 * (n % 2)
                kind, h = tile_of(name, p, 0)
                g = int(name[1])
                act.wait_ge(mm_done, FIRST[name] + 4 * p + 4)
                two = psA[:, bank:bank + 2, 0:TOK]
                if name[0] == "a":
                    if p == 0:
                        after(act, "V", "us", g, 3)
                        after(act, "V", "oz", g, 2)
                        after(act, "P", "us", g, 3)
                    act.activation(reg[g][:, kind * 4 + h:kind * 4 + h + 2, :], two, ACT.Copy).then_inc(evac_done, 1)
                elif kind == 3:
                    act.activation(zz[:, g * 4 + h:g * 4 + h + 2, :], two, ACT.Silu).then_inc(evac_done, 1)
                else:
                    gp = g * 6 + p
                    if gp >= 1:
                        act.wait_ge(conv_done, gp)
                        act.wait_ge(new_done, gp)
                    act.activation(ue[:, :, 3:3 + SEQ], two[:, :, 0:SEQ], ACT.Copy)
                    for j in range(2):
                        ins = act.activation(ue[:, j, 3 + SEQ:347].rearrange("p (b s) -> p b s", b=DB)[:, :, 3:11],
                                             two[:, j, SEQ:TOK].rearrange("p (b t) -> p b t", b=DB), ACT.Copy)
                    ins.then_inc(evac_done, 1)

            def silu(n):
                name, p = PAIRS[n]
                kind, h = tile_of(name, p, 0)
                g = int(name[1])
                gp = g * 6 + p
                act.wait_ge(conv_done, gp + 1)
                if n == 0:
                    act.wait_ge(rb_out, 16)
                t = kind * 4 + h
                act.activation(reg[g][:, t:t + 2, 0:SEQ], acc[:, :, 0:SEQ], ACT.Silu)
                for j in range(2):
                    ins = act.activation(reg[g][:, t + j, SEQ:TOK].rearrange("p (b t) -> p b t", b=DB),
                                         sample_of_acc(j), ACT.Silu)
                ins.then_inc(silu_done, 1)

            def step(x):
                name = x[1]
                k = x[2:]
                if name == "alog":
                    act.wait_ge(rows_in, 16 * NROWS)
                    finish(act.activation(sm("alog"), sm("alog"), ACT.Exp))
                elif name == "prev":
                    after(act, "P", "rows")
                    act.activation(prevT[:, :, :].rearrange("p r f -> p (r f)")[:, 0:512], b1, ACT.Copy)
                    finish(act.activation(prevT[:, :, :].rearrange("p r f -> p (r f)")[:, 512:576], b2[:, 0:64], ACT.Copy))
                elif name == "rb":
                    after(act, "P", "rb")
                    finish(act.activation(rsb0[0:NH, :], b3[0:NH, 0:3 * P], ACT.Copy))
                elif name == "sq":
                    t = k[0]
                    n = unit(t)[0]
                    act.wait_ge(x_in[t], 16)
                    if t >= 2:
                        after(act, "P", "xt", t - 2, 3)
                    elif t == 0:
                        after(act, "V", "init")
                    finish(act.activation(xs[0:n, t % 2], xraw[0:n, t], ACT.Square, accum_out=sm("ssx", n, t, t + 1)))
                elif name == "xh":
                    t, q = k
                    n, c0 = unit(t)
                    after(act, "V", "xw", t, q)
                    finish(act.activation(xhi[:, 4 * q:4 * q + 4, c0:c0 + n], tmpx[:, q % 2, :, 0:n], ACT.Copy))
                elif name == "rt":
                    t, q = k
                    n, c0 = unit(t)
                    after(act, "P", "rt", t, q)
                    finish(act.activation(xres[:, 4 * q:4 * q + 4, c0:c0 + n],
                                          b3[:, 0:4 * n].rearrange("p (k n) -> p k n", k=4), ACT.Copy))
                elif name == "ab":
                    after(act, "P", "ab")
                    finish(act.activation(abT[0:16, :], b0[0:16, 0:TOK], ACT.Copy))
                elif name == "sc2":
                    after(act, "V", "sc1")
                    link(act, "A", act.activation(sm("sb"), sm("sb"), ACT.Exp, scale=-1.0))
                    act.activation(sm("tmp").rearrange("p (u h) -> p u h", u=3),
                                   sm("ab").rearrange("p (u c) -> p u c", u=3)[:, :, 8:16], ACT.Exp, scale=-1.0)
                    finish(act.activation(sm("sb"), sm("sb"), ACT.Ln, bias=1.0))
                elif name == "sc5":
                    after(act, "V", "sc4")
                    act.activation(sm("eg"), sm("cg"), ACT.Exp)
                    act.activation(sm("kd"), sm("nkd"), ACT.Exp)
                    act.activation(sm("eglP"), b2[:, 24:40], ACT.Exp)
                    finish(act.activation(sm("eglS"), b2[:, 64:128], ACT.Exp))
                elif name == "cp":
                    g, u = k
                    n, _ = unit(u)
                    after(act, "P", "tr", g, u)
                    after(act, *before_unit(g, u))
                    act.activation(tq[0:n].rearrange("p h d -> p (h d)"), b0[0:n], ACT.Copy)
                    act.activation(tk[0:n].rearrange("p h d -> p (h d)"), b1[0:n], ACT.Copy)
                    act.activation(xt[0:n].rearrange("p h d -> p (h d)"), b0[0:n], ACT.Square)
                    finish(act.activation(xx[0:n].rearrange("p h d -> p (h d)"), b1[0:n], ACT.Square))
                elif name == "tb1":
                    g, u = k
                    n, c0 = unit(u)
                    after(act, "P", "tb1", g, u)
                    act.activation(qn[:, :, c0:c0 + n], heads(b0, n), ACT.Copy)
                    finish(act.activation(reg[g][:, 4:8, c0:c0 + n], heads(b1, n), ACT.Copy))
                elif name == "tb2":
                    g, u = k
                    n, c0 = unit(u)
                    after(act, "P", "tb2", g, u)
                    finish(act.activation(reg[g][:, 0:4, c0:c0 + n], heads(b0, n), ACT.Copy))
                elif name == "de":
                    n = unit(k[1])[0]
                    after(act, "V", "dm", *k)
                    finish(act.activation(dec[0:n, :, 0:n], dec[0:n, :, 0:n], ACT.Exp))
                elif name in ("x1", "pl"):
                    n = unit(k[1])[0]
                    after(act, "P", name, *k)
                    if name == "x1":
                        after(act, "V", "kk", *k[:2])
                    dst = xx if name == "x1" else pp
                    finish(act.activation(dst[0:n, :, 0:n], heads(b0[0:n], n), ACT.Copy))
                elif name == "u":
                    n = unit(k[1])[0]
                    after(act, "P", "u", *k)
                    finish(act.activation(ub[0:n].rearrange("p h d -> p (h d)"), b1[0:n], ACT.Copy))
                elif name == "sh":
                    after(act, "P", "sh", k[0], 3)
                    finish(act.activation(pp[:, :, :].rearrange("p h d -> p (h d)"), b0, ACT.Copy))
                elif name == "o":
                    n = unit(k[1])[0]
                    after(act, "P", "os", *k)
                    act.activation(tq[0:n].rearrange("p h d -> p (h d)"), b2[0:n], ACT.Copy)
                    finish(act.activation(xx[0:n].rearrange("p h d -> p (h d)"), b2[0:n], ACT.Square))
                elif name == "gs":
                    r = k[0]
                    n = min(P, 648 - r * P)
                    after(act, "P", "gs", r)
                    finish(act.activation(gst[0:n, r, :], psB[0:n, r % 2, 0:P], ACT.Copy))
                elif name == "kv":
                    g, t = k
                    n = unit(t)[0]
                    after(act, "P", "kv", g, t)
                    if g == 0 and t == 0:
                        after(act, "V", "us", 1, 3)
                        act.wait_ge(hk_in, 16)
                    if 3 * g + t >= 1:
                        act.wait_ge(kv_out, 32 * (3 * g + t))
                    act.activation(kst[0:n].rearrange("p h d -> p (h d)"), b0[0:n], ACT.Copy)
                    finish(act.activation(vt[0:n, t].rearrange("p h d -> p (h d)"), b1[0:n], ACT.Copy))
                elif name == "E":
                    g, h = k
                    after(act, "V", "S", g, h)
                    s_ = sc[:, h % 2]
                    act.activation(s_[:, 0:256], s_[:, 0:256], ACT.Exp, bias=ast[:, 0:1], accum_out=ast[:, 2:3])
                    finish(act.activation(s_[:, 256:384], s_[:, 256:384], ACT.Exp, bias=ast[:, 1:2], accum_out=ast[:, 3:4]))
                elif name == "T":
                    g, h = k
                    after(act, "P", "T", g, h)
                    finish(act.activation(pt[:, h % 2], b2[:, 0:384], ACT.Copy))
                elif name == "O":
                    g, h = k
                    after(act, "P", "O", g, h)
                    finish(act.activation(reg[g][:, h, 0:SEQ], b3[:, 0:SEQ], ACT.Copy))
                elif name == "kt":
                    after(act, "P", "kt", *k)
                    finish(act.activation(ktp[:, :, 0:P], heads(b0, P), ACT.Copy))
                elif name == "SE":
                    after(act, "V", "SS", *k)
                    finish(act.activation(sc[:, 0, 0:TOK], sc[:, 0, 0:TOK], ACT.Exp, bias=ast[:, 0:1], accum_out=ast[:, 2:3]))
                elif name == "PT":
                    after(act, "P", "PT", *k)
                    act.activation(pt[:, 0, 0:256], b3[:, 0:256], ACT.Copy)
                    finish(act.activation(pt[0:NS, 0, 256:384], b3[0:NS, 256:384], ACT.Copy))
                elif name == "PV":
                    after(act, "P", "PV", *k)
                    finish(act.activation(ob[:, :], b0[:, 0:P], ACT.Copy))
                elif name == "OT":
                    g, b = k
                    after(act, "P", "OT", *k)
                    finish(act.activation(reg[g][:, 0:4, SEQ + b * DT:SEQ + b * DT + DT],
                                          b1[:, 0:P].rearrange("p (h s) -> p h s", h=4)[:, :, 0:DT], ACT.Copy))
                elif name == "mg":
                    after(act, "V", "oz", 1, 2)
                    act.wait_ge(mm_done, FIRST["wg"])
                    finish(act.activation(xhi[:, 8:16, :], zz[:, :, :], ACT.Copy))
                elif name == "ma":
                    after(act, "A", "OT", 1, DB - 1)
                    act.activation(xhi[:, 0:4, :], reg[0][:, 0:4, :], ACT.Copy)
                    finish(act.activation(xhi[:, 4:8, :], reg[1][:, 0:4, :], ACT.Copy))
                elif name == "fp":
                    r = k[0]
                    after(act, "P", "fp", r)
                    finish(act.activation(pF[:, :, 4 * r:4 * r + 4].rearrange("p f j -> p j f"),
                                          psB[:, r % 2, 0:4 * 88].rearrange("p (j f) -> p j f", j=4), ACT.Copy))
                else:
                    raise KeyError(x)

            def square2(p):
                act.wait_ge(add_done, 8 + p + 1)
                if p >= 2:
                    act.wait_ge(ssq2, p - 1)
                act.activation(sqb[:, p % 2], xres[:, 2 * p:2 * p + 2, :], ACT.Square).then_inc(sq2, 1)

            for x in SLOTS[-1]:
                if x[0] == "A":
                    step(x)
            for c in range(3):
                hi_part(c, c % RING, c // RING)
            for c in range(NC1):
                if c + 3 < NC1:
                    hi_part(c + 3, (c + 3) % RING, (c + 3) // RING)
                for n, (name, p) in enumerate(PAIRS[:NGA]):
                    if c - 1 == FIRST[name] + 4 * p + 3:
                        evac(n)
                    if c - 2 == FIRST[name] + 4 * p + 3 and name[0] == "g" and p < 6:
                        silu(n)
                for x in SLOTS[c]:
                    if x[0] == "A":
                        step(x)
                if wa_pair(c - 2) is not None:
                    p = wa_pair(c - 2)
                    square2(p)
            for p in range(7, 8):
                square2(p)
            act.wait_ge(rms_v, 1)
            act.activation(rs2[:, :], rs2[:, :], ACT.Sqrt).then_inc(xn_a, 1)
            for q in range(4):
                act.wait_ge(xn_v, q + 1)
                act.activation(xhi[:, 4 * q:4 * q + 4, :], xn[:, q % 2], ACT.Copy).then_inc(xn_h, 1)

            def f_evac(blk, r):
                n, kind = blk * 4 + r, r % 2
                act.wait_ge(mm_done, block_start(blk) + 4 * r + 4)
                if not isinstance(n, int) or n >= 2:
                    act.wait_ge(f["conv"], n - 1)
                two = psA[:, 2 * kind:2 * kind + 2, 0:TOK]
                act.activation(fue[:, kind, :, 2:2 + SEQ], two[:, :, 0:SEQ], ACT.Copy)
                for j in range(2):
                    ins = act.activation(fue[:, kind, j, 2 + SEQ:338].rearrange("p (b s) -> p b s", b=DB)[:, :, 2:10],
                                         two[:, j, SEQ:TOK].rearrange("p (b t) -> p b t", b=DB), ACT.Copy)
                ins.then_inc(f["evac"], 1)

            def f_silu(n):
                act.wait_ge(f["conv"], n + 1)
                act.activation(facc[:, 0, :, 0:336], facc[:, 0, :, 0:336], ACT.Silu).then_inc(f["silu"], 1)

            def f_hi(wv, par, pair):
                act.wait_ge(f["h"], wv + 1)
                act.activation(hhi[:, par, 2 * pair:2 * pair + 2, :], hf[:, pair], ACT.Copy).then_inc(f["hhi"], 1)

            def f_events(blk, q, par):
                if q in (4, 8, 12, 16):
                    f_evac(blk, q // 4 - 1)
                if q in (5, 13):
                    f_silu(blk * 4 + q // 4 - 1)
                if q in (10, 18):
                    f_hi(blk * 2 + (q == 18), par, int(q == 18))

            c = NC1
            for q in range(3):
                hi_part(c + q, q, (c + q) // RING)
            for q in range(16):
                hi_part(c + q + 3, (q + 3) % RING, (c + q + 3) // RING)
                f_events(0, q, 0)
            for q in (16, 17, 18):
                f_events(0, q, 0)
            c += 16
            with act.Fori(0, NLOOP) as it:
                for t in range(48):
                    half, q = t // 24, t % 24
                    hi_part(it * 48 + (c + t + 3), (t + 3) % RING, it * 12 + (c + t + 3) // RING)
                    f_events(it * 2 + (1 + half), q, (1 + half) % 2)
            c += 48 * NLOOP
            for d in range(3, 8):
                hi_part(c + d, d % RING, (c + d) // RING)

            for r in range(5):
                m_ = min(4, 18 - 4 * r)
                act.wait_ge(fin["nt"], r + 1)
                act.activation(frow[0:88, 4 * r:4 * r + m_, :],
                               psA[0:88, r % 4, 0:m_ * P].rearrange("p (j c) -> p j c", j=m_), ACT.Copy).then_inc(fin["ne"], 1)
            for p in range(8):
                act.wait_ge(f["add"], 8 * (NB - 1) + p + 3)
                if p >= 2:
                    act.wait_ge(fin["ss"], p - 1)
                act.activation(sqb[:, p % 2], xres[:, 2 * p:2 * p + 2, :], ACT.Square).then_inc(fin["sq"], 1)
            act.wait_ge(fin["ms"], 1)
            act.activation(rs2[:, :], rs2[:, :], ACT.Sqrt).then_inc(fin["root"], 1)
            for q in range(4):
                for t in range(3):
                    n, c0 = unit(t)
                    act.wait_ge(fin["t"], 3 * q + t + 1)
                    act.activation(yo[0:n, t, 512 * q:512 * q + 512], psA[0:n, (3 * q + t) % 4, :], ACT.Copy).then_inc(fin["ev"], 1)
        @block.vector
        def _(dve):
            def finish(ins):
                ins.then_inc(done["V"], 1)

            def chain(ins):
                link(dve, "V", ins)

            def tt(out, a_, b_, op):
                return dve.tensor_tensor(out, a_, b_, op)

            def lo_part(c, slot):
                dve.wait_ge(hi_done, c + 1)
                dve.tensor_tensor(wlo[:, slot], raw[:, slot], whi[:, slot].bitcast(F32), ALU.subtract).then_inc(lo_done, 1)

            def conv(n):
                name, p = PAIRS[n]
                kind, h = tile_of(name, p, 0)
                g = int(name[1])
                gp = g * 6 + p
                ft = kind * 8 + g * 4 + h
                dve.wait_ge(evac_done, n + 1)
                dve.wait_ge(pads_done, gp + 2)
                if gp >= 1:
                    dve.wait_ge(silu_done, gp)
                for tap in range(4):
                    for j in range(2):
                        wcol = pT[:, tap * 24 + ft + j:tap * 24 + ft + j + 1]
                        u = ue[:, j, tap:tap + 344]
                        if tap == 0:
                            ins = dve.tensor_scalar(acc[:, j, 0:344], u, wcol, None, ALU.mult)
                        else:
                            ins = dve.scalar_tensor_tensor(out=acc[:, j, 0:344], in0=u, scalar=wcol, in1=acc[:, j, 0:344],
                                                           op0=ALU.mult, op1=ALU.add)
                    if tap < 3:
                        chain(ins)
                ins.then_inc(conv_done, 1)

            def add_pair(m_):
                n = NGA + m_
                name, p = PAIRS[n]
                dve.wait_ge(mm_done, FIRST[name] + 2 * p + 2)
                bank = 2 * (n % 2)
                x = xres[:, 2 * p:2 * p + 2, :]
                tt(x, psA[:, bank:bank + 2, 0:TOK], x, ALU.add).then_inc(add_done, 1)

            def step(x):
                name, k = x[1], x[2:]
                if name == "init":
                    chain(dve.memset(small[:, :], 0.0))
                    finish(dve.memset(sm("mh"), -0.5))
                elif name == "rows":
                    after(dve, "P", "rows")
                    finish(dve.tensor_copy(pT[:, 0:145], b0[:, 0:145]))
                elif name == "ms":
                    t = k[0]
                    n = unit(t)[0]
                    after(dve, "A", "sq", t)
                    finish(dve.tensor_scalar(sm("rsx", n, t, t + 1), sm("ssx", n, t, t + 1), 1.0 / DM, EPS, ALU.mult, ALU.add))
                elif name == "xs":
                    t = k[0]
                    n = unit(t)[0]
                    after(dve, "G", "rs", t)
                    finish(dve.tensor_scalar(xs[0:n, t % 2], xraw[0:n, t], sm("rsx", n, t, t + 1), None, ALU.mult))
                elif name == "xw":
                    t, q = k
                    n, _ = unit(t)
                    after(dve, "P", "xt", t, q)
                    finish(tt(tmpx[:, q % 2, :, 0:n], heads(psA[:, q, :], n), over_free(pT[:, 96 + 4 * q:100 + 4 * q], n), ALU.mult))
                elif name == "xl":
                    t, q = k
                    n, c0 = unit(t)
                    after(dve, "A", "xh", t, q)
                    finish(tt(xlo[:, 4 * q:4 * q + 4, c0:c0 + n], tmpx[:, q % 2, :, 0:n],
                              xhi[:, 4 * q:4 * q + 4, c0:c0 + n].bitcast(F32), ALU.subtract))
                elif name == "wab":
                    dve.wait_ge(ab_in, 16)
                    flat = wab[:, :, :].rearrange("p k c -> p (k c)")
                    dve.memset(wabh[:, 256:368].bitcast(F32), 0.0)
                    dve.memset(wabl[:, 256:368].bitcast(F32), 0.0)
                    chain(dve.tensor_copy(wabh[:, 0:256], flat))
                    finish(tt(wabl[:, 0:256], flat, wabh[:, 0:256].bitcast(F32), ALU.subtract))
                elif name == "sc1":
                    after(dve, "P", "abt")
                    after(dve, "A", "alog")
                    dve.tensor_copy(sm("ab", P, 0, 32), b1[:, 0:32])
                    chain(dve.tensor_copy(sm("ab", NS, 32, 48), b1[0:NS, 32:48]))
                    chain(tt(sm("sa").rearrange("p (u h) -> p u h", u=3),
                             sm("ab").rearrange("p (u c) -> p u c", u=3)[:, :, 0:8], over_heads(sm("dtb"), 3), ALU.add))
                    finish(dve.scalar_tensor_tensor(out=sm("sb"), in0=sm("sa"), scalar=-1.0, in1=sm("sa"),
                                                    op0=ALU.mult, op1=ALU.max))
                elif name == "sc3":
                    after(dve, "A", "sc2")
                    chain(dve.scalar_tensor_tensor(out=sm("sa"), in0=sm("sa"), scalar=0.0, in1=sm("sb"),
                                                   op0=ALU.max, op1=ALU.add))
                    chain(dve.scalar_tensor_tensor(out=sm("g").rearrange("p (u h) -> p u h", u=3),
                                                   in0=sm("sa").rearrange("p (u h) -> p u h", u=3), scalar=-1.0,
                                                   in1=over_heads(sm("alog"), 3), op0=ALU.mult, op1=ALU.mult))
                    chain(dve.tensor_scalar(sm("tmp"), sm("tmp"), 1.0, None, ALU.add))
                    dve.reciprocal(sm("beta"), sm("tmp"))
                    finish(tt(sm("gm", NS).rearrange("p (h b) -> p h b", h=8), over_free(sm("g", NS, 16, 24), DB),
                              over_heads(C("batch", NS), 8), ALU.mult))
                elif name == "sc4":
                    after(dve, "P", "cum")
                    dve.tensor_copy(sm("cg", P, 0, 16), b2[:, 0:16])
                    chain(dve.tensor_copy(sm("cg", NS, 16, 24), b2[0:NS, 16:24]))
                    tt(sm("nkd", P, 0, 16), b2[:, 24:40], sm("cg", P, 0, 16), ALU.subtract)
                    finish(tt(sm("nkd", NS, 16, 24), b2[0:NS, 40:48], sm("cg", NS, 16, 24), ALU.subtract))
                elif name == "ss":
                    g, u = k
                    n, _ = unit(u)
                    after(dve, "A", "cp", g, u)
                    dve.tensor_reduce(sm("ss", n, 0, 4), xt[0:n, :, :], AX.X, ALU.add)
                    chain(dve.tensor_reduce(sm("ss", n, 4, 8), xx[0:n, :, :], AX.X, ALU.add))
                    dve.tensor_scalar(sm("rn", n), sm("ss", n), EPS, None, ALU.add)
                    finish(tt(bv[0:n, :, :], heads(b2[0:n], P), over_free(per_head("beta", n, u, g), P), ALU.mult))
                elif name == "sc":
                    g, u = k
                    n, _ = unit(u)
                    after(dve, "G", "rn", g, u)
                    F = lambda i: sm("f", n, 4 * i, 4 * i + 4)
                    rk = sm("rn", n, 4, 8)
                    dve.tensor_scalar(F(0), sm("rn", n, 0, 4), SCALE, None, ALU.mult)
                    tt(F(3), rk, per_head("beta", n, u, g), ALU.mult)
                    chain(tt(F(5), rk, per_head("kd", n, u, g), ALU.mult))
                    tt(F(1), F(0), per_head("eg", n, u, g), ALU.mult)
                    chain(dve.scalar_tensor_tensor(out=F(4), in0=F(3), scalar=-1.0, in1=per_head("eg", n, u, g),
                                                   op0=ALU.mult, op1=ALU.mult))
                    tt(pp[0:n, :, :], tq[0:n, :, :], over_free(F(0), P), ALU.mult)
                    tt(tq[0:n, :, :], tq[0:n, :, :], over_free(F(1), P), ALU.mult)
                    tt(xx[0:n, :, :], tk[0:n, :, :], over_free(rk, P), ALU.mult)
                    tt(xt[0:n, :, :], tk[0:n, :, :], over_free(F(3), P), ALU.mult)
                    tt(at_[0:n, :, :], tk[0:n, :, :], over_free(F(4), P), ALU.mult)
                    finish(tt(tk[0:n, :, :], tk[0:n, :, :], over_free(F(5), P), ALU.mult))
                elif name == "tb1":
                    g, u = k
                    n, c0 = unit(u)
                    after(dve, "P", "tb1", g, u)
                    dve.tensor_copy(kb[:, :, c0:c0 + n], heads(b2, n))
                    finish(dve.tensor_copy(reg[g][:, 8:12, c0:c0 + n], heads(b3, n)))
                elif name == "gt":
                    g, u = k
                    n, _ = unit(u)
                    finish(tt(pp[0:n, :, 0:n], over_heads(C("upto" if u < 2 else "upto8", n, n), 4),
                              over_free(per_head("g", n, u, g), n), ALU.mult))
                elif name == "dm":
                    g, u = k
                    n, _ = unit(u)
                    after(dve, "P", "cg", g, u)
                    after(dve, "P", "tb1", g, u)
                    chain(tt(dec[0:n, :, 0:n], heads(b1[0:n], n), over_free(per_head("cg", n, u, g), n), ALU.subtract))
                    finish(dve.scalar_tensor_tensor(out=dec[0:n, :, 0:n], in0=dec[0:n, :, 0:n], scalar=0.0,
                                                    in1=over_heads(C("negP" if u < 2 else "neg8", n, n), 4),
                                                    op0=ALU.min, op1=ALU.add))
                elif name == "kk":
                    g, u = k
                    n, _ = unit(u)
                    after(dve, "P", "kk", g, u)
                    after(dve, "A", "de", g, u)
                    tt(qk[0:n, :, 0:n], heads(b3[0:n], n), dec[0:n, :, 0:n], ALU.mult)
                    chain(tt(at_[0:n, :, 0:n], heads(b2[0:n], n), dec[0:n, :, 0:n], ALU.mult))
                    chain(tt(pp[0:n, :, 0:n], at_[0:n, :, 0:n], over_heads(C("lev1", n, n), 4), ALU.mult))
                    tt(xt[0:n, :, 0:n], over_heads(C("ident", n, n), 4), pp[0:n, :, 0:n], ALU.subtract)
                    finish(tt(dec[0:n, :, 0:n], at_[0:n, :, 0:n], over_heads(C("lev2", n, n), 4), ALU.mult))
                elif name == "dl":
                    g, u, l = k
                    n, _ = unit(u)
                    last = l == (64 if u < 2 else 4)
                    after(dve, "P", "dl", g, u, l)
                    if not last:
                        tt(xx[0:n, :, 0:n], xx[0:n, :, 0:n], heads(b1[0:n], n), ALU.subtract)
                        tt(dec[0:n, :, 0:n], at_[0:n, :, 0:n], over_heads(C(f"lev{2 * l}", n, n), 4), ALU.mult)
                    finish(tt(xt[0:n, :, 0:n], xt[0:n, :, 0:n], heads(b2[0:n], n), ALU.subtract))
                elif name == "ks":
                    g, u = k
                    n, _ = unit(u)
                    after(dve, "P", "ks", g, u)
                    finish(tt(bv[0:n, :, :], heads((b0 if u == 1 else b1)[0:n], P), bv[0:n, :, :], ALU.add))
                elif name == "st":
                    g, u = k
                    after(dve, "P", "os", g, u)
                    if u == 0:
                        if g == 1:
                            dve.wait_ge(st_out, 16)
                        finish(dve.tensor_copy(S[:, :, :], heads(b3, P)))
                    else:
                        a0 = u * 8 + g * 4
                        chain(tt(S[:, :, :], S[:, :, :], over_free(sm("eglP", P, a0, a0 + 4), P), ALU.mult))
                        finish(tt(S[:, :, :], heads(b3, P), S[:, :, :], ALU.add))
                elif name == "o1":
                    n = unit(k[1])[0]
                    after(dve, "A", "o", *k)
                    chain(dve.tensor_reduce(sm("so", n), xx[0:n, :, :], AX.X, ALU.add))
                    finish(dve.tensor_scalar(sm("ro", n), sm("so", n), 1.0 / P, EPS, ALU.mult, ALU.add))
                elif name == "o2":
                    n = unit(k[1])[0]
                    after(dve, "G", "or", *k)
                    finish(tt(tq[0:n, :, :], tq[0:n, :, :], over_free(sm("ro", n), P), ALU.mult))
                elif name == "oz":
                    g, u = k
                    n, c0 = unit(u)
                    after(dve, "P", "ot", g, u)
                    dve.wait_ge(evac_done, 8 * (g + 1))
                    z = zz[:, 4 * g:4 * g + 4, c0:c0 + n]
                    finish(dve.scalar_tensor_tensor(out=z, in0=heads(b0, n), scalar=pT[:, 144:145], in1=z,
                                                    op0=ALU.mult, op1=ALU.mult))
                elif name == "um":
                    g, h = k
                    if h == 0:
                        after(dve, "A", "o", g, 2)
                    else:
                        after(dve, "P", "us", g, h - 1)
                    finish(tt(umask[0:NS, :, :], over_heads(ub[0:NS, h, :], DB), over_free(C("batch", NS), P), ALU.mult))
                elif name == "us":
                    g, h = k
                    after(dve, "P", "us", g, h)
                    dve.wait_ge(s_in, 16 * (8 * g + 4 + h + 1))
                    a0 = (4 * g + h) * DB
                    chain(tt(ssm[:, :, :], ssm[:, :, :], over_free(sm("eglS", P, a0, a0 + DB), P), ALU.mult))
                    finish(tt(ssm[:, :, :], psB[:, 2:4, :].rearrange("p k (b e) -> p (k b) e", b=4), ssm[:, :, :], ALU.add))
                elif name == "hk":
                    g = k[0]
                    after(dve, "P", "hk", g)
                    chain(dve.tensor_copy(bm[:, :, :], psB[:, 2:4, :].rearrange("p k (h x) -> p (k h) x", h=2)))
                    if g == 0:
                        dve.memset(bs[:, 0:2 * P], 0.0)
                        dve.memset(bs[:, 2 * P:], NEG)
                    chain(tt(bm[:, :, P:2 * P], bm[:, :, P:2 * P], over_heads(C("causal"), 4), ALU.add))
                    for h in range(4):
                        row = bs[32 * h:32 * h + DT]
                        dve.tensor_copy(row[:, 0:P], bm[0:DT, h, 0:1].broadcast_to([DT, P]))
                        dve.tensor_copy(row[:, P:2 * P], bm[0:DT, h, 0:P])
                        ins = dve.tensor_copy(row[:, 2 * P + 56:2 * P + 64], bm[0:DT, h, P:P + DT])
                    finish(ins)
                elif name == "S":
                    g, h = k
                    after(dve, "P", "S", g, h)
                    s_ = sc[:, h % 2]
                    b_ = psB[:, h % 2, :]
                    if h == 0:
                        after(dve, "V", "hk", g)
                    dve.scalar_tensor_tensor(out=s_[:, 0:256], in0=b_[:, 0:256], scalar=SCALE, in1=bm[:, h, :],
                                             op0=ALU.mult, op1=ALU.add)
                    chain(dve.scalar_tensor_tensor(out=s_[:, 256:384], in0=b_[:, 256:384], scalar=SCALE,
                                                   in1=bm[:, h, P:2 * P], op0=ALU.mult, op1=ALU.add))
                    dve.tensor_reduce(ast[:, 0:1], s_[:, 0:256], AX.X, ALU.max, negate=True)
                    finish(dve.tensor_reduce(ast[:, 1:2], s_[:, 256:384], AX.X, ALU.max, negate=True))
                elif name == "N":
                    g, h = k
                    s_ = sc[:, h % 2]
                    after(dve, "A", "E", g, h)
                    chain(dve.reciprocal(ast[:, 4:6], ast[:, 2:4]))
                    dve.tensor_scalar(s_[:, 0:256], s_[:, 0:256], ast[:, 4:5], None, ALU.mult)
                    finish(dve.tensor_scalar(s_[:, 256:384], s_[:, 256:384], ast[:, 5:6], None, ALU.mult))
                elif name == "kt":
                    after(dve, "P", "kt", *k)
                    finish(dve.tensor_copy(ktp[:, :, P:2 * P], heads(b1, P)))
                elif name == "SS":
                    g, b = k
                    after(dve, "P", "SS", g, b)
                    o_ = 2 * P + 56 - DT * b
                    dve.scalar_tensor_tensor(out=sc[:, 0, 0:256], in0=b2[:, 0:256], scalar=SCALE, in1=bs[:, 0:256],
                                             op0=ALU.mult, op1=ALU.add)
                    chain(dve.scalar_tensor_tensor(out=sc[:, 0, 256:TOK], in0=b2[:, 256:TOK], scalar=SCALE,
                                                   in1=bs[:, o_:o_ + NS], op0=ALU.mult, op1=ALU.add))
                    finish(dve.tensor_reduce(ast[:, 0:1], sc[:, 0, 0:TOK], AX.X, ALU.max, negate=True))
                elif name == "SN":
                    after(dve, "A", "SE", *k)
                    chain(dve.reciprocal(ast[:, 4:5], ast[:, 2:3]))
                    finish(dve.tensor_scalar(sc[:, 0, 0:TOK], sc[:, 0, 0:TOK], ast[:, 4:5], None, ALU.mult))
                elif name == "mg":
                    after(dve, "A", "mg")
                    finish(tt(xlo[:, 8:16, :], zz[:, :, :], xhi[:, 8:16, :].bitcast(F32), ALU.subtract))
                elif name == "ma":
                    after(dve, "A", "ma")
                    tt(xlo[:, 0:4, :], reg[0][:, 0:4, :], xhi[:, 0:4, :].bitcast(F32), ALU.subtract)
                    finish(tt(xlo[:, 4:8, :], reg[1][:, 0:4, :], xhi[:, 4:8, :].bitcast(F32), ALU.subtract))
                else:
                    raise KeyError(x)

            for x in SLOTS[-1]:
                if x[0] == "V":
                    step(x)
            for c in range(3):
                lo_part(c, c % RING)
            for c in range(NC1):
                if c + 3 < NC1:
                    lo_part(c + 3, (c + 3) % RING)
                for n, (name, p) in enumerate(PAIRS):
                    per = 4 if n < NGA else 2
                    if c - 1 == FIRST[name] + per * p + per - 1:
                        if n >= NGA:
                            add_pair(n - NGA)
                        elif name[0] == "g" and p < 6:
                            conv(n)
                for x in SLOTS[c]:
                    if x[0] == "V":
                        step(x)
            add_pair(15)
            dve.wait_ge(ssq2, 8)
            dve.tensor_scalar(rs2[:, :], b3[:, 0:TOK], 1.0 / DM, EPS, ALU.mult, ALU.add).then_inc(rms_v, 1)
            dve.wait_ge(xn_a, 1)
            chain(dve.reciprocal(rs2[:, :], rs2[:, :]))
            for q in range(4):
                if q >= 2:
                    dve.wait_ge(xn_h, q - 1)
                for j in range(4):
                    kk_ = 4 * q + j
                    ins = dve.scalar_tensor_tensor(out=xn[:, q % 2, j, :], in0=xres[:, kk_, :],
                                                   scalar=pT[:, 112 + kk_:113 + kk_], in1=rs2[:, :], op0=ALU.mult, op1=ALU.mult)
                ins.then_inc(xn_v, 1)
                dve.wait_ge(xn_h, q + 1)
                tt(xlo[:, 4 * q:4 * q + 4, :], xn[:, q % 2], xhi[:, 4 * q:4 * q + 4, :].bitcast(F32),
                   ALU.subtract).then_inc(xn_l, 1)

            def stage(blk, par):
                if isinstance(blk, int):
                    after(dve, "A", "fp", 4)
                else:
                    dve.wait_ge(f["pad"], blk * 4 + 1)
                for kind in range(2):
                    ins = dve.tensor_scalar(fst[:, par, kind, :, :], pF[:, bass.DynSlice(blk * 4 + kind * FT, 4), :],
                                            1.0, None, ALU.mult)
                ins.then_inc(f["stage"], 1)
                dve.wait_ge(f["stage"], blk + 1)

            def f_conv(blk, r, par):
                n = blk * 4 + r
                kind = r % 2
                dve.wait_ge(f["evac"], n + 1)
                dve.wait_ge(f["pad"], n + 2)
                ft = blk * 4 + (kind * FT + r // 2 * 2)
                dve.tensor_scalar(fnewT[:, bass.DynSlice(ft, 2), 0:2], fue[:, kind, :, SEQ:SEQ + 2], 1.0, None, ALU.mult)
                dve.tensor_scalar(fnewT[:, bass.DynSlice(ft, 2), 2:18].rearrange("p f (b r) -> p f b r", b=DB),
                                  fue[:, kind, :, 2 + SEQ:338].rearrange("p j (b s) -> p j b s", b=DB)[:, :, :, 8:10],
                                  1.0, None, ALU.mult)
                for tap in (2, 1, 0):
                    for j in range(2):
                        w_ = lambda i: fst[:, par, kind, r // 2 * 2 + j, i:i + 1]
                        u = fue[:, kind, j, tap:tap + 336]
                        if tap == 2:
                            ins = dve.tensor_scalar(facc[:, kind, j, 0:336], u, w_(2), w_(3), ALU.mult, ALU.add)
                        else:
                            ins = dve.scalar_tensor_tensor(out=facc[:, kind, j, 0:336], in0=u, scalar=w_(tap),
                                                           in1=facc[:, kind, j, 0:336], op0=ALU.mult, op1=ALU.add)
                    if tap:
                        ins.then_inc(f["tap"], 1)
                        dve.wait_ge(f["tap"], n * 2 + (3 - tap))
                ins.then_inc(f["conv"], 1)

            def f_hidden(blk, r):
                wv = blk * 2 + r // 2
                dve.wait_ge(f["silu"], wv + 1)
                dve.wait_ge(f["conv"], blk * 4 + r + 1)
                if not isinstance(wv, int) or wv >= 2:
                    dve.wait_ge(f["hhi"], wv - 1)
                tt(hf[:, r // 2, :, 0:SEQ], facc[:, 0, :, 0:SEQ], facc[:, 1, :, 0:SEQ], ALU.mult)
                for j in range(2):
                    ins = tt(hf[:, r // 2, j, SEQ:TOK].rearrange("p (b t) -> p b t", b=DB), f_sample(0, j), f_sample(1, j), ALU.mult)
                ins.then_inc(f["h"], 1)

            def f_lo(blk, r, par):
                dve.wait_ge(f["hhi"], blk * 2 + r // 2 + 1)
                lo_, hi_ = r - 1, r + 1
                tt(hlo[:, par, lo_:hi_, :], hf[:, r // 2], hhi[:, par, lo_:hi_, :].bitcast(F32), ALU.subtract).then_inc(f["hlo"], 1)

            def f_add(blk, d):
                dve.wait_ge(mm_done, down_start(blk) + d + 1)
                x = xres[:, 2 * d:2 * d + 2, :]
                bank = 2 * (d % 2)
                tt(x, psB[:, bank:bank + 2, 0:TOK], x, ALU.add).then_inc(f["add"], 1)

            def f_events(blk, q, par):
                if q == 0:
                    stage(blk, par)
                if q in (4, 8, 12, 16):
                    f_conv(blk, q // 4 - 1, par)
                if q in (9, 17):
                    f_hidden(blk, q // 4 - 1)
                if q in (10, 18):
                    f_lo(blk, q // 4 - 1, par)

            dve.memset(small[0:1, 0:1], 0.0).then_inc(f["add"], 2)
            c = NC1
            for q in range(3):
                lo_part(c + q, q)
            for q in range(16):
                lo_part(c + q + 3, (q + 3) % RING)
                f_events(0, q, 0)
            for q in (16, 17, 18):
                f_events(0, q, 0)
            c += 16
            with dve.Fori(0, NLOOP) as it:
                for t in range(48):
                    half, q = t // 24, t % 24
                    blk = it * 2 + (1 + half)
                    lo_part(it * 48 + (c + t + 3), (t + 3) % RING)
                    f_events(blk, q, (1 + half) % 2)
                    if q >= 17:
                        f_add(blk - 1, q - 17)
                    if t in (23, 47):
                        f_add(blk - 1, 7)
            c += 48 * NLOOP
            for d in range(8):
                if d + 3 < 8:
                    lo_part(c + d + 3, (d + 3) % RING)
                if d:
                    f_add(NB - 1, d - 1)
            f_add(NB - 1, 7)
            dve.wait_ge(fin["ss"], 8)
            dve.tensor_scalar(rs2[:, :], b3[:, 0:TOK], 1.0 / DM, EPS, ALU.mult, ALU.add).then_inc(fin["ms"], 1)
            dve.wait_ge(fin["root"], 1)
            chain(dve.reciprocal(rs2[:, :], rs2[:, :]))
            for kk_ in range(KT):
                dve.scalar_tensor_tensor(out=xres[:, kk_, :], in0=xres[:, kk_, :], scalar=pT[:, 128 + kk_:129 + kk_],
                                         in1=rs2[:, :], op0=ALU.mult, op1=ALU.mult).then_inc(fin["y"], 1)

        @block.tensor
        def _(pe):
            def finish(ins):
                ins.then_inc(done["P"], 1)

            def products(c, slot, out_bank, k0, first, last, tiles, rhs_hi, rhs_lo):
                pe.wait_ge(lo_done, c + 1)
                for j in range(2):
                    o = out_bank[:, j, 0:TOK]
                    for kk_ in range(CQ):
                        hi = whi[:, slot, kk_, j * P:(j + 1) * P]
                        lo = wlo[:, slot, kk_, j * P:(j + 1) * P]
                        pe.matmul(o, hi, rhs_hi[:, k0 + kk_, :], start=first and kk_ == 0, stop=False)
                        pe.matmul(o, hi, rhs_lo[:, k0 + kk_, :], start=False, stop=False)
                        ins = pe.matmul(o, lo, rhs_hi[:, k0 + kk_, :], start=False, stop=last and kk_ == CQ - 1)
                ins.then_inc(mm_done, 1)

            def project(c):
                name, p, q, per = CHUNKS[c]
                n = pair_index(name, p)
                if q == 0:
                    if n >= 2:
                        if n - 2 < NGA:
                            pe.wait_ge(evac_done, n - 1)
                        else:
                            pe.wait_ge(add_done, n - 1 - NGA)
                    else:
                        after(pe, "V", "xl", 2, 3)
                    if c == FIRST["wg"]:
                        after(pe, "V", "mg")
                    if c == FIRST["wa"]:
                        after(pe, "V", "ma")
                k0 = q * CQ + (8 if name == "wg" else 0)
                bank = 2 * (n % 2)
                products(c, c % RING, psA[:, bank:bank + 2, :], k0, q == 0, q == per - 1, None, xhi, xlo)

            def turn(out, in_, n):
                return pe.transpose(out, in_, C("ident", n, n))

            def sum_squares(p):
                pe.wait_ge(sq2, p + 1)
                for j in range(2):
                    ins = pe.matmul(b3[:, 0:TOK], C("ones"), sqb[:, p % 2, j, :], start=(p == 0 and j == 0), stop=(p == 7 and j == 1))
                ins.then_inc(ssq2, 1)

            def step(x):
                name, k = x[1], x[2:]
                if name == "rows":
                    pe.wait_ge(consts_in, 16)
                    pe.wait_ge(rows_in, 16 * NROWS)
                    turn(b0[:, 0:P], prow[:, 0, :], P)
                    turn(b0[:, P:P + 17], prow[0:17, 1, :], 17)
                    for r in range(4):
                        turn(b1[:, r * P:(r + 1) * P], prow[:, 2 + r, :], P)
                    finish(turn(b2[:, 0:64], prow[0:64, 6, :], 64))
                elif name == "rb":
                    finish(pe.matmul(b3[0:NH, 0:3 * P], sm("rb", NBK), C("bucket", NBK), start=True, stop=True))
                elif name == "xt":
                    t, q = k
                    n, _ = unit(t)
                    after(pe, "V", "xs", t)
                    if t >= 1:
                        after(pe, "V", "xw", t - 1, q)
                    for j in range(4):
                        ins = turn(psA[:, q, j * n:(j + 1) * n], xs[0:n, t % 2, (4 * q + j) * P:(4 * q + j + 1) * P], n)
                    finish(ins)
                elif name == "rt":
                    t, q = k
                    n, _ = unit(t)
                    if (t, q) == (0, 0):
                        after(pe, "A", "rb")
                    else:
                        after(pe, "A", "rt", *((t, q - 1) if q else (t - 1, 3)))
                    for j in range(4):
                        ins = turn(b3[:, j * n:(j + 1) * n], xraw[0:n, t, (4 * q + j) * P:(4 * q + j + 1) * P], n)
                    finish(ins)
                elif name == "ab":
                    after(pe, "V", "wab")
                    after(pe, "V", "rows")
                    for kk_ in range(KT):
                        hi, lo = (w_[:, kk_ * 16:kk_ * 16 + P] for w_ in (wabh, wabl))
                        pe.matmul(b0[:, 0:TOK], hi, xhi[:, kk_, :], start=kk_ == 0, stop=False)
                        pe.matmul(b0[:, 0:TOK], hi, xlo[:, kk_, :], start=False, stop=False)
                        ins = pe.matmul(b0[:, 0:TOK], lo, xhi[:, kk_, :], start=False, stop=kk_ == KT - 1)
                    finish(ins)
                elif name == "abt":
                    after(pe, "A", "ab")
                    after(pe, "A", "prev")
                    for u in range(3):
                        n, c0 = unit(u)
                        ins = pe.transpose(b1[0:n, 16 * u:16 * u + 16], abT[0:16, c0:c0 + n], C("ident", 16, 16))
                    finish(ins)
                elif name == "cum":
                    after(pe, "V", "sc3")
                    for u in range(2):
                        gg = sm("g", P, 8 * u, 8 * u + 8)
                        pe.matmul(b2[:, 8 * u:8 * u + 8], C("upto"), gg, start=True, stop=True)
                        pe.matmul(b2[:, 24 + 8 * u:32 + 8 * u], C("ones"), gg, start=True, stop=True)
                    gg = sm("g", NS, 16, 24)
                    pe.matmul(b2[0:NS, 16:24], C("upto8", NS, NS), gg, start=True, stop=True)
                    pe.matmul(b2[0:NS, 40:48], C("same8", NS, NS), gg, start=True, stop=True)
                    finish(pe.matmul(b2[:, 64:128], C("ones", NS), sm("gm", NS), start=True, stop=True))
                elif name == "tr":
                    g, u = k
                    n, c0 = unit(u)
                    pe.wait_ge(silu_done, 6 * g + 6)
                    after(pe, "A", "sc5")
                    after(pe, *before_unit(g, u))
                    if (g, u) == (1, 0):
                        after(pe, "A", "gs", 5)
                    for kind, bank in enumerate((b0, b1, b2)):
                        for h in range(4):
                            ins = turn(bank[0:n, h * P:(h + 1) * P], reg[g][:, 4 * kind + h, c0:c0 + n], P)
                    finish(ins)
                elif name == "tb1":
                    g, u = k
                    n, c0 = unit(u)
                    after(pe, "V", "sc", g, u)
                    for src, bank in ((pp, b0), (xx, b1), (xt, b2), (at_, b3)):
                        for h in range(4):
                            ins = turn(bank[:, h * n:(h + 1) * n], src[0:n, h, :], n)
                    finish(ins)
                elif name == "tb2":
                    g, u = k
                    n, c0 = unit(u)
                    after(pe, "A", "tb1", g, u)
                    for h in range(4):
                        ins = turn(b0[:, h * n:(h + 1) * n], tq[0:n, h, :], n)
                    finish(ins)
                elif name == "cg":
                    n = unit(k[1])[0]
                    after(pe, "V", "gt", *k)
                    finish(pe.matmul(heads(b1[0:n], n), C("ones", n, n), pp[0:n, :, 0:n], start=True, stop=True))
                elif name == "kk":
                    g, u = k
                    n, c0 = unit(u)
                    after(pe, "V", "tb1", g, u)
                    for h in range(4):
                        kT_ = reg[g][:, 4 + h, c0:c0 + n]
                        pe.matmul(b2[0:n, h * n:(h + 1) * n], kT_, kb[:, h, c0:c0 + n], start=True, stop=True)
                        ins = pe.matmul(b3[0:n, h * n:(h + 1) * n], kT_, qn[:, h, c0:c0 + n], start=True, stop=True)
                    finish(ins)
                elif name == "x1":
                    n = unit(k[1])[0]
                    after(pe, "V", "kk", *k)
                    after(pe, "A", "tb2", *k)
                    for h in range(4):
                        ins = turn(b0[0:n, h * n:(h + 1) * n], xt[0:n, h, 0:n], n)
                    finish(ins)
                elif name == "pl":
                    g, u, l = k
                    n = unit(u)[0]
                    after(pe, *(("A", "x1", g, u) if l == 2 else ("V", "dl", g, u, l // 2)))
                    for h in range(4):
                        ins = pe.matmul(b0[0:n, h * n:(h + 1) * n], dec[0:n, h, 0:n], xx[0:n, h, 0:n], start=True, stop=True)
                    finish(ins)
                elif name == "dl":
                    g, u, l = k
                    n = unit(u)[0]
                    after(pe, "A", "pl", g, u, l)
                    last = l == (64 if u < 2 else 4)
                    for h in range(4):
                        if not last:
                            pe.matmul(b1[0:n, h * n:(h + 1) * n], xt[0:n, h, 0:n], pp[0:n, h, 0:n], start=True, stop=True)
                        ins = pe.matmul(b2[0:n, h * n:(h + 1) * n], pp[0:n, h, 0:n], xt[0:n, h, 0:n], start=True, stop=True)
                    finish(ins)
                elif name == "ks":
                    g, u = k
                    n, c0 = unit(u)
                    if u == 1:
                        after(pe, "V", "st", g, 0)
                        after(pe, "V", "dl", g, u, 64)
                    else:
                        after(pe, "A", "sh", g, 0)
                        after(pe, "V", "dl", g, u, 4)
                    for h in range(4):
                        if u == 1:
                            ins = pe.matmul(b0[:, h * P:(h + 1) * P], reg[g][:, 8 + h, c0:c0 + n], S[:, h, :], start=True, stop=True)
                        else:
                            ins = pe.matmul(b1[0:n, h * P:(h + 1) * P], pp[:, h, NS:2 * NS], C("ident"), start=True, stop=True)
                    finish(ins)
                elif name == "u":
                    g, u = k
                    n = unit(u)[0]
                    after(pe, *(("V", "ks", g, u) if u else ("V", "dl", g, u, 64)))
                    for h in range(4):
                        ins = pe.matmul(b1[0:n, h * P:(h + 1) * P], xt[0:n, h, 0:n], bv[0:n, h, :], start=True, stop=True)
                    finish(ins)
                elif name == "os":
                    g, u = k
                    n, c0 = unit(u)
                    after(pe, "A", "u", g, u)
                    for h in range(4):
                        o = b2[0:n, h * P:(h + 1) * P]
                        if u == 1:
                            pe.matmul(o, reg[g][:, h, c0:c0 + n], S[:, h, :], start=True, stop=False)
                        if u == 2:
                            pe.matmul(o, pp[:, h, 0:NS], C("ident"), start=True, stop=False)
                        ins = pe.matmul(o, qk[0:n, h, 0:n], ub[0:n, h, :], start=u == 0, stop=True)
                        if u < 2:
                            ins = pe.matmul(b3[:, h * P:(h + 1) * P], tk[0:n, h, :], ub[0:n, h, :], start=True, stop=True)
                    finish(ins)
                elif name == "ot":
                    n = unit(k[1])[0]
                    after(pe, "V", "o2", *k)
                    for h in range(4):
                        ins = turn(b0[:, h * n:(h + 1) * n], tq[0:n, h, :], n)
                    finish(ins)
                elif name == "sh":
                    g, h = k
                    pe.wait_ge(s_in, 16 * (8 * g + h + 1))
                    if h == 0:
                        after(pe, "V", "dl", g, 2, 4)
                    for b in range(DB):
                        c0 = SEQ + b * DT
                        ins = pe.matmul(b0[:, h * P:(h + 1) * P].rearrange("p (q b t) -> p q b t", q=2, b=DB)[:, :, b, :],
                                        ssm[:, b, :], reg[g][:, h:h + 9:8, c0:c0 + DT], start=True, stop=True)
                    finish(ins)
                elif name == "us":
                    g, h = k
                    after(pe, "V", "um", g, h)
                    if h == 0:
                        after(pe, "A", "o", g, 2)
                    else:
                        after(pe, "V", "us", g, h - 1)
                    for i in range(2):
                        ins = pe.matmul(psB[:, 2 + i, :], tk[0:NS, h, :],
                                        umask[0:NS, 4 * i:4 * i + 4, :].rearrange("p b e -> p (b e)"), start=True, stop=True)
                    finish(ins)
                elif name == "gs":
                    r = k[0]
                    n = min(P, 648 - r * P)
                    pe.wait_ge(new_done, 12)
                    after(pe, *(("A", "gs", r - 2) if r >= 2 else ("V", "us", 0, 3)))
                    finish(turn(psB[0:n, r % 2, 0:P], gnew[:, :, :].rearrange("p r f -> p (r f)")[:, r * P:r * P + n], P))
                elif name == "hk":
                    g = k[0]
                    pe.wait_ge(hk_in, 16 * (g + 1))
                    after(pe, *(("V", "us", 1, 3) if g == 0 else ("A", "OT", 0, DB - 1)))
                    for i in range(2):
                        ins = pe.matmul(psB[:, 2 + i, :], C("flip"), hk[:, 2 * i:2 * i + 2, :].rearrange("p h x -> p (h x)"),
                                        start=True, stop=True)
                    finish(ins)
                elif name == "kv":
                    g, t = k
                    n, c0 = unit(t)
                    pe.wait_ge(evac_done, 16 + 6 * (g + 1))
                    if t:
                        after(pe, "A", "kv", g, t - 1)
                    for kind, bank in ((1, b0), (2, b1)):
                        for h in range(4):
                            ins = turn(bank[0:n, h * P:(h + 1) * P], reg[g][:, 4 * kind + h, c0:c0 + n], P)
                    finish(ins)
                elif name == "S":
                    g, h = k
                    if h == 0:
                        after(pe, "A", "kv", g, 2)
                    if h >= 2:
                        after(pe, "V", "S", g, h - 2)
                    qT, kT_ = reg[g][:, h, :], reg[g][:, 4 + h, :]
                    pe.matmul(psB[:, h % 2, 0:SEQ], qT[:, P:SEQ], kT_[:, 0:SEQ], start=True, stop=True)
                    finish(pe.matmul(psB[:, h % 2, SEQ:SEQ + P], qT[:, 0:P], kT_[:, 0:P], start=True, stop=True))
                elif name == "T":
                    g, h = k
                    after(pe, "V", "N", g, h)
                    s_ = sc[:, h % 2]
                    turn(b2[:, 0:P], s_[:, 256:384], P)
                    turn(b2[:, P:2 * P], s_[:, 0:P], P)
                    finish(turn(b2[:, 2 * P:3 * P], s_[:, P:2 * P], P))
                elif name == "O":
                    g, h = k
                    after(pe, "A", "T", g, h)
                    if h:
                        after(pe, "A", "O", g, h - 1)
                    pe.matmul(b3[:, 0:SEQ], vt[:, 0, h, :], pt[:, h % 2, 0:SEQ], start=True, stop=False)
                    finish(pe.matmul(b3[:, P:SEQ], vt[:, 1, h, :], pt[:, h % 2, SEQ:SEQ + P], start=False, stop=True))
                elif name == "kt":
                    g, b = k
                    pe.wait_ge(pg_in, 64 * (DB * g + b + 1))
                    after(pe, *(("A", "O", g, 3) if b == 0 else ("A", "OT", g, b - 1)))
                    for i, bank in ((0, b0), (1, b1)):
                        for h in range(4):
                            ins = turn(bank[:, h * P:(h + 1) * P], kp[:, i, h, :], P)
                    finish(ins)
                elif name == "SS":
                    g, b = k
                    after(pe, "A", "kt", g, b)
                    after(pe, "V", "kt", g, b)
                    c0 = SEQ + b * DT
                    for h in range(4):
                        qT = reg[g][:, h, c0:c0 + DT]
                        pe.matmul(b2[32 * h:32 * h + DT, 0:256], qT, ktp[:, h, :], start=True, stop=True)
                        ins = pe.matmul(b2[32 * h:32 * h + DT, 256:TOK], qT, reg[g][:, 4 + h, SEQ:TOK], start=True, stop=True)
                    finish(ins)
                elif name == "PT":
                    after(pe, "V", "SN", *k)
                    turn(b3[:, 0:P], sc[:, 0, 0:P], P)
                    turn(b3[:, P:2 * P], sc[:, 0, P:2 * P], P)
                    finish(turn(b3[0:NS, 2 * P:3 * P], sc[:, 0, 2 * P:TOK], P))
                elif name == "PV":
                    g, b = k
                    after(pe, "A", "PT", g, b)
                    for h in range(4):
                        o = b0[32 * h:32 * h + DT, 0:P]
                        for i in range(2):
                            pe.matmul(o, pt[:, 0, i * P + 32 * h:i * P + 32 * h + DT], vp[:, i, h, :], start=i == 0, stop=False)
                        ins = pe.matmul(o, pt[0:NS, 0, 2 * P + 32 * h:2 * P + 32 * h + DT], vt[0:NS, 2, h, :], start=False, stop=True)
                    finish(ins)
                elif name == "OT":
                    after(pe, "A", "PV", *k)
                    finish(turn(b1[:, 0:P], ob[:, :], P))
                elif name == "fp":
                    r = k[0]
                    pe.wait_ge(fl_in, 16 * (2 + 2 * DB))
                    if r >= 2:
                        after(pe, "A", "fp", r - 2)
                    for j in range(4):
                        ins = turn(psB[:, r % 2, 88 * j:88 * j + 88], frow[0:88, 4 * r + j, :], 88)
                    finish(ins)
                else:
                    raise KeyError(x)

            for x in SLOTS[-1]:
                if x[0] == "P":
                    step(x)
            for c in range(NC1):
                project(c)
                if wa_pair(c - 3) is not None:
                    sum_squares(wa_pair(c - 3))
                for x in SLOTS[c]:
                    if x[0] == "P":
                        step(x)
            for p in (6, 7):
                sum_squares(p)

            def up(c, blk, q):
                pair, kq = q // 4, q % 4
                n = blk * 4 + pair
                if kq == 0 and (not isinstance(n, int) or n >= 2):
                    pe.wait_ge(f["evac"], n - 1)
                if isinstance(c, int) and c < NC1 + 4:
                    pe.wait_ge(xn_l, kq + 1)
                bank = 2 * (pair % 2)
                products(c, q % RING, psA[:, bank:bank + 2, :], kq * CQ, kq == 0, kq == 3, None, xhi, xlo)

            def down(c, blk, d, par):
                n = blk * 8 + d
                pe.wait_ge(f["add"], n + 1)
                if d == 0:
                    pe.wait_ge(f["hlo"], blk * 2 + 2)
                bank = 2 * (d % 2)
                products(c, d % RING, psB[:, bank:bank + 2, :], 0, True, True, None, hhi[:, par], hlo[:, par])

            c = NC1
            for q in range(16):
                up(c + q, 0, q)
            c += 16
            with pe.Fori(0, NLOOP) as it:
                for t in range(48):
                    half, q = t // 24, t % 24
                    blk = it * 2 + (1 + half)
                    cc = it * 48 + (c + t)
                    if q < 16:
                        up(cc, blk, q)
                    else:
                        down(cc, it * 2 + half, q - 16, half)
            c += 48 * NLOOP
            for d in range(8):
                down(c + d, NB - 1, d, (NB - 1) % 2)
                if d < 5:
                    m_ = min(4, 18 - 4 * d)
                    pe.wait_ge(f["conv"], 4 * NB)
                    if d == 4:
                        pe.wait_ge(fin["ne"], 1)
                    for j in range(m_):
                        ins = turn(psA[0:88, d % 4, j * P:(j + 1) * P], fnewT[:, :, 4 * d + j], P)
                    ins.then_inc(fin["nt"], 1)
            for p in range(8):
                pe.wait_ge(fin["sq"], p + 1)
                pe.wait_ge(f["add"], NB * 8 + 2)
                for j in range(2):
                    ins = pe.matmul(b3[:, 0:TOK], C("ones"), sqb[:, p % 2, j, :], start=(p == 0 and j == 0), stop=(p == 7 and j == 1))
                ins.then_inc(fin["ss"], 1)
            for q in range(4):
                for t in range(3):
                    n, c0 = unit(t)
                    i = 3 * q + t
                    pe.wait_ge(fin["y"], 4 * q + 4)
                    if i >= 4:
                        pe.wait_ge(fin["ev"], i - 3)
                    else:
                        pe.wait_ge(fin["ne"], 5)
                    for j in range(4):
                        ins = turn(psA[0:n, i % 4, j * P:(j + 1) * P], xres[:, 4 * q + j, c0:c0 + n], P)
                    ins.then_inc(fin["t"], 1)

        @block.gpsimd
        def _(pool):
            def finish(ins):
                ins.then_inc(done["G"], 1)

            def pads(n):
                name, p = PAIRS[n]
                kind, h = tile_of(name, p, 0)
                g = int(name[1])
                gp = g * 6 + p
                ft = kind * 8 + g * 4 + h
                if gp == 0:
                    after(pool, "A", "prev")
                else:
                    pool.wait_ge(conv_done, gp)
                for j in range(2):
                    ins = pool.tensor_copy(ue[:, j, 3 + SEQ:347].rearrange("p (b s) -> p b s", b=DB)[:, :, 0:3],
                                           prevT[:, :, ft + j].rearrange("p (b r) -> p b r", b=DB))
                ins.then_inc(pads_done, 1)

            def new_rows(n):
                name, p = PAIRS[n]
                kind, h = tile_of(name, p, 0)
                g = int(name[1])
                ft = kind * 8 + g * 4 + h
                pool.wait_ge(evac_done, n + 1)
                for j in range(2):
                    pool.tensor_copy(gnew[:, 0:3, ft + j], ue[:, j, SEQ:SEQ + 3])
                    ins = pool.tensor_copy(gnew[:, 3:27, ft + j].rearrange("p (b r) -> p b r", b=DB),
                                           ue[:, j, 3 + SEQ:347].rearrange("p (b s) -> p b s", b=DB)[:, :, 8:11])
                ins.then_inc(new_done, 1)

            def power(out, in_, n, width):
                return pool.tensor_tensor(out, in_, sm("mh", n, 0, width), ALU.pow)

            pages = []

            def step(x):
                name, k = x[1], x[2:]
                if name == "rbout":
                    after(pool, "A", "rb")
                    pool.dma_start(rb_dram, rsb0[0:NH, :]).then_inc(rb_out, 16)
                    finish(pool.memset(ue[:, :, 0:3], 0.0))
                elif name == "rs":
                    t = k[0]
                    n = unit(t)[0]
                    after(pool, "V", "ms", t)
                    finish(power(sm("rsx", n, t, t + 1), sm("rsx", n, t, t + 1), n, 1))
                elif name == "rn":
                    n = unit(k[1])[0]
                    after(pool, "V", "ss", *k)
                    finish(power(sm("rn", n), sm("rn", n), n, 8))
                elif name == "or":
                    n = unit(k[1])[0]
                    after(pool, "V", "o1", *k)
                    finish(power(sm("ro", n), sm("ro", n), n, 4))
                elif name in ("si", "s2"):
                    g, h = k
                    if name == "si":
                        if h:
                            after(pool, "P", "sh", g, h - 1)
                        elif g:
                            pool.wait_ge(s_out, 16 * 4 * g)
                        else:
                            after(pool, "A", "rt", 2, 3)
                    else:
                        after(pool, "P", "sh", g, 3)
                        if h:
                            pool.wait_ge(s_out, 16 * (4 * g + h))
                    pool.dma_start(ssm[:, :, :], I["state_gdn"][0, :, 4 * g + h].rearrange("b d e -> d b e")).then_inc(s_in, 16)
                elif name == "so":
                    g, h = k
                    if h == 4:
                        after(pool, "V", "st", g, 1)
                        pool.dma_start(O["sp"][0, 0, 4 * g:4 * g + 4].rearrange("h d e -> d h e"), S[:, :, :]).then_inc(st_out, 16)
                    else:
                        after(pool, "V", "us", g, h)
                        pool.dma_start(O["ss"][0, :, 4 * g + h].rearrange("b d e -> d b e"), ssm[:, :, :]).then_inc(s_out, 16)
                elif name == "gs":
                    r = k[0]
                    n = min(P, 648 - r * P)
                    after(pool, "A", "gs", r)
                    rows_p, rows_s = 72, 576
                    gp_ = O["gcp"][0, 0].rearrange("r (f c) -> (r f) c", c=P)
                    gs_ = O["gcs"][0].rearrange("b r (f c) -> (b r f) c", c=P)
                    if r == 0:
                        pool.dma_start(gp_, gst[0:rows_p, 0, :]).then_inc(gs_out, 16)
                        pool.dma_start(gs_[0:P - rows_p, :], gst[rows_p:P, 0, :]).then_inc(gs_out, 16)
                    else:
                        pool.dma_start(gs_[r * P - rows_p:r * P - rows_p + n, :], gst[0:n, r, :]).then_inc(gs_out, 16)
                elif name == "hk":
                    g = k[0]
                    if g == 0:
                        pool.wait_ge(rb_out, 16)
                        after(pool, "V", "us", 1, 3)
                        pool.wait_ge(s_out, 16 * 8)
                        pool.wait_ge(st_out, 32)
                        pool.wait_ge(gs_out, 16 * 7)
                    else:
                        after(pool, "P", "hk", 0)
                    src = bass.AP(rb_dram.tensor, 4 * g * 3 * P, [[1, P], [3 * P, 4], [1, 2 * P]])
                    pool.dma_start(hk[:, :, :], src).then_inc(hk_in, 16)
                elif name == "kv":
                    g, t = k
                    n, c0 = unit(t)
                    after(pool, "A", "kv", g, t)
                    hs = slice(4 * g, 4 * g + 4)
                    for key, tile_ in (("k", kst[0:n]), ("v", vt[0:n, t])):
                        if t < 2:
                            out = O[key + "p"][0, 0, c0:c0 + n, hs]
                        else:
                            out = O[key + "s"][0, :, :, hs].rearrange("b t h d -> (b t) h d")
                        pool.dma_start(out, tile_).then_inc(kv_out, 16)
                elif name == "pg":
                    g, b = k
                    if (g, b) == (0, 0):
                        pool.wait_ge(pt_in, 16)
                        after(pool, "V", "us", 1, 3)
                    else:
                        after(pool, "P", "PV", *((g, b - 1) if b else (0, DB - 1)))
                    for i in range(2):
                        page = pool.value_load(ptab[0:1, 2 * b + i:2 * b + i + 1], min_val=0, max_val=n_pool - 1)
                        for cache, tile_ in ((I["cache_k"], kp), (I["cache_v"], vp)):
                            src = cache[0].rearrange("n s h d -> n s (h d)")[bass.DynSlice(page, 1), :, 512 * g:512 * g + 512]
                            pool.dma_start(tile_[:, i].rearrange("p h d -> p (h d)"), src.rearrange("a s c -> (a s) c"))\
                                .then_inc(pg_in, 16)
                elif name == "fload":
                    after(pool, "V", "ma")
                    pool.dma_start(frow[0:88, 0:3, :], I["ffn_conv_w"][0].rearrange("m (f c) -> f m c", c=P)).then_inc(fl_in, 16)
                    pool.dma_start(frow[0:88, 3, :], I["ffn_conv_b"][0].rearrange("(f c) -> f c", c=P)).then_inc(fl_in, 16)
                    for b in range(DB):
                        for r in range(2):
                            pool.dma_start(frow[0:88, 4 + 2 * b + r, :],
                                           I["state_ffn_conv"][0, b, r].rearrange("(f c) -> f c", c=P)).then_inc(fl_in, 16)
                    pool.wait_ge(kv_out, 32 * 6)
                    finish(pool.memset(fue[:, :, :, 0:2], 0.0))
                else:
                    raise KeyError(x)

            pool.dma_start(prow[0:96, 0, :], I["gdn_conv_w"][0].rearrange("m (f c) -> (m f) c", c=P)).then_inc(rows_in, 16)
            pool.dma_start(prow[96:112, 0, :], I["rms_mix_w"][0].rearrange("(f c) -> f c", c=P)).then_inc(rows_in, 16)
            pool.dma_start(prow[112:128, 0, :], I["rms_ffn_w"][0].rearrange("(f c) -> f c", c=P)).then_inc(rows_in, 16)
            pool.dma_start(prow[0:16, 1, :], I["final_norm_w"].rearrange("(f c) -> f c", c=P)).then_inc(rows_in, 16)
            pool.dma_start(prow[16:17, 1, :], I["gdn_norm_w"]).then_inc(rows_in, 16)
            prev_rows = I["state_gdn_conv"][0].rearrange("b r (f c) -> (b r f) c", c=P)
            pool.dma_start(prow[:, 2:6, :], prev_rows[0:512, :].rearrange("(r p) c -> p r c", p=P)).then_inc(rows_in, 16)
            pool.dma_start(prow[0:64, 6, :], prev_rows[512:576, :]).then_inc(rows_in, 16)
            after(pool, "V", "init")
            pool.dma_start(sm("dtb"), I["gdn_dt_bias"].broadcast_to([P, NH])).then_inc(rows_in, 16)
            pool.dma_start(sm("alog"), I["gdn_a_log"].broadcast_to([P, NH])).then_inc(rows_in, 16)
            pool.dma_start(sm("rb", NBK), I["rel_bias"]).then_inc(rows_in, 16)
            pool.dma_start(wab[:, :, :], w_in[:, 7 * W:].rearrange("(k p) n -> p k n", p=P)).then_inc(ab_in, 16)
            pool.dma_start(ptab[:, :], I["page_table"].rearrange("b n -> (b n)").rearrange("(a n) -> a n", a=1)).then_inc(pt_in, 16)
            for x in SLOTS[-1]:
                if x[0] == "G":
                    step(x)
            after(pool, "G", "rbout")
            pool.memset(ue[:, :, 0:3], 0.0).then_inc(pads_done, 1)
            pads(0)
            for c in range(NC1):
                for n, (name, p) in enumerate(PAIRS[:NGA]):
                    if c - 1 == FIRST[name] + 4 * p + 3 and name[0] == "g":
                        if p < 6:
                            new_rows(n)
                        nxt = {5: n + 3}.get(p, n + 1)
                        if p < 5 or (p == 5 and name == "g0"):
                            pads(nxt)
                for x in SLOTS[c]:
                    if x[0] == "G":
                        step(x)

            def f_pads(blk, r, par):
                n = blk * 4 + r
                kind = r % 2
                if r == 0:
                    pool.wait_ge(f["stage"], blk + 1)
                if not isinstance(n, int) or n >= 2:
                    pool.wait_ge(f["conv"], n - 1)
                for j in range(2):
                    old = fst[:, par, kind, r // 2 * 2 + j, 4:20].rearrange("p (b r) -> p b r", b=DB)
                    ins = pool.tensor_tensor(fue[:, kind, j, 2 + SEQ:338].rearrange("p (b s) -> p b s", b=DB)[:, :, 0:2],
                                             old, C("ones", P, 16).rearrange("p (b r) -> p b r", b=DB), ALU.mult)
                ins.then_inc(f["pad"], 1)

            def f_events(blk, q, par):
                if q in (2, 6, 10, 14):
                    f_pads(blk, q // 4, par)

            after(pool, "G", "fload")
            pool.memset(fue[:, :, :, 0:2], 0.0).then_inc(f["pad"], 1)
            for q in range(16):
                f_events(0, q, 0)
            with pool.Fori(0, NLOOP) as it:
                for t in range(48):
                    half, q = t // 24, t % 24
                    f_events(it * 2 + (1 + half), q, (1 + half) % 2)
            for r in range(5):
                pool.wait_ge(fin["ne"], r + 1)
            pool.dma_start(O["fcp"][0, 0].rearrange("r (f c) -> f r c", c=P), frow[0:88, 0:2, :]).then_inc(fin["no"], 16)
            for b in range(DB):
                pool.dma_start(O["fcs"][0, b].rearrange("r (f c) -> f r c", c=P), frow[0:88, 2 + 2 * b:4 + 2 * b, :])\
                    .then_inc(fin["no"], 16)
            for q in range(4):
                for t in range(3):
                    n, c0 = unit(t)
                    pool.wait_ge(fin["ev"], 3 * q + t + 1)
                    y = O["yp"][0, c0:c0 + n] if t < 2 else O["ys"].rearrange("b t d -> (b t) d")
                    pool.dma_start(y[:, 512 * q:512 * q + 512], yo[0:n, t, 512 * q:512 * q + 512]).then_inc(fin["out"], 16)
            pool.wait_ge(fin["out"], 16 * 12)
            pool.wait_ge(fin["no"], 16 * 9)
            pool.wait_ge(gs_out, 16 * 7)
            pool.wait_ge(st_out, 32)
            pool.wait_ge(s_out, 16 * 8)
            pool.wait_ge(kv_out, 32 * 6)


_INS = ["x_prompt", "x_sample", "cache_k", "cache_v", "page_table", "state_gdn", "state_gdn_conv", "state_ffn_conv",
        "rms_mix_w", "w_in", "gdn_conv_w", "gdn_a_log", "gdn_dt_bias", "gdn_norm_w", "w_out", "rms_ffn_w", "w_up",
        "ffn_conv_w", "ffn_conv_b", "w_down", "rel_bias", "final_norm_w"]
_OUTS = [("yp", (1, SEQ, DM)), ("ys", (DB, DT, DM)), ("kp", (1, 1, SEQ, NH, P)), ("vp", (1, 1, SEQ, NH, P)),
         ("sp", (1, 1, NH, P, P)), ("gcp", (1, 1, 3, 3 * W)), ("fcp", (1, 1, 2, 2 * DFF)),
         ("ks", (1, DB, DT, NH, P)), ("vs", (1, DB, DT, NH, P)), ("ss", (1, DB, NH, P, P)),
         ("gcs", (1, DB, 3, 3 * W)), ("fcs", (1, DB, 2, 2 * DFF))]


def kernel(**inputs):
    import concourse.bacc as bacc
    from concourse.bass_utils import run_bass_kernel_spmd

    nc = bacc.Bacc("TRN2", target_bir_lowering=False, num_devices=1)
    arrays = {f"in_{n}_dram": np.ascontiguousarray(inputs[n]) for n in _INS}
    arrays["in_consts_dram"] = CONSTS
    I = {n[3:-5]: nc.dram_tensor(n, a.shape, mybir.dt.from_np(a.dtype), kind="ExternalInput").ap() for n, a in arrays.items()}
    O = {n: nc.dram_tensor(f"out_{n}_dram", s, F32, kind="ExternalOutput").ap() for n, s in _OUTS}
    build(nc, I, O)
    r = run_bass_kernel_spmd(nc, [arrays], core_ids=[0])
    return tuple(r.results[0][f"out_{n}_dram"] for n, _ in _OUTS)
```

```python
import math

import numpy as np

import concourse.bass as bass
from concourse import mybir

F32 = mybir.dt.float32
F32R = mybir.dt.float32r
I32 = mybir.dt.int32
ACT = mybir.ActivationFunctionType
ALU = mybir.AluOpType
AX = mybir.AxisListType

P = 128
DM = 2048
KT = DM // P
SEQ, DB, DT = 256, 8, 8
NS = DB * DT
TOK = SEQ + NS
NH = 8
W = NH * P
DIN = 7 * W + 2 * NH
DFF = 5632
FT = DFF // P
NBK = 32
NEG = -1e30
EPS = 1e-6
SCALE = P ** -0.5
CQ = 4
CC = 256
RING = 4

LEVELS = [1, 2, 4, 8, 16, 32, 64]
CONST_COLS = {}


def constants():
    i = np.arange(P)
    c, r = i[None, :], i[:, None]
    parts = {
        "ident": c == r,
        "flip": c == P - 1 - r,
        "ones": np.ones((P, P)),
        "upto": r <= c,
        "upto8": (r <= c) & (r // DT == c // DT),
        "same8": r // DT == c // DT,
        "negP": np.where(r <= c, 0.0, NEG),
        "neg8": np.where((r <= c) & (r // DT == c // DT), 0.0, NEG),
        "causal": np.where(c <= r, 0.0, NEG),
        "batch": (r // DT == np.arange(DB)[None, :]),
    }
    for s in LEVELS:
        parts[f"lev{s}"] = (r // (2 * s) == c // (2 * s)) & (r // s != c // s) & (r < c)
    m = np.arange(3 * P)
    n = np.maximum(2 * P - 1 - m, 0)
    nf = np.maximum(n, 1).astype(np.float32)
    half = NBK // 2
    large = half + (np.log(nf / np.float32(half)) / np.float32(math.log(128 / half)) * half).astype(np.int32)
    bucket = np.where(n < half, n, np.minimum(large, NBK - 1))
    parts["bucket"] = np.concatenate([bucket[None, :] == np.arange(NBK)[:, None], np.zeros((P - NBK, 3 * P))], 0)
    at = 0
    for k, v in parts.items():
        CONST_COLS[k] = (at, v.shape[1])
        at += v.shape[1]
    return np.concatenate([np.asarray(v, np.float32) for v in parts.values()], 1)


CONSTS = constants()


PHASES = [("g0", 8, 4), ("g1", 8, 4), ("a0", 6, 4), ("a1", 6, 4), ("wg", 8, 2),
          ("wa0", 8, 1), ("wa1", 8, 1)]


OUT_ROWS = {"wg": 2, "wa0": 0, "wa1": 1}


def chunk_list():
    out = []
    for name, pairs, per in PHASES:
        for p in range(pairs):
            for q in range(per):
                out.append((name, p, q, per))
    return out


CHUNKS = chunk_list()
NC1 = len(CHUNKS)
FIRST = {}
for _n, (_name, _p, _q, _per) in enumerate(CHUNKS):
    FIRST.setdefault(_name, _n)
FIRST["end"] = NC1
PER = {name: per for name, _, per in PHASES}
PAIRS = [(n, p) for n, ps, _ in PHASES for p in range(ps)]


def pair_index(name, p):
    return PAIRS.index((name, p))


KINDS_A = (1, 2, 0)


def tile_of(name, p, j):
    t = 2 * p + j
    return (KINDS_A[t // 4] if name[0] == "a" else t // 4), t % 4


def setup_steps():
    s = [("V", "init"), ("A", "sq", 0), ("V", "ms", 0), ("G", "rs", 0), ("V", "xs", 0), ("A", "sq", 1), ("V", "ms", 1),
         ("G", "rs", 1), ("P", "rows"), ("V", "rows"), ("A", "sq", 2), ("V", "ms", 2), ("G", "rs", 2)]
    xl = None
    for t in range(3):
        for q in range(4):
            s += [("P", "xt", t, q), ("V", "xw", t, q), ("A", "xh", t, q)] + ([xl] if xl else [])
            xl = ("V", "xl", t, q)
            if q == 0 and t < 2:
                s += [("V", "xs", t + 1)]
    return s + [xl, ("A", "alog"), ("V", "wab"), ("P", "prev"), ("A", "prev"), ("P", "rb"), ("A", "rb"), ("G", "rbout")]


def scalar_steps():
    return [("P", "ab"), ("A", "ab"), ("P", "abt"), ("V", "sc1"), ("A", "sc2"), ("V", "sc3"), ("P", "cum"),
            ("V", "sc4"), ("A", "sc5")]


def raw_steps():
    return [x for t in range(3) for q in range(4) for x in (("P", "rt", t, q), ("A", "rt", t, q))]


def gdn_steps(g):
    s = []
    tail = []
    for u in (0, 1, 2):
        k = (g, u)
        if u == 2:
            s += [("G", "si", g, 0), ("G", "si", g, 1)]
        s += [("V", "gt", *k), ("P", "tr", *k), ("A", "qs", *k), ("A", "cp", *k)] + tail
        s += [("P", "cg", *k), ("V", "dm", *k), ("A", "de", *k), ("V", "ss", *k), ("G", "rn", *k)] + ([("V", "bv", *k)] if u else []) + [("V", "sc", *k),
              ("P", "tq", *k), ("V", "sb", *k), ("A", "tb1", *k), ("P", "tb1", *k), ("V", "sk", *k), ("V", "tb1", *k),
              ("P", "kk", *k)]
        if u:
            s += [("P", "tb2", *k), ("A", "tb2", *k)]
        s += [("V", "kk", *k), ("G", "mk", *k, 2), ("P", "x1", *k), ("A", "x1", *k)]
        levels = unit_levels(u)
        states = [("P", "sh", g, 0), ("G", "si", g, 2)], [("P", "sh", g, 1), ("G", "si", g, 3)], \
            [("P", "sh", g, 2), ("G", "s2", g, 0)], [("P", "sh", g, 3), ("G", "s2", g, 1)]
        for l in levels:
            s += [("P", "pl", *k, l), ("A", "pl", *k, l)]
            if u == 2:
                s += states[0] if l == 2 else states[2]
            if l != levels[-1]:
                s += [("G", "mk", *k, 2 * l), ("P", "dx", *k, l), ("V", "dx", *k, l)]
            s += [("P", "dt", *k, l), ("V", "dt", *k, l)]
            if u == 0 and l == 16:
                s += [("P", "tv", *k), ("V", "bv", *k)]
            if u == 2:
                s += states[1] if l == 2 else states[3]
        if u == 1:
            s += [("P", "ks", *k), ("V", "ks", *k)]
        if u == 2:
            s += [("A", "sh", g, 0), ("P", "ks", *k), ("V", "ks", *k)]
        s += [("P", "u", *k), ("A", "u", *k), ("P", "os", *k), ("A", "o", *k)]
        if u < 2:
            s += [("V", "st", *k)]
            if u == 1:
                s += [("G", "so", g, 4)]
        s += [("V", "o1", *k), ("G", "or", *k)]
        tail = [("V", "o2", *k), ("P", "ot", *k), ("V", "oz", *k)]
    s += [("V", "um", g, 0)]
    for h in range(4):
        s += [("P", "us", g, h)] + ([("V", "um", g, h + 1)] if h < 3 else [])
        s += [("V", "us", g, h), ("G", "so", g, h)] + ([("G", "s2", g, h + 2)] if h < 2 else [])
        if h == 0:
            s += tail
    return s


def unit_levels(u):
    return LEVELS[1:] if u < 2 else [2, 4]


def state_steps():
    s = []
    for r in range(6):
        s += [("P", "gs", r), ("A", "gs", r), ("G", "gs", r)]
    return s


def att_steps(g):
    s = ([] if g else [("G", "hk", g)]) + [("G", "pk", g, 0), ("G", "pv", g, 0), ("G", "pk", g, 1), ("G", "pv", g, 1), ("P", "hk", g), ("V", "hk", g)]
    if g == 0:
        s += [("G", "hk", 1)]
    for t in range(3):
        s += [("P", "kv", g, t), ("A", "kv", g, t), ("G", "kv", g, t)]
    s += [("P", "S", g, 0), ("V", "S", g, 0), ("A", "E", g, 0)]
    for h in range(4):
        if h < 3:
            s += [("P", "S", g, h + 1), ("V", "S", g, h + 1)]
        s += [("V", "N", g, h), ("P", "T", g, h), ("A", "T", g, h)] + ([("A", "E", g, h + 1)] if h < 3 else [])
        s += [("P", "O", g, h), ("A", "O", g, h)]
    s += [("P", "kt", g, 0), ("A", "kt", g, 0), ("V", "kt", g, 0), ("G", "pk", g, 2)]
    for b in range(DB):
        s += [("P", "SS", g, b), ("V", "SS", g, b), ("A", "SE", g, b)]
        if b < DB - 1:
            s += [("P", "kt", g, b + 1), ("A", "kt", g, b + 1), ("V", "kt", g, b + 1)]
            if b < DB - 3:
                s += [("G", "pk", g, b + 3)]
        s += [("V", "SN", g, b), ("P", "PT", g, b), ("A", "PT", g, b), ("P", "PV", g, b),
              ("A", "PV", g, b), ("P", "OT", g, b), ("A", "OT", g, b)]
        if b < DB - 2:
            s += [("G", "pv", g, b + 2)]
    return s


def ffn_param_steps():
    s = []
    for r in range(5):
        s += [("P", "fp", r), ("A", "fp", r)]
    return s


LENGTH = {
    "P": {"tr": 17, "tb1": 17, "tq": 17, "tb2": 6, "cg": 11, "kk": 17, "x1": 7, "pl": 11, "dx": 11, "dt": 11, "u": 11,
          "os": 24, "ot": 5,
          "ks": 13, "us": 40, "sh": 11, "hk": 20, "kv": 12, "S": 11, "O": 12, "kt": 17, "SS": 11, "PV": 11, "OT": 2, "ab": 76},
    "A": {"sc2": 25, "sc5": 20, "ab": 10, "qs": 12, "cp": 0, "tb1": 10, "o": 12, "kv": 12, "E": 11, "SE": 7, "fp": 22},
    "V": {"sc1": 11, "sc3": 50, "sc4": 15, "ss": 17, "bv": 0, "sc": 27, "sb": 10, "sk": 0, "gt": 0, "tb1": 12, "dm": 0, "kk": 32,
          "dt": 3, "dx": 7, "st": 11, "o1": 9, "um": 14, "us": 19, "hk": 40,
          "S": 13, "SS": 17, "SN": 7},
    "G": {"rn": 29, "or": 14, "so": 0, "si": 0, "s2": 0, "gs": 0, "kv": 0, "pk": 0, "pv": 0, "hk": 100, "mk": 0},
}
AHEAD = {"P": 0, "A": -1, "V": -1, "G": -4}
PACE = {"P": 0.85, "A": 1, "V": 1, "G": 1}
SPREAD = {"delta": 1.1, "attention": 1}
PARTS = 4

EARLY_A = ("hk", "pk", "pv", "kv")


def gdn_first(x, start):
    if x[2:4] in ((0, 0), (1, 0)):
        if x[1] in ("tr", "gt", "qs", "cp"):
            return start + 19
        if x[1] == "tv":
            return start + 27
    return start + 34 if x[1] == "oz" else 0


def schedule():
    slots = {(c, r): [] for c in range(-1, NC1) for r in range(PARTS)}
    slots[-1, 0] = setup_steps()
    chain = [(x, 4) for x in scalar_steps()] + [(x, 10) for x in raw_steps()]
    chain += [(x, gdn_first(x, FIRST["g0"])) for x in gdn_steps(0)]
    chain += [(x, gdn_first(x, FIRST["g1"])) for x in gdn_steps(1)]
    chain += [(x, FIRST["g1"] + 27) for x in state_steps()]
    chain += [(x, FIRST["a0"] + 18 if x[1] in EARLY_A else FIRST["a1"] + 2) for x in att_steps(0)]
    chain += [(x, FIRST["wg"] + 1) for x in (("A", "ma", 0), ("V", "ma", 0))]
    chain += [(x, FIRST["a1"] + 18 if x[1] in EARLY_A else FIRST["wg"] + 2) for x in att_steps(1)]
    order = [x for x, _ in chain]
    attention = set(att_steps(0) + att_steps(1))

    def length(x):
        return LENGTH[x[0]].get(x[1], 5) * PACE[x[0]] * SPREAD["attention" if x in attention else "delta"]

    at, i = 0, 0
    ready = 0
    for c in range(NC1):
        for r in range(PARTS):
            at += 40 / PARTS
            while i < len(chain):
                x, first = chain[i]
                if first > c or ready > at:
                    break
                slots[c, r].append(x)
                if x[0] == "P":
                    at += length(x)
                    ready = at + AHEAD["P"]
                else:
                    ready = max(ready, at) + length(x) + AHEAD[x[0]]
                i += 1
                while i < len(chain) and chain[i][0][0] != "P" and chain[i][1] <= c:
                    x = chain[i][0]
                    slots[c, r].append(x)
                    ready += length(x) + AHEAD[x[0]]
                    i += 1
            for until, last in ((FIRST["a0"] + 3, ("G", "so", 0, 3)), (FIRST["a1"] + 3, ("G", "so", 1, 3)),
                                (FIRST["wa1"] - 1, chain[-1][0])):
                end = order.index(last) + 1
                if (c, r) == (until, 0 if until < FIRST["wg"] else PARTS - 1) and i < end:
                    slots[c, r] += order[i:end]
                    i = end
                    ready = at
    slots[FIRST["wg"] - 1, PARTS - 1] += [("A", "mg", 0), ("V", "mg", 0), ("A", "mg", 1), ("V", "mg", 1)]
    slots[FIRST["wg"] + 1, 0].append(("A", "fload"))
    slots[FIRST["wa1"] - 1, PARTS - 1] += [("A", "ma", 1), ("V", "ma", 1), ("G", "fz")]
    steps = ffn_param_steps()
    for n in range(5):
        slots[FIRST["wa1"] + 1 + n, 0] += steps[2 * n:2 * n + 2]
    return slots


SLOTS = schedule()
TRANSFERS = {"si", "s2", "so", "gs", "hk", "kv", "pk", "pv"}


def tallies():
    n, at = {}, {}
    for at_ in sorted(SLOTS):
        for x in SLOTS[at_]:
            if (x[0] == "G" and x[1] in TRANSFERS) or x[1] == "fload":
                continue
            n[x[0]] = n.get(x[0], 0) + 1
            at[x] = n[x[0]]
    return at


TALLY = tallies()

NGA = 28
NB = FT // 4
NLOOP = (NB - 1) // 2
NROWS = 3


def before_unit(g, u):
    if u:
        return ("A", "o", g, u - 1)
    return ("V", "us", 0, 3) if g else ("A", "rt", 2, 3)


def wa_pair(c):
    return c - FIRST["wa1"] if FIRST["wa1"] <= c < NC1 else None


def block_start(blk):
    if isinstance(blk, int) and blk == 0:
        return NC1
    return blk * 24 + (NC1 + 16 - 24)


def down_start(blk):
    return blk * 24 + (NC1 + 16 + 16) if not (isinstance(blk, int) and blk == NB - 1) else NC1 + 16 + 24 * (NB - 1)


def heads(ap, n):
    return ap[:, 0:4 * n].rearrange("p (h n) -> p h n", h=4)


def build(nc, I, O):
    base = -(-nc.sbuf_base // 64) * 64
    top = nc.sbuf_usable_end

    class Span:
        def __init__(self, at):
            self.at = at

        def put(self, name, shape, dt=F32):
            size = 4 * int(np.prod(shape[1:]))
            t = nc.alloc_sbuf_tensor_at(name, shape, dt, offset=self.at)
            self.at += -(-size // 64) * 64
            assert self.at <= top, (name, self.at - top)
            return t

    sp_ = Span(base)
    raw = sp_.put("w_raw", [P, RING, CQ, CC])
    whi = sp_.put("w_hi", [P, RING, CQ, CC], F32R)
    wlo = sp_.put("w_lo", [P, RING, CQ, CC], F32R)
    xres = sp_.put("x_res", [P, KT, TOK])
    yo_at = sp_.at
    xhi = sp_.put("x_hi", [P, KT, TOK], F32R)
    xlo = sp_.put("x_lo", [P, KT, TOK], F32R)
    cst = sp_.put("consts", [P, CONSTS.shape[1]])
    small = sp_.put("small", [P, 640])
    pT = sp_.put("params_t", [P, 160])
    ptab = sp_.put("page_table_row", [1, 16], I32)
    mixer_at = sp_.at

    m = Span(mixer_at)
    reg = [m.put(f"reg{g}", [P, 12, TOK]) for g in range(2)]
    zz_at = m.at
    zz = m.put("z_gate", [P, 8, TOK])
    work_at = m.at
    qn = m.put("q_norm", [P, 4, P])
    kb = m.put("k_beta", [P, 4, P])
    setat = m.at
    tq = m.put("tok_q", [P, 4, P])
    tk = m.put("tok_k", [P, 4, P])
    bv = m.put("tok_bv", [P, 4, P])
    qk = m.put("qk_t", [P, 4, P])
    at_ = m.put("a_t", [P, 4, P])
    xx = m.put("inv", [P, 4, P])
    pp = m.put("prod", [P, 4, P])
    dec = m.put("decay", [P, 4, P])
    xt = m.put("inv_t", [P, 4, P])
    ub = m.put("u_tok", [P, 4, P])
    S = m.put("state", [P, 4, P])
    ssm = m.put("state_s", [P, 2, DB, P])
    ue_at = m.at
    ue = m.put("u_ext", [P, 2, 348])
    acc = m.put("conv_acc", [P, 2, 348])
    prevT = m.put("prev_t", [P, DB * 3, 24])
    gnew = m.put("gdn_new", [P, 27, 24])
    umask = nc.alloc_sbuf_tensor_at("u_mask", [P, DB, P], F32, offset=setat + 4 * 2048)
    w = Span(work_at)
    xraw = w.put("x_raw", [P, 3, DM])
    tmpx = w.put("x_tmp", [P, 2, 4, P])
    prow = w.put("p_rows", [P, 7, P])
    assert w.at <= ue_at
    r0 = Span(mixer_at)
    xs = r0.put("x_scaled", [P, 2, DM])
    xsq = r0.put("x_squares", [P, DM])
    wab = r0.put("w_ab", [P, KT, 16])
    wabh = r0.put("w_ab_hi", [P, KT * 16 + 112], F32R)
    wabl = r0.put("w_ab_lo", [P, KT * 16 + 112], F32R)
    abT = r0.put("ab_t", [P, TOK])
    rsb0 = r0.put("rb_rows", [P, 3 * P])
    a = Span(work_at)
    vt = a.put("v_tok", [P, 3, 4, P])
    kst = a.put("k_tok", [P, 2, 4, P])
    hk = a.put("hankel", [P, 4, 2 * P])
    bm = a.put("bias_q", [P, 4, 2 * P])
    bs = a.put("bias_s", [P, 2 * P + 120])
    sc = a.put("scores", [P, 2, 384])
    pt = a.put("probs_t", [P, 2, 384])
    ktp = a.put("k_t_past", [P, 4, 2 * P])
    kp = a.put("k_pages", [P, 2, 2, 4, P])
    vp = a.put("v_pages", [P, 2, 2, 4, P])
    ob = a.put("o_tok", [P, P])
    ast = a.put("att_small", [P, 2, 8])
    gst = nc.alloc_sbuf_tensor_at("gdn_new_rows", [P, 6, P], F32, offset=ue_at)

    fm = Span(mixer_at)
    pF = fm.put("ffn_params_t", [P, 2 * FT, 20])
    fnewT = fm.put("ffn_new_t", [P, 2 * FT, 18])
    hf = fm.put("hid", [P, 2, 2, TOK])
    fue = fm.put("ffn_ext", [P, 2, 2, 338])
    sqb = fm.put("squares", [P, 2, 2, TOK])
    rs2 = fm.put("root", [P, TOK])
    assert fm.at <= zz_at
    frow = nc.alloc_sbuf_tensor_at("ffn_rows", [P, 20, P], F32, offset=zz_at)
    fm = Span(work_at)
    hhi = fm.put("hid_hi", [P, 2, 4, TOK], F32R)
    hlo = fm.put("hid_lo", [P, 2, 4, TOK], F32R)
    facc = fm.put("ffn_acc", [P, 2, 2, 338])
    xn = fm.put("x_normed", [P, 2, 4, TOK])
    fst = fm.put("ffn_stage", [P, 2, 2, 4, 20])
    yo = nc.alloc_sbuf_tensor_at("y_rows", [P, 3, DM], F32, offset=yo_at)

    n_pool = I["cache_k"].shape[1]
    rb_dram = nc.dram_tensor("rb_scratch", (NH, 3 * P), F32, kind="Internal").ap()
    psA = nc.alloc_psum_tensor("ps_proj", [P, 4, 512], F32)
    psB = nc.alloc_psum_tensor("ps_small", [P, 4, 512], F32)
    b0, b1, b2, b3 = (psB[:, i, :] for i in range(4))

    def C(name, n=P, m_=None):
        at, width = CONST_COLS[name]
        return cst[0:n, at:at + (width if m_ is None else m_)]

    cols = {}
    at = 0
    for name, n in (("ssx", 3), ("rsx", 3), ("mh", 8), ("dtb", 8), ("alog", 8), ("ab", 48), ("sa", 24), ("sb", 24),
                    ("beta", 24), ("g", 24), ("cg", 24), ("eg", 24), ("kd", 24), ("eglP", 16), ("eglS", 64),
                    ("ss", 8), ("rn", 8), ("f", 24), ("so", 4), ("ro", 4), ("gm", 64), ("nkd", 24), ("rb", 8), ("tmp", 24)):
        cols[name] = (at, n)
        at += n
    assert at <= 640

    def sm(name, n=P, lo=0, hi=None):
        a0, width = cols[name]
        return small[0:n, a0 + lo:a0 + (width if hi is None else hi)]

    def over_free(ap, count):
        return ap.unsqueeze(2).broadcast_to([ap.shape[0], ap.shape[1], count])

    def over_heads(ap, count):
        return ap.unsqueeze(1).broadcast_to([ap.shape[0], count, ap.shape[1]])

    def per_head(name, n, u, g):
        return sm(name, n, 8 * u + 4 * g, 8 * u + 4 * g + 4)

    def f_sample(kind, j):
        return facc[:, kind, j, 258:338].rearrange("p (b s) -> p b s", b=DB)[:, :, 0:DT]

    def sample_of_acc(j):
        return acc[:, j, 259:347].rearrange("p (b s) -> p b s", b=DB)[:, :, 0:DT]

    sems = {}

    def sem(name):
        sems[name] = nc.alloc_semaphore(name)
        return sems[name]

    raw_in = [sem(f"raw_in{i}") for i in range(RING)]
    hi_done, lo_done, mm_done = sem("hi_done"), sem("lo_done"), sem("mm_done")
    evac_done, conv_done, silu_done = sem("evac_done"), sem("conv_done"), sem("silu_done")
    pads_done, new_done, add_done = sem("pads_done"), sem("new_done"), sem("add_done")
    done = {"P": sem("pe_step"), "V": sem("dve_step"), "A": sem("act_step"), "G": sem("pool_step")}
    link_sem = {"V": sem("dve_link"), "A": sem("act_link"), "G": sem("pool_link")}
    consts_in, ident_in, prow_in, prev_in, rows_in = (sem(k) for k in ("consts_in", "ident_in", "param_rows_in",
                                                                       "old_rows_in", "rows_in"))
    x_in = [sem(f"x_in{t}") for t in range(3)]
    ab_in, pt_in = sem("ab_in"), sem("page_table_in")
    rb_out, hk_in, kv_out = sem("rb_out"), sem("hankel_in"), [sem(f"kv_out{i}") for i in range(2)]
    pk_in, pv_in, s_in, s_out = ([sem(f"{k}{i}") for i in range(2)] for k in ("k_pages_in", "v_pages_in", "state_in", "state_out"))
    st_out, gs_out, fl_in = sem("stateP_out"), sem("gnew_out"), sem("ffn_rows_in")
    sq2, ssq2, xn_a, xn_v, xn_h = sem("sq2"), sem("ssq2"), sem("rms2_root"), sem("xn_made"), sem("xn_hi")
    xn_l, rms_v = sem("xn_lo"), sem("rms_mean")
    f = {k: sem("ffn_" + k) for k in ("evac", "pad", "conv", "silu", "h", "hhi", "hlo", "add", "stage", "tap")}
    fin = {k: sem("fin_" + k) for k in ("sq", "ss", "ms", "mt", "mr", "r", "w", "t", "ev", "y0", "y1", "out", "nt", "ne", "no")}

    links = {"V": 0, "A": 0, "G": 0}

    def link(e, E, ins):
        links[E] += 1
        ins.then_inc(link_sem[E], 1)
        e.wait_ge(link_sem[E], links[E])

    def after(e, *key):
        e.wait_ge(done[key[0]], TALLY[key])

    def unit(u):
        return (P, u * P) if u < 2 else (NS, SEQ)

    w_in, w_out, w_up, w_down = (I[k][0] for k in ("w_in", "w_out", "w_up", "w_down"))

    def chunk_source(c):
        name, p, q, per = CHUNKS[c]
        if name[0] == "w":
            k0 = (q + OUT_ROWS[name]) * CQ
            return w_out[k0 * P:(k0 + CQ) * P, p * CC:(p + 1) * CC].rearrange("(k p) n -> p k n", p=P)
        kind, _ = tile_of(name, p, 0)
        g = int(name[1])
        col = (3 * W if name[0] == "g" else 0) + kind * W + g * 512 + (p % 2) * CC
        return w_in[q * CQ * P:(q + 1) * CQ * P, col:col + CC].rearrange("(k p) n -> p k n", p=P)

    block = nc.Block()
    with block:
        @block.sync
        def _(sp):
            def load(slot, src, use):
                sp.dma_start(raw[:, slot], src).then_inc(raw_in[slot], 16)

            for t, (r_, n) in enumerate(((0, P), (P, P), (0, NS))):
                x = I["x_prompt"][0] if t < 2 else I["x_sample"].rearrange("b t d -> (b t) d")
                sp.dma_start(xraw[0:n, t], x[r_:r_ + n, :]).then_inc(x_in[t], 16)
                if t == 0:
                    sp.dma_start(cst[:, 0:P], I["consts"][:, 0:P]).then_inc(ident_in, 16)
            sp.dma_start(cst[:, P:], I["consts"][:, P:]).then_inc(consts_in, 16)
            for c in range(NC1):
                if c >= RING:
                    sp.wait_ge(hi_done, c - RING + 1)
                    sp.wait_ge(lo_done, c - RING + 1)
                load(c % RING, chunk_source(c), c)

            def up_source(i, q):
                pp_, kind, kq = q // 8, (q // 4) % 2, q % 4
                rows = w_up[kq * CQ * P:(kq + 1) * CQ * P, :].rearrange("(k p) n -> p k n", p=P)
                return rows[:, :, bass.DynSlice(i * 512 + kind * DFF + pp_ * CC, CC)]

            def down_source(i, d):
                return w_down[bass.DynSlice(i * 512, 512), d * CC:(d + 1) * CC].rearrange("(k p) n -> p k n", p=P)

            def stream(c, src):
                sp.wait_ge(hi_done, c - RING + 1)
                sp.wait_ge(lo_done, c - RING + 1)

            c = NC1
            for q in range(16):
                stream(c + q, None)
                load((c + q) % RING, up_source(0, q), None)
            c += 16
            with sp.Fori(0, NLOOP) as it:
                for t in range(48):
                    half, q = t // 24, t % 24
                    stream(it * 48 + (c + t), None)
                    i = it * 2 + half
                    load(t % RING, up_source(i + 1, q) if q < 16 else down_source(i, q - 16), None)
            c += 48 * NLOOP
            for d in range(8):
                stream(c + d, None)
                load(d % RING, down_source(NB - 1, d), None)
            for t, (ready, count) in enumerate((("y0", 1), ("y1", 1), ("y0", 2))):
                n, c0 = unit(t)
                sp.wait_ge(fin[ready], count)
                y = O["yp"][0, c0:c0 + n] if t < 2 else O["ys"].rearrange("b t d -> (b t) d")
                sp.dma_start(y, yo[0:n, t, :]).then_inc(fin["out"], 16)
            sp.wait_ge(fin["out"], 16 * 3)

        @block.scalar
        def _(act):
            def finish(ins):
                ins.then_inc(done["A"], 1)

            def hi_part(c, slot, use):
                act.wait_ge(raw_in[slot], use * 16 + 16)
                if not isinstance(c, int) or c >= RING:
                    act.wait_ge(mm_done, c - RING + 1)
                act.activation(whi[:, slot], raw[:, slot], ACT.Copy).then_inc(hi_done, 1)

            def evac(n):
                name, p = PAIRS[n]
                bank = 2 * (n % 2)
                kind, h = tile_of(name, p, 0)
                g = int(name[1])
                act.wait_ge(mm_done, FIRST[name] + 4 * p + 4)
                two = psA[:, bank:bank + 2, 0:TOK]
                if name[0] == "a":
                    if p == 0:
                        after(act, "V", "us", g, 3)
                        after(act, "V", "oz", g, 2)
                        after(act, "P", "us", g, 3)
                    act.activation(reg[g][:, kind * 4 + h:kind * 4 + h + 2, :], two, ACT.Copy).then_inc(evac_done, 1)
                elif kind == 3:
                    act.activation(zz[:, g * 4 + h:g * 4 + h + 2, :], two, ACT.Silu).then_inc(evac_done, 1)
                else:
                    gp = g * 6 + p
                    if gp >= 1:
                        act.wait_ge(conv_done, gp)
                        act.wait_ge(new_done, gp)
                    act.activation(ue[:, :, 3:3 + SEQ], two[:, :, 0:SEQ], ACT.Copy)
                    for j in range(2):
                        ins = act.activation(ue[:, j, 3 + SEQ:347].rearrange("p (b s) -> p b s", b=DB)[:, :, 3:11],
                                             two[:, j, SEQ:TOK].rearrange("p (b t) -> p b t", b=DB), ACT.Copy)
                    ins.then_inc(evac_done, 1)

            def silu(n):
                name, p = PAIRS[n]
                kind, h = tile_of(name, p, 0)
                g = int(name[1])
                gp = g * 6 + p
                act.wait_ge(conv_done, gp + 1)
                if n == 0:
                    act.wait_ge(rb_out, 16)
                t = kind * 4 + h
                act.activation(reg[g][:, t:t + 2, 0:SEQ], acc[:, :, 0:SEQ], ACT.Silu)
                for j in range(2):
                    ins = act.activation(reg[g][:, t + j, SEQ:TOK].rearrange("p (b t) -> p b t", b=DB),
                                         sample_of_acc(j), ACT.Silu)
                ins.then_inc(silu_done, 1)

            def step(x):
                name = x[1]
                k = x[2:]
                if name == "alog":
                    act.wait_ge(rows_in, 16 * NROWS)
                    finish(act.activation(sm("alog"), sm("alog"), ACT.Exp))
                elif name == "prev":
                    after(act, "P", "prev")
                    act.activation(prevT[:, :, :].rearrange("p r f -> p (r f)")[:, 0:512], b1, ACT.Copy)
                    finish(act.activation(prevT[:, :, :].rearrange("p r f -> p (r f)")[:, 512:576], b2[:, 0:64], ACT.Copy))
                elif name == "rb":
                    after(act, "P", "rb")
                    finish(act.activation(rsb0[0:NH, :], b3[0:NH, 0:3 * P], ACT.Copy))
                elif name == "sq":
                    t = k[0]
                    n = unit(t)[0]
                    act.wait_ge(x_in[t], 16)
                    after(act, *(("A", "sq", t - 1) if t else ("V", "init")))
                    finish(act.activation(xsq[0:n], xraw[0:n, t], ACT.Square, accum_out=sm("ssx", n, t, t + 1)))
                elif name == "xh":
                    t, q = k
                    n, c0 = unit(t)
                    after(act, "V", "xw", t, q)
                    finish(act.activation(xhi[:, 4 * q:4 * q + 4, c0:c0 + n], tmpx[:, q % 2, :, 0:n], ACT.Copy))
                elif name == "rt":
                    t, q = k
                    n, c0 = unit(t)
                    after(act, "P", "rt", t, q)
                    finish(act.activation(xres[:, 4 * q:4 * q + 4, c0:c0 + n],
                                          b3[:, 0:4 * n].rearrange("p (k n) -> p k n", k=4), ACT.Copy))
                elif name == "ab":
                    after(act, "P", "ab")
                    finish(act.activation(abT[0:16, :], b0[0:16, 0:TOK], ACT.Copy))
                elif name == "sc2":
                    after(act, "V", "sc1")
                    link(act, "A", act.activation(sm("sb"), sm("sb"), ACT.Exp, scale=-1.0))
                    act.activation(sm("tmp").rearrange("p (u h) -> p u h", u=3),
                                   sm("ab").rearrange("p (u c) -> p u c", u=3)[:, :, 8:16], ACT.Exp, scale=-1.0)
                    finish(act.activation(sm("sb"), sm("sb"), ACT.Ln, bias=1.0))
                elif name == "sc5":
                    after(act, "V", "sc4")
                    act.activation(sm("eg"), sm("cg"), ACT.Exp)
                    act.activation(sm("kd"), sm("nkd"), ACT.Exp)
                    act.activation(sm("eglP"), b2[:, 24:40], ACT.Exp)
                    finish(act.activation(sm("eglS"), b2[:, 64:128], ACT.Exp))
                elif name == "qs":
                    g, u = k
                    n, _ = unit(u)
                    after(act, "P", "tr", g, u)
                    act.activation(xt[0:n].rearrange("p h d -> p (h d)"), b0[0:n], ACT.Square)
                    finish(act.activation(xx[0:n].rearrange("p h d -> p (h d)"), b1[0:n], ACT.Square))
                elif name == "cp":
                    n = unit(k[1])[0]
                    after(act, "P", "tr", *k)
                    act.activation(tq[0:n].rearrange("p h d -> p (h d)"), b0[0:n], ACT.Copy)
                    finish(act.activation(tk[0:n].rearrange("p h d -> p (h d)"), b1[0:n], ACT.Copy))
                elif name == "tb1":
                    g, u = k
                    n, c0 = unit(u)
                    after(act, "P", "tq", g, u)
                    act.activation(qn[:, :, 0:n], heads(b0, n), ACT.Copy)
                    finish(act.activation(reg[g][:, 4:8, c0:c0 + n], heads(b1, n), ACT.Copy))
                elif name == "tb2":
                    g, u = k
                    n, c0 = unit(u)
                    after(act, "P", "tb2", g, u)
                    finish(act.activation(reg[g][:, 0:4, c0:c0 + n], heads(b0, n), ACT.Copy))
                elif name == "de":
                    n = unit(k[1])[0]
                    after(act, "V", "dm", *k)
                    finish(act.activation(dec[0:n, :, 0:n], dec[0:n, :, 0:n], ACT.Exp))
                elif name in ("x1", "pl"):
                    n = unit(k[1])[0]
                    after(act, "P", name, *k)
                    if name == "x1":
                        after(act, "V", "kk", *k[:2])
                    dst = xx if name == "x1" else pp
                    finish(act.activation(dst[0:n, :, 0:n], heads(b0[0:n], n), ACT.Copy))
                elif name == "u":
                    n = unit(k[1])[0]
                    after(act, "P", "u", *k)
                    finish(act.activation(ub[0:n].rearrange("p h d -> p (h d)"), b1[0:n], ACT.Copy))
                elif name == "sh":
                    after(act, "P", "sh", k[0], 3)
                    finish(act.activation(pp[:, :, :].rearrange("p h d -> p (h d)"), b3, ACT.Copy))
                elif name == "o":
                    n = unit(k[1])[0]
                    after(act, "P", "os", *k)
                    act.activation(bv[0:n].rearrange("p h d -> p (h d)"), b2[0:n], ACT.Copy)
                    finish(act.activation(qk[0:n].rearrange("p h d -> p (h d)"), b2[0:n], ACT.Square))
                elif name == "gs":
                    r = k[0]
                    n = min(P, 648 - r * P)
                    after(act, "P", "gs", r)
                    finish(act.activation(gst[0:n, r, :], psB[0:n, r % 2, 0:P], ACT.Copy))
                elif name == "kv":
                    g, t = k
                    n = unit(t)[0]
                    after(act, "P", "kv", g, t)
                    if g == 0 and t == 0:
                        after(act, "V", "us", 1, 3)
                        act.wait_ge(hk_in, 16)
                    if 3 * g + t >= 2:
                        act.wait_ge(kv_out[t % 2 if g == 0 else (t + 1) % 2], 32 * ((3 * g + t) // 2))
                    if g == 1:
                        act.wait_ge(kv_out[t % 2], 32 * (1 if t == 1 else 2))
                    act.activation(kst[0:n, (3 * g + t) % 2].rearrange("p h d -> p (h d)"), b0[0:n], ACT.Copy)
                    finish(act.activation(vt[0:n, t].rearrange("p h d -> p (h d)"), b1[0:n], ACT.Copy))
                elif name == "E":
                    g, h = k
                    after(act, "V", "S", g, h)
                    s_ = sc[:, h % 2]
                    r_ = ast[:, h % 2]
                    act.activation(s_[:, 0:256], s_[:, 0:256], ACT.Exp, bias=r_[:, 0:1], accum_out=r_[:, 2:3])
                    finish(act.activation(s_[:, 256:384], s_[:, 256:384], ACT.Exp, bias=r_[:, 1:2], accum_out=r_[:, 3:4]))
                elif name == "T":
                    g, h = k
                    after(act, "P", "T", g, h)
                    finish(act.activation(pt[:, h % 2], b2[:, 0:384], ACT.Copy))
                elif name == "O":
                    g, h = k
                    after(act, "P", "O", g, h)
                    finish(act.activation(reg[g][:, h, 0:SEQ], b3[:, 0:SEQ], ACT.Copy))
                elif name == "kt":
                    after(act, "P", "kt", *k)
                    finish(act.activation(ktp[:, :, 0:P], heads(b0, P), ACT.Copy))
                elif name == "SE":
                    after(act, "V", "SS", *k)
                    finish(act.activation(sc[:, 0, 0:TOK], sc[:, 0, 0:TOK], ACT.Exp, bias=ast[:, 0, 0:1], accum_out=ast[:, 0, 2:3]))
                elif name == "PT":
                    after(act, "P", "PT", *k)
                    act.activation(pt[:, 0, 0:256], b3[:, 0:256], ACT.Copy)
                    finish(act.activation(pt[0:NS, 0, 256:384], b3[0:NS, 256:384], ACT.Copy))
                elif name == "PV":
                    after(act, "P", "PV", *k)
                    finish(act.activation(ob[:, :], b0[:, 0:P], ACT.Copy))
                elif name == "OT":
                    g, b = k
                    after(act, "P", "OT", *k)
                    finish(act.activation(reg[g][:, 0:4, SEQ + b * DT:SEQ + b * DT + DT],
                                          b1[:, 0:P].rearrange("p (h s) -> p h s", h=4)[:, :, 0:DT], ACT.Copy))
                elif name == "mg":
                    g = k[0]
                    after(act, "V", "oz", g, 2)
                    act.wait_ge(mm_done, FIRST["wg"])
                    finish(act.activation(xhi[:, 8 + 4 * g:12 + 4 * g, :], zz[:, 4 * g:4 * g + 4, :], ACT.Copy))
                elif name == "ma":
                    g = k[0]
                    act.wait_ge(mm_done, FIRST["wg"])
                    after(act, "A", "OT", g, DB - 1)
                    finish(act.activation(xhi[:, 4 * g:4 * g + 4, :], reg[g][:, 0:4, :], ACT.Copy))
                elif name == "fload":
                    after(act, "V", "mg", 1)
                    act.dma_start(frow[0:88, 0:3, :], I["ffn_conv_w"][0].rearrange("m (f c) -> f m c", c=P)).then_inc(fl_in, 16)
                    act.dma_start(frow[0:88, 3, :], I["ffn_conv_b"][0].rearrange("(f c) -> f c", c=P)).then_inc(fl_in, 16)
                    for b in range(DB):
                        act.dma_start(frow[0:88, 4 + 2 * b:6 + 2 * b, :],
                                      I["state_ffn_conv"][0, b].rearrange("r (f c) -> f r c", c=P)).then_inc(fl_in, 16)
                elif name == "fp":
                    r = k[0]
                    after(act, "P", "fp", r)
                    finish(act.activation(pF[:, :, 4 * r:4 * r + 4].rearrange("p f j -> p j f"),
                                          psB[:, r % 2, 0:4 * 88].rearrange("p (j f) -> p j f", j=4), ACT.Copy))
                else:
                    raise KeyError(x)

            def square2(p):
                act.wait_ge(add_done, 16 + p + 1)
                if p >= 2:
                    act.wait_ge(ssq2, p - 1)
                act.activation(sqb[:, p % 2], xres[:, 2 * p:2 * p + 2, :], ACT.Square).then_inc(sq2, 1)

            act.dma_start(prow[0:96, 0, :], I["gdn_conv_w"][0].rearrange("m (f c) -> (m f) c", c=P)).then_inc(prow_in, 16)
            act.dma_start(prow[96:112, 0, :], I["rms_mix_w"][0].rearrange("(f c) -> f c", c=P)).then_inc(prow_in, 16)
            act.dma_start(prow[112:128, 0, :], I["rms_ffn_w"][0].rearrange("(f c) -> f c", c=P)).then_inc(prow_in, 16)
            act.dma_start(prow[0:16, 1, :], I["final_norm_w"].rearrange("(f c) -> f c", c=P)).then_inc(prow_in, 16)
            act.dma_start(prow[16:17, 1, :], I["gdn_norm_w"]).then_inc(prow_in, 16)
            prev_rows = I["state_gdn_conv"][0].rearrange("b r (f c) -> (b r f) c", c=P)
            act.dma_start(prow[:, 2:6, :], prev_rows[0:512, :].rearrange("(r p) c -> p r c", p=P)).then_inc(prev_in, 16)
            act.dma_start(prow[0:64, 6, :], prev_rows[512:576, :]).then_inc(prev_in, 16)
            for x in SLOTS[-1, 0]:
                if x[0] == "A":
                    step(x)
                if x == ("A", "xh", 1, 3):
                    for c in range(3):
                        hi_part(c, c % RING, c // RING)
            for c in range(NC1):
                hi_part(c + 3, (c + 3) % RING, (c + 3) // RING)
                for n, (name, p) in enumerate(PAIRS[:NGA]):
                    if c - 1 == FIRST[name] + 4 * p + 3:
                        evac(n)
                    if c - 2 == FIRST[name] + 4 * p + 3 and name[0] == "g" and p < 6:
                        silu(n)
                for x in (x for r in range(PARTS) for x in SLOTS[c, r]):
                    if x[0] == "A":
                        step(x)
                if wa_pair(c - 1) is not None:
                    square2(wa_pair(c - 1))
            square2(7)
            act.wait_ge(rms_v, 1)
            act.activation(rs2[:, :], rs2[:, :], ACT.Sqrt).then_inc(xn_a, 1)
            for q in range(4):
                act.wait_ge(xn_v, q + 1)
                act.activation(xhi[:, 4 * q:4 * q + 4, :], xn[:, q % 2], ACT.Copy).then_inc(xn_h, 1)

            def f_evac(blk, r):
                n, kind = blk * 4 + r, r % 2
                act.wait_ge(mm_done, block_start(blk) + 4 * r + 4)
                if not isinstance(n, int) or n >= 2:
                    act.wait_ge(f["conv"], n - 1)
                two = psA[:, 2 * kind:2 * kind + 2, 0:TOK]
                act.activation(fue[:, kind, :, 2:2 + SEQ], two[:, :, 0:SEQ], ACT.Copy)
                for j in range(2):
                    ins = act.activation(fue[:, kind, j, 2 + SEQ:338].rearrange("p (b s) -> p b s", b=DB)[:, :, 2:10],
                                         two[:, j, SEQ:TOK].rearrange("p (b t) -> p b t", b=DB), ACT.Copy)
                ins.then_inc(f["evac"], 1)

            def f_silu(n):
                act.wait_ge(f["conv"], n + 1)
                act.activation(facc[:, 0, :, 0:336], facc[:, 0, :, 0:336], ACT.Silu).then_inc(f["silu"], 1)

            def f_hi(wv, par, pair):
                act.wait_ge(f["h"], wv + 1)
                act.activation(hhi[:, par, 2 * pair:2 * pair + 2, :], hf[:, pair], ACT.Copy).then_inc(f["hhi"], 1)

            def f_events(blk, q, par):
                if q in (4, 8, 12, 16):
                    f_evac(blk, q // 4 - 1)
                if q in (5, 13):
                    f_silu(blk * 4 + q // 4 - 1)
                if q in (10, 18):
                    f_hi(blk * 2 + (q == 18), par, int(q == 18))

            c = NC1
            for q in range(16):
                hi_part(c + q + 3, (q + 3) % RING, (c + q + 3) // RING)
                f_events(0, q, 0)
            for q in (16, 17, 18):
                f_events(0, q, 0)
            c += 16
            with act.Fori(0, NLOOP) as it:
                for t in range(48):
                    half, q = t // 24, t % 24
                    hi_part(it * 48 + (c + t + 3), (t + 3) % RING, it * 12 + (c + t + 3) // RING)
                    f_events(it * 2 + (1 + half), q, (1 + half) % 2)
            c += 48 * NLOOP
            def new_rows_out(r):
                m_ = min(4, 18 - 4 * r)
                act.wait_ge(fin["nt"], r + 1)
                act.activation(frow[0:88, 4 * r:4 * r + m_, :],
                               psA[0:88, r % 4, 0:m_ * P].rearrange("p (j c) -> p j c", j=m_), ACT.Copy).then_inc(fin["ne"], 1)

            def last_square(p):
                act.wait_ge(f["add"], 8 * (NB - 1) + p + 3)
                if p >= 2:
                    act.wait_ge(fin["ss"], p - 1)
                act.activation(sqb[:, p % 2], xres[:, 2 * p:2 * p + 2, :], ACT.Square).then_inc(fin["sq"], 1)

            def rows_of_y(q):
                for t in range(3):
                    n, c0 = unit(t)
                    act.wait_ge(fin["t"], 3 * q + t + 1)
                    act.activation(yo[0:n, t, 512 * q:512 * q + 512], psA[0:n, t, :], ACT.Copy).then_inc(fin["ev"], 1)

            for d in range(3, 8):
                hi_part(c + d, d % RING, (c + d) // RING)
                if d == 3:
                    for r in range(4):
                        new_rows_out(r)
                elif d == 4:
                    new_rows_out(4)
                elif d < 7:
                    last_square(d - 5)
            rows_of_y(0)
            for q in range(1, 4):
                if q == 1:
                    last_square(2)
                last_square(2 * q + 1)
                if q < 3:
                    last_square(2 * q + 2)
                rows_of_y(q)
            act.wait_ge(fin["r"], 1)
            act.wait_ge(fin["ev"], 12)
            act.activation(yo[:, 1, :], yo[:, 1, :], ACT.Copy, scale=sm("rsx", P, 1, 2)).then_inc(fin["y1"], 1)
        @block.vector
        def _(dve):
            def finish(ins):
                ins.then_inc(done["V"], 1)

            def chain(ins):
                link(dve, "V", ins)

            def tt(out, a_, b_, op):
                return dve.tensor_tensor(out, a_, b_, op)

            def lo_part(c, slot):
                dve.wait_ge(hi_done, c + 1)
                dve.tensor_tensor(wlo[:, slot], raw[:, slot], whi[:, slot].bitcast(F32), ALU.subtract).then_inc(lo_done, 1)

            def conv(n):
                name, p = PAIRS[n]
                kind, h = tile_of(name, p, 0)
                g = int(name[1])
                gp = g * 6 + p
                ft = kind * 8 + g * 4 + h
                dve.wait_ge(evac_done, n + 1)
                dve.wait_ge(pads_done, gp + 2)
                if gp >= 1:
                    dve.wait_ge(silu_done, gp)
                for tap in range(4):
                    for j in range(2):
                        wcol = pT[:, tap * 24 + ft + j:tap * 24 + ft + j + 1]
                        u = ue[:, j, tap:tap + 344]
                        if tap == 0:
                            ins = dve.tensor_scalar(acc[:, j, 0:344], u, wcol, None, ALU.mult)
                        else:
                            ins = dve.scalar_tensor_tensor(out=acc[:, j, 0:344], in0=u, scalar=wcol, in1=acc[:, j, 0:344],
                                                           op0=ALU.mult, op1=ALU.add)
                    if tap < 3:
                        chain(ins)
                ins.then_inc(conv_done, 1)

            def add_pair(m_):
                n = NGA + m_
                name, p = PAIRS[n]
                dve.wait_ge(mm_done, FIRST[name] + PER[name] * (p + 1))
                bank = 2 * (n % 2)
                x = xres[:, 2 * p:2 * p + 2, :]
                tt(x, psA[:, bank:bank + 2, 0:TOK], x, ALU.add).then_inc(add_done, 1)

            def step(x):
                name, k = x[1], x[2:]
                if name == "init":
                    chain(dve.memset(small[:, :], 0.0))
                    finish(dve.memset(sm("mh"), -0.5))
                elif name == "rows":
                    after(dve, "P", "rows")
                    finish(dve.tensor_copy(pT[:, 0:145], b0[:, 0:145]))
                elif name == "ms":
                    t = k[0]
                    n = unit(t)[0]
                    after(dve, "A", "sq", t)
                    finish(dve.tensor_scalar(sm("rsx", n, t, t + 1), sm("ssx", n, t, t + 1), 1.0 / DM, EPS, ALU.mult, ALU.add))
                elif name == "xs":
                    t = k[0]
                    n = unit(t)[0]
                    after(dve, "G", "rs", t)
                    if t == 2:
                        after(dve, "P", "xt", 0, 3)
                    finish(dve.tensor_scalar(xs[0:n, t % 2], xraw[0:n, t], sm("rsx", n, t, t + 1), None, ALU.mult))
                elif name == "xw":
                    t, q = k
                    n, _ = unit(t)
                    after(dve, "P", "xt", t, q)
                    i = 4 * t + q
                    if i == 0:
                        after(dve, "V", "rows")
                    if i >= 2:
                        after(dve, "V", "xl", (i - 2) // 4, (i - 2) % 4)
                    finish(tt(tmpx[:, q % 2, :, 0:n], heads(psA[:, q, :], n), over_free(pT[:, 96 + 4 * q:100 + 4 * q], n), ALU.mult))
                elif name == "xl":
                    t, q = k
                    n, c0 = unit(t)
                    after(dve, "A", "xh", t, q)
                    finish(tt(xlo[:, 4 * q:4 * q + 4, c0:c0 + n], tmpx[:, q % 2, :, 0:n],
                              xhi[:, 4 * q:4 * q + 4, c0:c0 + n].bitcast(F32), ALU.subtract))
                elif name == "wab":
                    dve.wait_ge(ab_in, 16)
                    flat = wab[:, :, :].rearrange("p k c -> p (k c)")
                    dve.memset(wabh[:, 256:368].bitcast(F32), 0.0)
                    dve.memset(wabl[:, 256:368].bitcast(F32), 0.0)
                    chain(dve.tensor_copy(wabh[:, 0:256], flat))
                    finish(tt(wabl[:, 0:256], flat, wabh[:, 0:256].bitcast(F32), ALU.subtract))
                elif name == "sc1":
                    after(dve, "P", "abt")
                    after(dve, "A", "alog")
                    dve.tensor_copy(sm("ab", P, 0, 32), b1[:, 0:32])
                    chain(dve.tensor_copy(sm("ab", NS, 32, 48), b1[0:NS, 32:48]))
                    chain(tt(sm("sa").rearrange("p (u h) -> p u h", u=3),
                             sm("ab").rearrange("p (u c) -> p u c", u=3)[:, :, 0:8], over_heads(sm("dtb"), 3), ALU.add))
                    finish(dve.scalar_tensor_tensor(out=sm("sb"), in0=sm("sa"), scalar=-1.0, in1=sm("sa"),
                                                    op0=ALU.mult, op1=ALU.max))
                elif name == "sc3":
                    after(dve, "A", "sc2")
                    chain(dve.scalar_tensor_tensor(out=sm("sa"), in0=sm("sa"), scalar=0.0, in1=sm("sb"),
                                                   op0=ALU.max, op1=ALU.add))
                    chain(dve.scalar_tensor_tensor(out=sm("g").rearrange("p (u h) -> p u h", u=3),
                                                   in0=sm("sa").rearrange("p (u h) -> p u h", u=3), scalar=-1.0,
                                                   in1=over_heads(sm("alog"), 3), op0=ALU.mult, op1=ALU.mult))
                    chain(dve.tensor_scalar(sm("tmp"), sm("tmp"), 1.0, None, ALU.add))
                    dve.reciprocal(sm("beta"), sm("tmp"))
                    finish(tt(sm("gm", NS).rearrange("p (h b) -> p h b", h=8), over_free(sm("g", NS, 16, 24), DB),
                              over_heads(C("batch", NS), 8), ALU.mult))
                elif name == "sc4":
                    after(dve, "P", "cum")
                    dve.tensor_copy(sm("cg", P, 0, 16), b2[:, 0:16])
                    chain(dve.tensor_copy(sm("cg", NS, 16, 24), b2[0:NS, 16:24]))
                    tt(sm("nkd", P, 0, 16), b2[:, 24:40], sm("cg", P, 0, 16), ALU.subtract)
                    finish(tt(sm("nkd", NS, 16, 24), b2[0:NS, 40:48], sm("cg", NS, 16, 24), ALU.subtract))
                elif name == "ss":
                    g, u = k
                    n, _ = unit(u)
                    after(dve, "A", "qs", g, u)
                    dve.tensor_reduce(sm("ss", n, 0, 4), xt[0:n, :, :], AX.X, ALU.add)
                    chain(dve.tensor_reduce(sm("ss", n, 4, 8), xx[0:n, :, :], AX.X, ALU.add))
                    finish(dve.tensor_scalar(sm("rn", n), sm("ss", n), EPS, None, ALU.add))
                elif name == "bv":
                    g, u = k
                    n, _ = unit(u)
                    after(dve, "P", "tr" if u else "tv", g, u)
                    finish(tt(bv[0:n, :, :], heads((b2 if u else b3)[0:n], P), over_free(per_head("beta", n, u, g), P), ALU.mult))
                elif name == "sc":
                    g, u = k
                    n, _ = unit(u)
                    after(dve, "G", "rn", g, u)
                    after(dve, "A", "cp", g, u)
                    F = lambda i: sm("f", n, 4 * i, 4 * i + 4)
                    rk = sm("rn", n, 4, 8)
                    dve.tensor_scalar(F(0), sm("rn", n, 0, 4), SCALE, None, ALU.mult)
                    tt(F(3), rk, per_head("beta", n, u, g), ALU.mult)
                    chain(tt(F(5), rk, per_head("kd", n, u, g), ALU.mult))
                    tt(F(1), F(0), per_head("eg", n, u, g), ALU.mult)
                    chain(dve.scalar_tensor_tensor(out=F(4), in0=F(3), scalar=-1.0, in1=per_head("eg", n, u, g),
                                                   op0=ALU.mult, op1=ALU.mult))
                    tt(pp[0:n, :, :], tq[0:n, :, :], over_free(F(0), P), ALU.mult)
                    finish(tt(xx[0:n, :, :], tk[0:n, :, :], over_free(rk, P), ALU.mult))
                elif name == "sb":
                    g, u = k
                    n, _ = unit(u)
                    F = lambda i: sm("f", n, 4 * i, 4 * i + 4)
                    if u:
                        tt(at_[0:n, :, :], tk[0:n, :, :], over_free(F(4), P), ALU.mult)
                    finish(tt(xt[0:n, :, :], tk[0:n, :, :], over_free(F(3), P), ALU.mult))
                elif name == "sk":
                    g, u = k
                    n, _ = unit(u)
                    F = lambda i: sm("f", n, 4 * i, 4 * i + 4)
                    if u:
                        tt(tq[0:n, :, :], tq[0:n, :, :], over_free(F(1), P), ALU.mult)
                    finish(tt(tk[0:n, :, :], tk[0:n, :, :], over_free(F(5), P), ALU.mult))
                elif name == "tb1":
                    g, u = k
                    n, c0 = unit(u)
                    after(dve, "P", "tb1", g, u)
                    ins = dve.tensor_copy(kb[:, :, 0:n], heads(b2, n))
                    if u:
                        ins = dve.tensor_copy(reg[g][:, 8:12, c0:c0 + n], heads(b3, n))
                    finish(ins)
                elif name == "gt":
                    g, u = k
                    n, _ = unit(u)
                    after(dve, *before_unit(g, u))
                    finish(tt(dec[0:n, :, 0:n], over_heads(C("upto" if u < 2 else "upto8", n, n), 4),
                              over_free(per_head("g", n, u, g), n), ALU.mult))
                elif name == "dm":
                    g, u = k
                    n, _ = unit(u)
                    after(dve, "P", "cg", g, u)
                    chain(tt(dec[0:n, :, 0:n], heads(b3[0:n], n), over_free(per_head("cg", n, u, g), n), ALU.subtract))
                    finish(dve.scalar_tensor_tensor(out=dec[0:n, :, 0:n], in0=dec[0:n, :, 0:n], scalar=0.0,
                                                    in1=over_heads(C("negP" if u < 2 else "neg8", n, n), 4),
                                                    op0=ALU.min, op1=ALU.add))
                elif name == "kk":
                    g, u = k
                    n, _ = unit(u)
                    after(dve, "P", "kk", g, u)
                    after(dve, "A", "de", g, u)
                    chain(tt(at_[0:n, :, 0:n], heads(b2[0:n], n), dec[0:n, :, 0:n], ALU.mult))
                    chain(tt(pp[0:n, :, 0:n], at_[0:n, :, 0:n], over_heads(C("lev1", n, n), 4), ALU.mult))
                    tt(qk[0:n, :, 0:n], heads(b3[0:n], n), dec[0:n, :, 0:n], ALU.mult)
                    finish(tt(xt[0:n, :, 0:n], over_heads(C("ident", n, n), 4), pp[0:n, :, 0:n], ALU.subtract))
                elif name in ("dx", "dt"):
                    g, u, l = k
                    n, _ = unit(u)
                    after(dve, "P", name, g, u, l)
                    dst, bank = (xx, b1) if name == "dx" else (xt, b2)
                    finish(tt(dst[0:n, :, 0:n], dst[0:n, :, 0:n], heads(bank[0:n], n), ALU.subtract))
                elif name == "ks":
                    g, u = k
                    n, _ = unit(u)
                    after(dve, "P", "ks", g, u)
                    finish(tt(bv[0:n, :, :], heads((b0 if u == 1 else b1)[0:n], P), bv[0:n, :, :], ALU.add))
                elif name == "st":
                    g, u = k
                    after(dve, "P", "os", g, u)
                    if u == 0:
                        if g == 1:
                            dve.wait_ge(st_out, 16)
                        finish(dve.tensor_copy(S[:, :, :], heads(b3, P)))
                    else:
                        a0 = u * 8 + g * 4
                        chain(tt(S[:, :, :], S[:, :, :], over_free(sm("eglP", P, a0, a0 + 4), P), ALU.mult))
                        finish(tt(S[:, :, :], heads(b3, P), S[:, :, :], ALU.add))
                elif name == "o1":
                    n = unit(k[1])[0]
                    after(dve, "A", "o", *k)
                    chain(dve.tensor_reduce(sm("so", n), qk[0:n, :, :], AX.X, ALU.add))
                    finish(dve.tensor_scalar(sm("ro", n), sm("so", n), 1.0 / P, EPS, ALU.mult, ALU.add))
                elif name == "o2":
                    n = unit(k[1])[0]
                    after(dve, "G", "or", *k)
                    finish(tt(bv[0:n, :, :], bv[0:n, :, :], over_free(sm("ro", n), P), ALU.mult))
                elif name == "oz":
                    g, u = k
                    n, c0 = unit(u)
                    after(dve, "P", "ot", g, u)
                    dve.wait_ge(evac_done, 8 * (g + 1))
                    z = zz[:, 4 * g:4 * g + 4, c0:c0 + n]
                    finish(dve.scalar_tensor_tensor(out=z, in0=heads(b3, n), scalar=pT[:, 144:145], in1=z,
                                                    op0=ALU.mult, op1=ALU.mult))
                elif name == "um":
                    g, h = k
                    if h == 0:
                        after(dve, "A", "o", g, 2)
                    else:
                        after(dve, "P", "us", g, h - 1)
                    finish(tt(umask[0:NS, :, :], over_heads(ub[0:NS, h, :], DB), over_free(C("batch", NS), P), ALU.mult))
                elif name == "us":
                    g, h = k
                    after(dve, "P", "us", g, h)
                    dve.wait_ge(s_in[h % 2], 16 * (4 * g + 2 + h // 2 + 1))
                    a0 = (4 * g + h) * DB
                    st_ = ssm[:, h % 2]
                    chain(tt(st_, st_, over_free(sm("eglS", P, a0, a0 + DB), P), ALU.mult))
                    bank = h % 2 * 2
                    finish(tt(st_, psB[:, bank:bank + 2, :].rearrange("p k (b e) -> p (k b) e", b=4), st_, ALU.add))
                elif name == "hk":
                    g = k[0]
                    after(dve, "P", "hk", g)
                    chain(dve.tensor_copy(bm[:, :, :], psB[:, 2:4, :].rearrange("p k (h x) -> p (k h) x", h=2)))
                    if g == 0:
                        dve.memset(bs[:, 0:2 * P], 0.0)
                        dve.memset(bs[:, 2 * P:], NEG)
                    chain(tt(bm[:, :, P:2 * P], bm[:, :, P:2 * P], over_heads(C("causal"), 4), ALU.add))
                    for h in range(4):
                        row = bs[32 * h:32 * h + DT]
                        dve.tensor_copy(row[:, 0:P], bm[0:DT, h, 0:1].broadcast_to([DT, P]))
                        dve.tensor_copy(row[:, P:2 * P], bm[0:DT, h, 0:P])
                        ins = dve.tensor_copy(row[:, 2 * P + 56:2 * P + 64], bm[0:DT, h, P:P + DT])
                    finish(ins)
                elif name == "S":
                    g, h = k
                    after(dve, "P", "S", g, h)
                    s_ = sc[:, h % 2]
                    b_ = psB[:, h % 2, :]
                    if h == 0:
                        after(dve, "V", "hk", g)
                    dve.scalar_tensor_tensor(out=s_[:, 0:256], in0=b_[:, 0:256], scalar=SCALE, in1=bm[:, h, :],
                                             op0=ALU.mult, op1=ALU.add)
                    chain(dve.scalar_tensor_tensor(out=s_[:, 256:384], in0=b_[:, 256:384], scalar=SCALE,
                                                   in1=bm[:, h, P:2 * P], op0=ALU.mult, op1=ALU.add))
                    dve.tensor_reduce(ast[:, h % 2, 0:1], s_[:, 0:256], AX.X, ALU.max, negate=True)
                    finish(dve.tensor_reduce(ast[:, h % 2, 1:2], s_[:, 256:384], AX.X, ALU.max, negate=True))
                elif name == "N":
                    g, h = k
                    s_ = sc[:, h % 2]
                    after(dve, "A", "E", g, h)
                    r_ = ast[:, h % 2]
                    chain(dve.reciprocal(r_[:, 4:6], r_[:, 2:4]))
                    dve.tensor_scalar(s_[:, 0:256], s_[:, 0:256], r_[:, 4:5], None, ALU.mult)
                    finish(dve.tensor_scalar(s_[:, 256:384], s_[:, 256:384], r_[:, 5:6], None, ALU.mult))
                elif name == "kt":
                    after(dve, "P", "kt", *k)
                    finish(dve.tensor_copy(ktp[:, :, P:2 * P], heads(b1, P)))
                elif name == "SS":
                    g, b = k
                    after(dve, "P", "SS", g, b)
                    o_ = 2 * P + 56 - DT * b
                    dve.scalar_tensor_tensor(out=sc[:, 0, 0:256], in0=b2[:, 0:256], scalar=SCALE, in1=bs[:, 0:256],
                                             op0=ALU.mult, op1=ALU.add)
                    chain(dve.scalar_tensor_tensor(out=sc[:, 0, 256:TOK], in0=b2[:, 256:TOK], scalar=SCALE,
                                                   in1=bs[:, o_:o_ + NS], op0=ALU.mult, op1=ALU.add))
                    finish(dve.tensor_reduce(ast[:, 0, 0:1], sc[:, 0, 0:TOK], AX.X, ALU.max, negate=True))
                elif name == "SN":
                    after(dve, "A", "SE", *k)
                    chain(dve.reciprocal(ast[:, 0, 4:5], ast[:, 0, 2:3]))
                    finish(dve.tensor_scalar(sc[:, 0, 0:TOK], sc[:, 0, 0:TOK], ast[:, 0, 4:5], None, ALU.mult))
                elif name in ("mg", "ma"):
                    g = k[0]
                    after(dve, "A", name, g)
                    src, k0 = (zz[:, 4 * g:4 * g + 4, :], 8 + 4 * g) if name == "mg" else (reg[g][:, 0:4, :], 4 * g)
                    finish(tt(xlo[:, k0:k0 + 4, :], src, xhi[:, k0:k0 + 4, :].bitcast(F32), ALU.subtract))
                else:
                    raise KeyError(x)

            for x in SLOTS[-1, 0]:
                if x[0] == "V":
                    step(x)
                if x == ("V", "xl", 1, 3):
                    for c in range(3):
                        lo_part(c, c % RING)
            for c in range(NC1):
                lo_part(c + 3, (c + 3) % RING)
                for n, (name, p) in enumerate(PAIRS):
                    if c == FIRST[name] + PER[name] * (p + 1):
                        if n >= NGA:
                            add_pair(n - NGA)
                        elif name[0] == "g" and p < 6:
                            conv(n)
                for x in (x for r in range(PARTS) for x in SLOTS[c, r]):
                    if x[0] == "V":
                        step(x)
            add_pair(len(PAIRS) - NGA - 1)
            dve.wait_ge(ssq2, 8)
            dve.tensor_scalar(rs2[:, :], b3[:, 0:TOK], 1.0 / DM, EPS, ALU.mult, ALU.add).then_inc(rms_v, 1)
            dve.wait_ge(xn_a, 1)
            chain(dve.reciprocal(rs2[:, :], rs2[:, :]))
            for q in range(5):
                if q < 4:
                    for j in range(4):
                        kk_ = 4 * q + j
                        ins = dve.scalar_tensor_tensor(out=xn[:, q % 2, j, :], in0=xres[:, kk_, :],
                                                       scalar=pT[:, 112 + kk_:113 + kk_], in1=rs2[:, :], op0=ALU.mult, op1=ALU.mult)
                    ins.then_inc(xn_v, 1)
                if q:
                    dve.wait_ge(xn_h, q)
                    tt(xlo[:, 4 * q - 4:4 * q, :], xn[:, (q - 1) % 2], xhi[:, 4 * q - 4:4 * q, :].bitcast(F32),
                       ALU.subtract).then_inc(xn_l, 1)
                    dve.wait_ge(xn_l, q)

            def stage(blk, par):
                if isinstance(blk, int):
                    after(dve, "A", "fp", 4)
                else:
                    dve.wait_ge(f["pad"], blk * 4 + 1)
                for kind in range(2):
                    ins = dve.tensor_scalar(fst[:, par, kind, :, :], pF[:, bass.DynSlice(blk * 4 + kind * FT, 4), :],
                                            1.0, None, ALU.mult)
                ins.then_inc(f["stage"], 1)
                dve.wait_ge(f["stage"], blk + 1)

            def f_conv(blk, r, par):
                n = blk * 4 + r
                kind = r % 2
                dve.wait_ge(f["evac"], n + 1)
                dve.wait_ge(f["pad"], n + 2)
                ft = blk * 4 + (kind * FT + r // 2 * 2)
                dve.tensor_scalar(fnewT[:, bass.DynSlice(ft, 2), 0:2], fue[:, kind, :, SEQ:SEQ + 2], 1.0, None, ALU.mult)
                dve.tensor_scalar(fnewT[:, bass.DynSlice(ft, 2), 2:18].rearrange("p f (b r) -> p f b r", b=DB),
                                  fue[:, kind, :, 2 + SEQ:338].rearrange("p j (b s) -> p j b s", b=DB)[:, :, :, 8:10],
                                  1.0, None, ALU.mult)
                for tap in (2, 1, 0):
                    for j in range(2):
                        w_ = lambda i: fst[:, par, kind, r // 2 * 2 + j, i:i + 1]
                        u = fue[:, kind, j, tap:tap + 336]
                        if tap == 2:
                            ins = dve.tensor_scalar(facc[:, kind, j, 0:336], u, w_(2), w_(3), ALU.mult, ALU.add)
                        else:
                            ins = dve.scalar_tensor_tensor(out=facc[:, kind, j, 0:336], in0=u, scalar=w_(tap),
                                                           in1=facc[:, kind, j, 0:336], op0=ALU.mult, op1=ALU.add)
                    if tap:
                        ins.then_inc(f["tap"], 1)
                        dve.wait_ge(f["tap"], n * 2 + (3 - tap))
                ins.then_inc(f["conv"], 1)

            def f_hidden(blk, r):
                wv = blk * 2 + r // 2
                dve.wait_ge(f["silu"], wv + 1)
                dve.wait_ge(f["conv"], blk * 4 + r + 1)
                if not isinstance(wv, int) or wv >= 2:
                    dve.wait_ge(f["hhi"], wv - 1)
                tt(hf[:, r // 2, :, 0:SEQ], facc[:, 0, :, 0:SEQ], facc[:, 1, :, 0:SEQ], ALU.mult)
                for j in range(2):
                    ins = tt(hf[:, r // 2, j, SEQ:TOK].rearrange("p (b t) -> p b t", b=DB), f_sample(0, j), f_sample(1, j), ALU.mult)
                ins.then_inc(f["h"], 1)

            def f_lo(blk, r, par):
                dve.wait_ge(f["hhi"], blk * 2 + r // 2 + 1)
                lo_, hi_ = r - 1, r + 1
                tt(hlo[:, par, lo_:hi_, :], hf[:, r // 2], hhi[:, par, lo_:hi_, :].bitcast(F32), ALU.subtract).then_inc(f["hlo"], 1)

            def f_add(blk, d):
                dve.wait_ge(mm_done, down_start(blk) + d + 1)
                x = xres[:, 2 * d:2 * d + 2, :]
                bank = 2 * (d % 2)
                tt(x, psB[:, bank:bank + 2, 0:TOK], x, ALU.add).then_inc(f["add"], 1)

            def f_events(blk, q, par):
                if q == 0:
                    stage(blk, par)
                if q in (4, 8, 12, 16):
                    f_conv(blk, q // 4 - 1, par)
                if q in (9, 17):
                    f_hidden(blk, q // 4 - 1)
                if q in (10, 18):
                    f_lo(blk, q // 4 - 1, par)

            dve.memset(small[0:1, 0:1], 0.0).then_inc(f["add"], 2)
            c = NC1
            for q in range(16):
                lo_part(c + q + 3, (q + 3) % RING)
                f_events(0, q, 0)
            for q in (16, 17, 18):
                f_events(0, q, 0)
            c += 16
            with dve.Fori(0, NLOOP) as it:
                for t in range(48):
                    half, q = t // 24, t % 24
                    blk = it * 2 + (1 + half)
                    lo_part(it * 48 + (c + t + 3), (t + 3) % RING)
                    if q >= 17:
                        f_add(blk - 1, q - 17)
                    f_events(blk, q, (1 + half) % 2)
                    if t in (23, 47):
                        f_add(blk - 1, 7)
            c += 48 * NLOOP
            def weigh(p):
                dve.wait_ge(f["add"], 8 * (NB - 1) + p + 3)
                if p >= 4:
                    dve.wait_ge(fin["t"], 3 * ((p - 4) // 2 + 1))
                for j in range(2):
                    kk_ = 2 * p + j
                    ins = dve.tensor_scalar(xn[:, p // 2 % 2, 2 * (p % 2) + j, :], xres[:, kk_, :],
                                            pT[:, 128 + kk_:129 + kk_], None, ALU.mult)
                ins.then_inc(fin["w"], 1)

            for d in range(8):
                if d + 3 < 8:
                    lo_part(c + d + 3, (d + 3) % RING)
                if d:
                    f_add(NB - 1, d - 1)
                    weigh(d - 1)
            f_add(NB - 1, 7)
            weigh(7)
            dve.wait_ge(fin["ss"], 8)
            dve.tensor_scalar(rs2[0:1, :], psA[0:1, 3, 0:TOK], 1.0 / DM, EPS, ALU.mult, ALU.add).then_inc(fin["ms"], 1)
            dve.wait_ge(fin["mt"], 1)
            dve.tensor_copy(sm("ssx", P, 0, 2), b0[:, 0:2])
            dve.tensor_copy(sm("ssx", NS, 2, 3), b0[0:NS, 2:3]).then_inc(fin["mr"], 1)
            dve.wait_ge(fin["r"], 1)
            dve.wait_ge(fin["ev"], 12)
            for t in (0, 2):
                n = unit(t)[0]
                dve.tensor_scalar(yo[0:n, t, :], yo[0:n, t, :], sm("rsx", n, t, t + 1), None, ALU.mult).then_inc(fin["y0"], 1)

        @block.tensor
        def _(pe):
            def finish(ins):
                ins.then_inc(done["P"], 1)

            def products(c, slot, out_bank, k0, first, last, rhs_hi, rhs_lo, between=lambda r: None):
                pe.wait_ge(lo_done, c + 1)
                for j in range(2):
                    o = out_bank[:, j, 0:TOK]
                    for kk_ in range(CQ):
                        hi = whi[:, slot, kk_, j * P:(j + 1) * P]
                        lo = wlo[:, slot, kk_, j * P:(j + 1) * P]
                        pe.matmul(o, hi, rhs_hi[:, k0 + kk_, :], start=first and kk_ == 0, stop=False)
                        pe.matmul(o, hi, rhs_lo[:, k0 + kk_, :], start=False, stop=False)
                        ins = pe.matmul(o, lo, rhs_hi[:, k0 + kk_, :], start=False, stop=last and kk_ == CQ - 1)
                        done_ = CQ * j + kk_ + 1
                        if done_ % (2 * CQ // PARTS) == 0 and done_ < 2 * CQ:
                            between(done_ * PARTS // (2 * CQ) - 1)
                ins.then_inc(mm_done, 1)
                between(PARTS - 1)

            def project(c):
                name, p, q, per = CHUNKS[c]
                n = pair_index(name, p)
                if q == 0:
                    if n >= 2:
                        if n - 2 < NGA:
                            pe.wait_ge(evac_done, n - 1)
                        else:
                            pe.wait_ge(add_done, n - 1 - NGA)
                    else:
                        after(pe, "V", "xl", 2, 3)
                    if name in ("wa0", "wa1") and p == 0:
                        after(pe, "V", "ma", int(name[2]))
                if name == "wg" and p == 0:
                    after(pe, "V", "mg", q)
                k0 = (q + OUT_ROWS.get(name, 0)) * CQ
                bank = 2 * (n % 2)
                products(c, c % RING, psA[:, bank:bank + 2, :], k0, q == 0, q == per - 1, xhi, xlo, lambda r: quarter(c, r))

            def quarter(c, r):
                for x in SLOTS[c, r]:
                    if x[0] == "P":
                        step(x)

            def turn(out, in_, n):
                return pe.transpose(out, in_, C("ident", n, n))

            def sum_squares(p):
                pe.wait_ge(sq2, p + 1)
                for j in range(2):
                    ins = pe.matmul(b3[:, 0:TOK], C("ones"), sqb[:, p % 2, j, :], start=(p == 0 and j == 0), stop=(p == 7 and j == 1))
                ins.then_inc(ssq2, 1)

            def step(x):
                name, k = x[1], x[2:]
                if name == "rows":
                    pe.wait_ge(ident_in, 16)
                    pe.wait_ge(prow_in, 16 * 5)
                    turn(b0[:, 0:P], prow[:, 0, :], P)
                    finish(turn(b0[:, P:P + 17], prow[0:17, 1, :], 17))
                elif name == "prev":
                    pe.wait_ge(prev_in, 16 * 2)
                    for r in range(4):
                        turn(b1[:, r * P:(r + 1) * P], prow[:, 2 + r, :], P)
                    finish(turn(b2[:, 0:64], prow[0:64, 6, :], 64))
                elif name == "rb":
                    pe.wait_ge(consts_in, 16)
                    pe.wait_ge(rows_in, 16 * NROWS)
                    finish(pe.matmul(b3[0:NH, 0:3 * P], sm("rb", NBK), C("bucket", NBK), start=True, stop=True))
                elif name == "xt":
                    t, q = k
                    n, _ = unit(t)
                    after(pe, "V", "xs", t)
                    if t >= 1:
                        after(pe, "V", "xw", t - 1, q)
                    for j in range(4):
                        ins = turn(psA[:, q, j * n:(j + 1) * n], xs[0:n, t % 2, (4 * q + j) * P:(4 * q + j + 1) * P], n)
                    finish(ins)
                elif name == "rt":
                    t, q = k
                    n, _ = unit(t)
                    if (t, q) == (0, 0):
                        after(pe, "A", "rb")
                    else:
                        after(pe, "A", "rt", *((t, q - 1) if q else (t - 1, 3)))
                    for j in range(4):
                        ins = turn(b3[:, j * n:(j + 1) * n], xraw[0:n, t, (4 * q + j) * P:(4 * q + j + 1) * P], n)
                    finish(ins)
                elif name == "ab":
                    after(pe, "V", "wab")
                    after(pe, "V", "rows")
                    for kk_ in range(KT):
                        hi, lo = (w_[:, kk_ * 16:kk_ * 16 + P] for w_ in (wabh, wabl))
                        pe.matmul(b0[:, 0:TOK], hi, xhi[:, kk_, :], start=kk_ == 0, stop=False)
                        pe.matmul(b0[:, 0:TOK], hi, xlo[:, kk_, :], start=False, stop=False)
                        ins = pe.matmul(b0[:, 0:TOK], lo, xhi[:, kk_, :], start=False, stop=kk_ == KT - 1)
                    finish(ins)
                elif name == "abt":
                    after(pe, "A", "ab")
                    after(pe, "A", "prev")
                    for u in range(3):
                        n, c0 = unit(u)
                        ins = pe.transpose(b1[0:n, 16 * u:16 * u + 16], abT[0:16, c0:c0 + n], C("ident", 16, 16))
                    finish(ins)
                elif name == "cum":
                    after(pe, "V", "sc3")
                    for u in range(2):
                        gg = sm("g", P, 8 * u, 8 * u + 8)
                        pe.matmul(b2[:, 8 * u:8 * u + 8], C("upto"), gg, start=True, stop=True)
                        pe.matmul(b2[:, 24 + 8 * u:32 + 8 * u], C("ones"), gg, start=True, stop=True)
                    gg = sm("g", NS, 16, 24)
                    pe.matmul(b2[0:NS, 16:24], C("upto8", NS, NS), gg, start=True, stop=True)
                    pe.matmul(b2[0:NS, 40:48], C("same8", NS, NS), gg, start=True, stop=True)
                    finish(pe.matmul(b2[:, 64:128], C("ones", NS), sm("gm", NS), start=True, stop=True))
                elif name == "tr":
                    g, u = k
                    n, c0 = unit(u)
                    pe.wait_ge(silu_done, 6 * g + (6 if u else 4))
                    after(pe, "A", "sc5")
                    after(pe, *before_unit(g, u))
                    for kind, bank in enumerate((b0, b1, b2)[:3 if u else 2]):
                        for h in range(4):
                            ins = turn(bank[0:n, h * P:(h + 1) * P], reg[g][:, 4 * kind + h, c0:c0 + n], P)
                    finish(ins)
                elif name == "tv":
                    g, u = k
                    n, c0 = unit(u)
                    pe.wait_ge(silu_done, 6 * g + 6)
                    after(pe, "V", "kk", g, u)
                    for h in range(4):
                        ins = turn(b3[0:n, h * P:(h + 1) * P], reg[g][:, 8 + h, c0:c0 + n], P)
                    finish(ins)
                elif name == "tq":
                    g, u = k
                    n, c0 = unit(u)
                    after(pe, "V", "sc", g, u)
                    for src, bank in ((pp, b0), (xx, b1)):
                        for h in range(4):
                            ins = turn(bank[:, h * n:(h + 1) * n], src[0:n, h, :], n)
                    finish(ins)
                elif name == "tb1":
                    g, u = k
                    n, c0 = unit(u)
                    after(pe, "V", "sb", g, u)
                    for src, bank in ((xt, b2), (at_, b3))[:2 if u else 1]:
                        for h in range(4):
                            ins = turn(bank[:, h * n:(h + 1) * n], src[0:n, h, :], n)
                    finish(ins)
                elif name == "tb2":
                    g, u = k
                    n, c0 = unit(u)
                    after(pe, "A", "tb1", g, u)
                    after(pe, "V", "sk", g, u)
                    for h in range(4):
                        ins = turn(b0[:, h * n:(h + 1) * n], tq[0:n, h, :], n)
                    finish(ins)
                elif name == "cg":
                    g, u = k
                    n = unit(u)[0]
                    after(pe, "V", "gt", *k)
                    if u:
                        after(pe, "V", "oz", g, u - 1)
                    finish(pe.matmul(heads(b3[0:n], n), C("ones", n, n), dec[0:n, :, 0:n], start=True, stop=True))
                elif name == "kk":
                    g, u = k
                    n, c0 = unit(u)
                    after(pe, "V", "tb1", g, u)
                    after(pe, "A", "tb1", g, u)
                    for h in range(4):
                        kT_ = reg[g][:, 4 + h, c0:c0 + n]
                        pe.matmul(b2[0:n, h * n:(h + 1) * n], kT_, kb[:, h, 0:n], start=True, stop=True)
                        ins = pe.matmul(b3[0:n, h * n:(h + 1) * n], kT_, qn[:, h, 0:n], start=True, stop=True)
                    finish(ins)
                elif name == "x1":
                    n = unit(k[1])[0]
                    after(pe, "V", "kk", *k)
                    after(pe, "A", *(("tb2", *k) if k[1] else ("tb1", *k)))
                    for h in range(4):
                        ins = turn(b0[0:n, h * n:(h + 1) * n], xt[0:n, h, 0:n], n)
                    finish(ins)
                elif name == "pl":
                    g, u, l = k
                    n = unit(u)[0]
                    after(pe, *(("A", "x1", g, u) if l == 2 else ("V", "dx", g, u, l // 2)))
                    after(pe, "G", "mk", g, u, l)
                    for h in range(4):
                        ins = pe.matmul(b0[0:n, h * n:(h + 1) * n], dec[0:n, h, 0:n], xx[0:n, h, 0:n], start=True, stop=True)
                    finish(ins)
                elif name in ("dx", "dt"):
                    g, u, l = k
                    n = unit(u)[0]
                    after(pe, "A", "pl", g, u, l)
                    after(pe, "V", *(("dt", g, u, l // 2) if l > 2 else ("kk", g, u)))
                    left, right, bank = (xt, pp, b1) if name == "dx" else (pp, xt, b2)
                    for h in range(4):
                        ins = pe.matmul(bank[0:n, h * n:(h + 1) * n], left[0:n, h, 0:n], right[0:n, h, 0:n], start=True, stop=True)
                    finish(ins)
                elif name == "ks":
                    g, u = k
                    n, c0 = unit(u)
                    if u == 1:
                        after(pe, "V", "st", g, 0)
                        after(pe, "V", "dt", g, u, 64)
                    else:
                        after(pe, "A", "sh", g, 0)
                        after(pe, "V", "dt", g, u, 4)
                    for h in range(4):
                        if u == 1:
                            ins = pe.matmul(b0[:, h * P:(h + 1) * P], reg[g][:, 8 + h, c0:c0 + n], S[:, h, :], start=True, stop=True)
                        else:
                            ins = pe.matmul(b1[0:n, h * P:(h + 1) * P], pp[:, h, NS:2 * NS], C("ident"), start=True, stop=True)
                    finish(ins)
                elif name == "u":
                    g, u = k
                    n = unit(u)[0]
                    after(pe, *(("V", "ks", g, u) if u else ("V", "dt", g, u, 64)))
                    for h in range(4):
                        ins = pe.matmul(b1[0:n, h * P:(h + 1) * P], xt[0:n, h, 0:n], bv[0:n, h, :], start=True, stop=True)
                    finish(ins)
                elif name == "os":
                    g, u = k
                    n, c0 = unit(u)
                    after(pe, "A", "u", g, u)
                    for h in range(4):
                        o = b2[0:n, h * P:(h + 1) * P]
                        if u == 1:
                            pe.matmul(o, reg[g][:, h, c0:c0 + n], S[:, h, :], start=True, stop=False)
                        if u == 2:
                            pe.matmul(o, pp[:, h, 0:NS], C("ident"), start=True, stop=False)
                        ins = pe.matmul(o, qk[0:n, h, 0:n], ub[0:n, h, :], start=u == 0, stop=True)
                        if u < 2:
                            ins = pe.matmul(b3[:, h * P:(h + 1) * P], tk[0:n, h, :], ub[0:n, h, :], start=True, stop=True)
                    finish(ins)
                elif name == "ot":
                    n = unit(k[1])[0]
                    after(pe, "V", "o2", *k)
                    for h in range(4):
                        ins = turn(b3[:, h * n:(h + 1) * n], bv[0:n, h, :], n)
                    finish(ins)
                elif name == "sh":
                    g, h = k
                    pe.wait_ge(s_in[h % 2], 16 * (4 * g + h // 2 + 1))
                    if h == 0:
                        after(pe, "A", "tb2", g, 2)
                        after(pe, "V", "kk", g, 2)
                    for b in range(DB):
                        c0 = SEQ + b * DT
                        ins = pe.matmul(b3[:, h * P:(h + 1) * P].rearrange("p (q b t) -> p q b t", q=2, b=DB)[:, :, b, :],
                                        ssm[:, h % 2, b, :], reg[g][:, h:h + 9:8, c0:c0 + DT], start=True, stop=True)
                    finish(ins)
                elif name == "us":
                    g, h = k
                    after(pe, "V", "um", g, h)
                    if h == 0:
                        after(pe, "A", "o", g, 2)
                    else:
                        after(pe, *(("V", "us", g, h - 2) if h > 1 else ("V", "oz", g, 2)))
                    for i in range(2):
                        ins = pe.matmul(psB[:, h % 2 * 2 + i, :], tk[0:NS, h, :],
                                        umask[0:NS, 4 * i:4 * i + 4, :].rearrange("p b e -> p (b e)"), start=True, stop=True)
                    finish(ins)
                elif name == "gs":
                    r = k[0]
                    n = min(P, 648 - r * P)
                    pe.wait_ge(new_done, 12)
                    after(pe, *(("A", "gs", r - 2) if r >= 2 else ("V", "us", 1, 3)))
                    finish(turn(psB[0:n, r % 2, 0:P], gnew[:, :, :].rearrange("p r f -> p (r f)")[:, r * P:r * P + n], P))
                elif name == "hk":
                    g = k[0]
                    pe.wait_ge(hk_in, 16 * (g + 1))
                    after(pe, *(("V", "us", 1, 3) if g == 0 else ("A", "OT", 0, DB - 1)))
                    for i in range(2):
                        ins = pe.matmul(psB[:, 2 + i, :], C("flip"), hk[:, 2 * i:2 * i + 2, :].rearrange("p h x -> p (h x)"),
                                        start=True, stop=True)
                    finish(ins)
                elif name == "kv":
                    g, t = k
                    n, c0 = unit(t)
                    pe.wait_ge(evac_done, 16 + 6 * g + 4)
                    after(pe, *(("A", "kv", g, t - 1) if t else ("V", "hk", g)))
                    for kind, bank in ((1, b0), (2, b1)):
                        for h in range(4):
                            ins = turn(bank[0:n, h * P:(h + 1) * P], reg[g][:, 4 * kind + h, c0:c0 + n], P)
                    finish(ins)
                elif name == "S":
                    g, h = k
                    if h == 0:
                        pe.wait_ge(evac_done, 16 + 6 * g + 6)
                        after(pe, "A", "kv", g, 2)
                    if h >= 2:
                        after(pe, "V", "S", g, h - 2)
                    qT, kT_ = reg[g][:, h, :], reg[g][:, 4 + h, :]
                    pe.matmul(psB[:, h % 2, 0:SEQ], qT[:, P:SEQ], kT_[:, 0:SEQ], start=True, stop=True)
                    finish(pe.matmul(psB[:, h % 2, SEQ:SEQ + P], qT[:, 0:P], kT_[:, 0:P], start=True, stop=True))
                elif name == "T":
                    g, h = k
                    after(pe, "V", "N", g, h)
                    s_ = sc[:, h % 2]
                    turn(b2[:, 0:P], s_[:, 256:384], P)
                    turn(b2[:, P:2 * P], s_[:, 0:P], P)
                    finish(turn(b2[:, 2 * P:3 * P], s_[:, P:2 * P], P))
                elif name == "O":
                    g, h = k
                    after(pe, "A", "T", g, h)
                    if h:
                        after(pe, "A", "O", g, h - 1)
                    pe.matmul(b3[:, 0:SEQ], vt[:, 0, h, :], pt[:, h % 2, 0:SEQ], start=True, stop=False)
                    finish(pe.matmul(b3[:, P:SEQ], vt[:, 1, h, :], pt[:, h % 2, SEQ:SEQ + P], start=False, stop=True))
                elif name == "kt":
                    g, b = k
                    pe.wait_ge(pk_in[b % 2], 32 * (DB // 2 * g + b // 2 + 1))
                    after(pe, *(("A", "O", g, 3) if b == 0 else ("V", "SS", g, b - 1)))
                    if b >= 2:
                        after(pe, "A", "OT", g, b - 2)
                    for i, bank in ((0, b0), (1, b1)):
                        for h in range(4):
                            ins = turn(bank[:, h * P:(h + 1) * P], kp[:, b % 2, i, h, :], P)
                    finish(ins)
                elif name == "SS":
                    g, b = k
                    after(pe, "A", "kt", g, b)
                    after(pe, "V", "kt", g, b)
                    c0 = SEQ + b * DT
                    for h in range(4):
                        qT = reg[g][:, h, c0:c0 + DT]
                        pe.matmul(b2[32 * h:32 * h + DT, 0:256], qT, ktp[:, h, :], start=True, stop=True)
                        ins = pe.matmul(b2[32 * h:32 * h + DT, 256:TOK], qT, reg[g][:, 4 + h, SEQ:TOK], start=True, stop=True)
                    finish(ins)
                elif name == "PT":
                    after(pe, "V", "SN", *k)
                    turn(b3[:, 0:P], sc[:, 0, 0:P], P)
                    turn(b3[:, P:2 * P], sc[:, 0, P:2 * P], P)
                    finish(turn(b3[0:NS, 2 * P:3 * P], sc[:, 0, 2 * P:TOK], P))
                elif name == "PV":
                    g, b = k
                    pe.wait_ge(pv_in[b % 2], 32 * (DB // 2 * g + b // 2 + 1))
                    after(pe, "A", "PT", g, b)
                    for h in range(4):
                        o = b0[32 * h:32 * h + DT, 0:P]
                        for i in range(2):
                            pe.matmul(o, pt[:, 0, i * P + 32 * h:i * P + 32 * h + DT], vp[:, b % 2, i, h, :], start=i == 0, stop=False)
                        ins = pe.matmul(o, pt[0:NS, 0, 2 * P + 32 * h:2 * P + 32 * h + DT], vt[0:NS, 2, h, :], start=False, stop=True)
                    finish(ins)
                elif name == "OT":
                    after(pe, "A", "PV", *k)
                    finish(turn(b1[:, 0:P], ob[:, :], P))
                elif name == "fp":
                    r = k[0]
                    pe.wait_ge(fl_in, 16 * (2 + DB))
                    if r >= 2:
                        after(pe, "A", "fp", r - 2)
                    for j in range(4):
                        ins = turn(psB[:, r % 2, 88 * j:88 * j + 88], frow[0:88, 4 * r + j, :], 88)
                    finish(ins)
                else:
                    raise KeyError(x)

            for x in SLOTS[-1, 0]:
                if x[0] == "P":
                    step(x)
            for c in range(NC1):
                project(c)
                if wa_pair(c - 2) is not None:
                    sum_squares(wa_pair(c - 2))
            for p in (6, 7):
                sum_squares(p)

            def up(c, blk, q):
                pair, kq = q // 4, q % 4
                n = blk * 4 + pair
                if kq == 0 and (not isinstance(n, int) or n >= 2):
                    pe.wait_ge(f["evac"], n - 1)
                if isinstance(c, int) and c < NC1 + 4:
                    pe.wait_ge(xn_l, kq + 1)
                bank = 2 * (pair % 2)
                products(c, q % RING, psA[:, bank:bank + 2, :], kq * CQ, kq == 0, kq == 3, xhi, xlo)

            def down(c, blk, d, par):
                n = blk * 8 + d
                pe.wait_ge(f["add"], n + 1)
                if d == 0:
                    pe.wait_ge(f["hlo"], blk * 2 + 2)
                bank = 2 * (d % 2)
                products(c, d % RING, psB[:, bank:bank + 2, :], 0, True, True, hhi[:, par], hlo[:, par])

            c = NC1
            for q in range(16):
                up(c + q, 0, q)
            c += 16
            with pe.Fori(0, NLOOP) as it:
                for t in range(48):
                    half, q = t // 24, t % 24
                    blk = it * 2 + (1 + half)
                    cc = it * 48 + (c + t)
                    if q < 16:
                        up(cc, blk, q)
                    else:
                        down(cc, it * 2 + half, q - 16, half)
            c += 48 * NLOOP
            def new_rows_turn(r):
                m_ = min(4, 18 - 4 * r)
                if r == 4:
                    pe.wait_ge(fin["ne"], 1)
                for j in range(m_):
                    ins = turn(psA[0:88, r % 4, j * P:(j + 1) * P], fnewT[:, :, 4 * r + j], P)
                ins.then_inc(fin["nt"], 1)

            def last_sum(p):
                pe.wait_ge(fin["sq"], p + 1)
                for j in range(2):
                    ins = pe.matmul(psA[0:1, 3, 0:TOK], C("ones", P, 1), sqb[:, p % 2, j, :],
                                    start=(p == 0 and j == 0), stop=(p == 7 and j == 1))
                ins.then_inc(fin["ss"], 1)

            def turn_y(q):
                pe.wait_ge(fin["w"], 2 * q + 2)
                pe.wait_ge(*((fin["ev"], 3 * q) if q else (fin["ne"], 5)))
                for t in range(3):
                    n, c0 = unit(t)
                    for j in range(4):
                        ins = turn(psA[0:n, t, j * P:(j + 1) * P], xn[:, q % 2, j, c0:c0 + n], P)
                    ins.then_inc(fin["t"], 1)

            for d in range(8):
                down(c + d, NB - 1, d, (NB - 1) % 2)
                if d == 0:
                    pe.wait_ge(f["conv"], 4 * NB)
                    for r in range(4):
                        new_rows_turn(r)
                elif d == 1:
                    new_rows_turn(4)
                else:
                    if d == 2:
                        pe.wait_ge(fin["ne"], 5)
                    last_sum(d - 2)
                if d in (3, 5):
                    turn_y(d // 2 - 1)
            last_sum(6)
            turn_y(2)
            last_sum(7)
            turn_y(3)
            pe.wait_ge(fin["ms"], 1)
            pe.wait_ge(f["add"], NB * 8 + 2)
            for t in range(3):
                n, c0 = unit(t)
                ins = pe.transpose(b0[0:n, t:t + 1], rs2[0:1, c0:c0 + n], C("ident", 1, 1))
            ins.then_inc(fin["mt"], 1)

        @block.gpsimd
        def _(pool):
            def finish(ins):
                ins.then_inc(done["G"], 1)

            def pads(n):
                name, p = PAIRS[n]
                kind, h = tile_of(name, p, 0)
                g = int(name[1])
                gp = g * 6 + p
                ft = kind * 8 + g * 4 + h
                if gp == 0:
                    after(pool, "A", "prev")
                else:
                    pool.wait_ge(conv_done, gp)
                for j in range(2):
                    ins = pool.tensor_copy(ue[:, j, 3 + SEQ:347].rearrange("p (b s) -> p b s", b=DB)[:, :, 0:3],
                                           prevT[:, :, ft + j].rearrange("p (b r) -> p b r", b=DB))
                ins.then_inc(pads_done, 1)

            def new_rows(n):
                name, p = PAIRS[n]
                kind, h = tile_of(name, p, 0)
                g = int(name[1])
                ft = kind * 8 + g * 4 + h
                pool.wait_ge(evac_done, n + 1)
                for j in range(2):
                    pool.tensor_copy(gnew[:, 0:3, ft + j], ue[:, j, SEQ:SEQ + 3])
                    ins = pool.tensor_copy(gnew[:, 3:27, ft + j].rearrange("p (b r) -> p b r", b=DB),
                                           ue[:, j, 3 + SEQ:347].rearrange("p (b s) -> p b s", b=DB)[:, :, 8:11])
                ins.then_inc(new_done, 1)

            def power(out, in_, n, width):
                return pool.tensor_tensor(out, in_, sm("mh", n, 0, width), ALU.pow)

            pages = []

            def step(x):
                name, k = x[1], x[2:]
                if name == "rbout":
                    after(pool, "A", "rb")
                    pool.dma_start(rb_dram, rsb0[0:NH, :]).then_inc(rb_out, 16)
                    finish(pool.memset(ue[:, :, 0:3], 0.0))
                elif name == "rs":
                    t = k[0]
                    n = unit(t)[0]
                    after(pool, "V", "ms", t)
                    finish(power(sm("rsx", n, t, t + 1), sm("rsx", n, t, t + 1), n, 1))
                elif name == "rn":
                    n = unit(k[1])[0]
                    after(pool, "V", "ss", *k)
                    finish(power(sm("rn", n), sm("rn", n), n, 8))
                elif name == "mk":
                    g, u, l = k
                    n = unit(u)[0]
                    after(pool, *(("P", "pl", g, u, l // 2) if l > 2 else ("V", "kk", g, u)))
                    finish(pool.tensor_tensor(dec[0:n, :, 0:n], at_[0:n, :, 0:n], over_heads(C(f"lev{l}", n, n), 4), ALU.mult))
                elif name == "or":
                    n = unit(k[1])[0]
                    after(pool, "V", "o1", *k)
                    finish(power(sm("ro", n), sm("ro", n), n, 4))
                elif name in ("si", "s2"):
                    g, h = k
                    if name == "si":
                        if h >= 2:
                            after(pool, "P", "sh", g, h - 2)
                        elif g:
                            pool.wait_ge(s_out[h % 2], 16 * 2 * g)
                        else:
                            after(pool, "A", "rt", 2, 3)
                    elif h < 2:
                        after(pool, "P", "sh", g, h + 2)
                    else:
                        pool.wait_ge(s_out[h % 2], 16 * (2 * g + 1))
                    pool.dma_start(ssm[:, h % 2], I["state_gdn"][0, :, 4 * g + h].rearrange("b d e -> d b e"))\
                        .then_inc(s_in[h % 2], 16)
                elif name == "so":
                    g, h = k
                    if h == 4:
                        after(pool, "V", "st", g, 1)
                        pool.dma_start(O["sp"][0, 0, 4 * g:4 * g + 4].rearrange("h d e -> d h e"), S[:, :, :]).then_inc(st_out, 16)
                    else:
                        after(pool, "V", "us", g, h)
                        pool.dma_start(O["ss"][0, :, 4 * g + h].rearrange("b d e -> d b e"), ssm[:, h % 2]).then_inc(s_out[h % 2], 16)
                elif name == "gs":
                    r = k[0]
                    n = min(P, 648 - r * P)
                    after(pool, "A", "gs", r)
                    rows_p, rows_s = 72, 576
                    gp_ = O["gcp"][0, 0].rearrange("r (f c) -> (r f) c", c=P)
                    gs_ = O["gcs"][0].rearrange("b r (f c) -> (b r f) c", c=P)
                    if r == 0:
                        pool.dma_start(gp_, gst[0:rows_p, 0, :]).then_inc(gs_out, 16)
                        pool.dma_start(gs_[0:P - rows_p, :], gst[rows_p:P, 0, :]).then_inc(gs_out, 16)
                    else:
                        pool.dma_start(gs_[r * P - rows_p:r * P - rows_p + n, :], gst[0:n, r, :]).then_inc(gs_out, 16)
                elif name == "hk":
                    g = k[0]
                    if g == 0:
                        pool.wait_ge(rb_out, 16)
                        after(pool, "V", "us", 1, 3)
                        for i in range(2):
                            pool.wait_ge(s_out[i], 16 * 4)
                        pool.wait_ge(st_out, 32)
                        pool.wait_ge(gs_out, 16 * 7)
                    else:
                        after(pool, "P", "hk", 0)
                    src = bass.AP(rb_dram.tensor, 4 * g * 3 * P, [[1, P], [3 * P, 4], [1, 2 * P]])
                    pool.dma_start(hk[:, :, :], src).then_inc(hk_in, 16)
                elif name == "kv":
                    g, t = k
                    n, c0 = unit(t)
                    after(pool, "A", "kv", g, t)
                    hs = slice(4 * g, 4 * g + 4)
                    for key, tile_ in (("k", kst[0:n, (3 * g + t) % 2]), ("v", vt[0:n, t])):
                        if t < 2:
                            out = O[key + "p"][0, 0, c0:c0 + n, hs]
                        else:
                            out = O[key + "s"][0, :, :, hs].rearrange("b t h d -> (b t) h d")
                        pool.dma_start(out, tile_).then_inc(kv_out[(3 * g + t) % 2], 16)
                elif name in ("pk", "pv"):
                    g, b = k
                    if (g, b) == (0, 0):
                        pool.wait_ge(pt_in, 16)
                        after(pool, "V", "us", 1, 3)
                    elif (g, b) != (0, 1):
                        after(pool, "P", "kt" if name == "pk" else "PV", *((g, b - 2) if b > 1 else (0, DB - 2 + b)))
                    cache, tile_, arrived = (I["cache_k"], kp, pk_in) if name == "pk" else (I["cache_v"], vp, pv_in)
                    for i in range(2):
                        page = pool.value_load(ptab[0:1, 2 * b + i:2 * b + i + 1], min_val=0, max_val=n_pool - 1)
                        src = cache[0].rearrange("n s h d -> n s (h d)")[bass.DynSlice(page, 1), :, 512 * g:512 * g + 512]
                        pool.dma_start(tile_[:, b % 2, i].rearrange("p h d -> p (h d)"), src.rearrange("a s c -> (a s) c"))\
                            .then_inc(arrived[b % 2], 16)
                elif name == "fz":
                    after(pool, "V", "ma", 1)
                    for i in range(2):
                        pool.wait_ge(kv_out[i], 32 * 3)
                    finish(pool.memset(fue[:, :, :, 0:2], 0.0))
                else:
                    raise KeyError(x)

            after(pool, "V", "init")
            pool.dma_start(sm("dtb"), I["gdn_dt_bias"].broadcast_to([P, NH])).then_inc(rows_in, 16)
            pool.dma_start(sm("alog"), I["gdn_a_log"].broadcast_to([P, NH])).then_inc(rows_in, 16)
            pool.dma_start(sm("rb", NBK), I["rel_bias"]).then_inc(rows_in, 16)
            pool.dma_start(wab[:, :, :], w_in[:, 7 * W:].rearrange("(k p) n -> p k n", p=P)).then_inc(ab_in, 16)
            pool.dma_start(ptab[:, :], I["page_table"].rearrange("b n -> (b n)").rearrange("(a n) -> a n", a=1)).then_inc(pt_in, 16)
            for x in SLOTS[-1, 0]:
                if x[0] == "G":
                    step(x)
            after(pool, "G", "rbout")
            pool.memset(ue[:, :, 0:3], 0.0).then_inc(pads_done, 1)
            pads(0)
            for c in range(NC1):
                for n, (name, p) in enumerate(PAIRS[:NGA]):
                    if c - 1 == FIRST[name] + 4 * p + 3 and name[0] == "g":
                        if p < 6:
                            new_rows(n)
                        nxt = {5: n + 3}.get(p, n + 1)
                        if p < 5 or (p == 5 and name == "g0"):
                            pads(nxt)
                for x in (x for r in range(PARTS) for x in SLOTS[c, r]):
                    if x[0] == "G":
                        step(x)

            def f_pads(blk, r, par):
                n = blk * 4 + r
                kind = r % 2
                if r == 0:
                    pool.wait_ge(f["stage"], blk + 1)
                if not isinstance(n, int) or n >= 2:
                    pool.wait_ge(f["conv"], n - 1)
                for j in range(2):
                    old = fst[:, par, kind, r // 2 * 2 + j, 4:20].rearrange("p (b r) -> p b r", b=DB)
                    ins = pool.tensor_tensor(fue[:, kind, j, 2 + SEQ:338].rearrange("p (b s) -> p b s", b=DB)[:, :, 0:2],
                                             old, C("ones", P, 16).rearrange("p (b r) -> p b r", b=DB), ALU.mult)
                ins.then_inc(f["pad"], 1)

            def f_events(blk, q, par):
                if q in (2, 6, 10, 14):
                    f_pads(blk, q // 4, par)

            after(pool, "G", "fz")
            pool.memset(fue[:, :, :, 0:2], 0.0).then_inc(f["pad"], 1)
            for q in range(16):
                f_events(0, q, 0)
            with pool.Fori(0, NLOOP) as it:
                for t in range(48):
                    half, q = t // 24, t % 24
                    f_events(it * 2 + (1 + half), q, (1 + half) % 2)
            for r in range(5):
                pool.wait_ge(fin["ne"], r + 1)
            pool.dma_start(O["fcp"][0, 0].rearrange("r (f c) -> f r c", c=P), frow[0:88, 0:2, :]).then_inc(fin["no"], 16)
            for b in range(DB):
                pool.dma_start(O["fcs"][0, b].rearrange("r (f c) -> f r c", c=P), frow[0:88, 2 + 2 * b:4 + 2 * b, :])\
                    .then_inc(fin["no"], 16)
            pool.wait_ge(fin["mr"], 1)
            power(sm("rsx", P, 0, 2), sm("ssx", P, 0, 2), P, 2)
            power(sm("rsx", NS, 2, 3), sm("ssx", NS, 2, 3), NS, 1).then_inc(fin["r"], 1)
            pool.wait_ge(fin["no"], 16 * 9)
            pool.wait_ge(gs_out, 16 * 7)
            pool.wait_ge(st_out, 32)
            for i in range(2):
                pool.wait_ge(s_out[i], 16 * 4)
            for i in range(2):
                        pool.wait_ge(kv_out[i], 32 * 3)


_INS = ["x_prompt", "x_sample", "cache_k", "cache_v", "page_table", "state_gdn", "state_gdn_conv", "state_ffn_conv",
        "rms_mix_w", "w_in", "gdn_conv_w", "gdn_a_log", "gdn_dt_bias", "gdn_norm_w", "w_out", "rms_ffn_w", "w_up",
        "ffn_conv_w", "ffn_conv_b", "w_down", "rel_bias", "final_norm_w"]
_OUTS = [("yp", (1, SEQ, DM)), ("ys", (DB, DT, DM)), ("kp", (1, 1, SEQ, NH, P)), ("vp", (1, 1, SEQ, NH, P)),
         ("sp", (1, 1, NH, P, P)), ("gcp", (1, 1, 3, 3 * W)), ("fcp", (1, 1, 2, 2 * DFF)),
         ("ks", (1, DB, DT, NH, P)), ("vs", (1, DB, DT, NH, P)), ("ss", (1, DB, NH, P, P)),
         ("gcs", (1, DB, 3, 3 * W)), ("fcs", (1, DB, 2, 2 * DFF))]


def kernel(**inputs):
    import concourse.bacc as bacc
    from concourse.bass_utils import run_bass_kernel_spmd

    nc = bacc.Bacc("TRN2", target_bir_lowering=False, num_devices=1)
    arrays = {f"in_{n}_dram": np.ascontiguousarray(inputs[n]) for n in _INS}
    arrays["in_consts_dram"] = CONSTS
    I = {n[3:-5]: nc.dram_tensor(n, a.shape, mybir.dt.from_np(a.dtype), kind="ExternalInput").ap() for n, a in arrays.items()}
    O = {n: nc.dram_tensor(f"out_{n}_dram", s, F32, kind="ExternalOutput").ap() for n, s in _OUTS}
    build(nc, I, O)
    r = run_bass_kernel_spmd(nc, [arrays], core_ids=[0])
    return tuple(r.results[0][f"out_{n}_dram"] for n, _ in _OUTS)
```
